# Optimizing a Trainium2 kernel written in Bass

```python
import math
import jax, jax.numpy as jnp
from jax import lax
import numpy as np

D_MODEL = 1024
BATCH = 1
SEQ = 256
DEPTH = 2

MLA_HEADS = 8
MLA_Q_LORA = 512
MLA_KV_LORA = 256
MLA_NOPE = 128
MLA_ROPE = 64
MLA_V = 128
ROPE_THETA = 10000.0
DIFF_HEADS = 8
DIFF_HEAD_DIM = 64
D_FF_DENSE = 2816
N_EXPERTS = 8
TOP_K = 2
D_FF_EXPERT = 3584
Q_BLOCK = 128
EPS = 1e-6
N_DENSE = (DEPTH + 1) // 2
N_MOE = DEPTH // 2

W_CQ = MLA_Q_LORA
W_CKV = MLA_KV_LORA
W_KR = MLA_ROPE
W_DQ = DIFF_HEADS * 2 * DIFF_HEAD_DIM
W_DK = DIFF_HEADS * 2 * DIFF_HEAD_DIM
W_DV = DIFF_HEADS * 2 * DIFF_HEAD_DIM
D_IN = W_CQ + W_CKV + W_KR + W_DQ + W_DK + W_DV
MLA_OUT = MLA_HEADS * MLA_V
DIFF_OUT = DIFF_HEADS * 2 * DIFF_HEAD_DIM

kernel_name = "hybrid_mla_diffattn_gated_moe_encoder"

def rms_norm(x, gain):
    xf = x.astype(jnp.float32)
    y = xf * lax.rsqrt(jnp.mean(xf * xf, axis=-1, keepdims=True) + EPS)
    return (y * gain.astype(jnp.float32)).astype(x.dtype)

def apply_rope(x, pos):
    half = x.shape[-1] // 2
    inv_freq = ROPE_THETA ** (-jnp.arange(half, dtype=jnp.float32) / half)
    ang = pos.astype(jnp.float32)[..., None] * inv_freq
    ang = ang.reshape(ang.shape[:2] + (1,) * (x.ndim - 3) + (half,))
    cos, sin = jnp.cos(ang), jnp.sin(ang)
    xf = x.astype(jnp.float32)
    x1, x2 = xf[..., :half], xf[..., half:]
    return jnp.concatenate([x1 * cos - x2 * sin, x2 * cos + x1 * sin], axis=-1).astype(x.dtype)

def alibi_slopes():
    return 2.0 ** (-8.0 * jnp.arange(1, DIFF_HEADS + 1, dtype=jnp.float32) / DIFF_HEADS)

def to_blocks(a):
    b, s = a.shape[:2]
    a = a.reshape((b, s // Q_BLOCK, Q_BLOCK) + a.shape[2:])
    return jnp.moveaxis(a, 1, 0)

def from_blocks(a):
    a = jnp.moveaxis(a, 0, 1)
    return a.reshape((a.shape[0], a.shape[1] * a.shape[2]) + a.shape[3:])

def mla_attention(c_q, c_kv, k_rope, pos, q_norm_g, kv_norm_g, w_uq, w_ukv,
                  qn_nope_g, qn_rope_g, kn_nope_g, kn_rope_g):
    b, s, _ = c_q.shape
    q = (rms_norm(c_q, q_norm_g) @ w_uq).reshape(b, s, MLA_HEADS, MLA_NOPE + MLA_ROPE)
    kv = (rms_norm(c_kv, kv_norm_g) @ w_ukv).reshape(b, s, MLA_HEADS, MLA_NOPE + MLA_V)
    q_nope = rms_norm(q[..., :MLA_NOPE], qn_nope_g)
    q_rope = apply_rope(rms_norm(q[..., MLA_NOPE:], qn_rope_g), pos)
    k_nope = rms_norm(kv[..., :MLA_NOPE], kn_nope_g)
    v = kv[..., MLA_NOPE:]
    k_r = apply_rope(rms_norm(k_rope, kn_rope_g), pos)
    scale = (MLA_NOPE + MLA_ROPE) ** -0.5

    def block(args):
        qn, qr = args
        sc = (jnp.einsum('bqhn,bkhn->bhqk', qn, k_nope)
              + jnp.einsum('bqhr,bkr->bhqk', qr, k_r))
        p = jax.nn.softmax(sc.astype(jnp.float32) * scale, axis=-1).astype(v.dtype)
        return jnp.einsum('bhqk,bkhv->bqhv', p, v)

    o = from_blocks(lax.map(block, (to_blocks(q_nope), to_blocks(q_rope))))
    return o.reshape(b, s, MLA_OUT)

def diff_attention(q, k, v, pos, qn_g, kn_g, lam_q1, lam_k1, lam_q2, lam_k2,
                   subln_g, lambda_init):
    b, s, _ = q.shape
    q = rms_norm(q.reshape(b, s, DIFF_HEADS, 2, DIFF_HEAD_DIM), qn_g)
    k = rms_norm(k.reshape(b, s, DIFF_HEADS, 2, DIFF_HEAD_DIM), kn_g)
    v = v.reshape(b, s, DIFF_HEADS, 2 * DIFF_HEAD_DIM)
    lam = (jnp.exp(jnp.sum(lam_q1.astype(jnp.float32) * lam_k1.astype(jnp.float32)))
           - jnp.exp(jnp.sum(lam_q2.astype(jnp.float32) * lam_k2.astype(jnp.float32)))
           + lambda_init)
    slopes = alibi_slopes()
    pos_f = pos.astype(jnp.float32)
    scale = DIFF_HEAD_DIM ** -0.5

    def block(args):
        qb, pq = args
        sc = jnp.einsum('bqhcd,bkhcd->bhcqk', qb, k).astype(jnp.float32) * scale
        dist = jnp.abs(pq[:, :, None] - pos_f[:, None, :])
        sc = sc - slopes[None, :, None, None, None] * dist[:, None, None]
        p = jax.nn.softmax(sc, axis=-1)
        w = (p[:, :, 0] - lam * p[:, :, 1]).astype(v.dtype)
        return jnp.einsum('bhqk,bkhv->bqhv', w, v)

    o = from_blocks(lax.map(block, (to_blocks(q), to_blocks(pos_f))))
    o = rms_norm(o, subln_g) * (1.0 - lambda_init)
    return o.reshape(b, s, DIFF_OUT)

def swiglu(h, w_gate, w_up, w_down):
    return (jax.nn.silu(h @ w_gate) * (h @ w_up)) @ w_down

def moe_swiglu(h, w_router, w_gate_e, w_up_e, w_down_e):
    b, s, d = h.shape
    t = h.reshape(b * s, d)
    logits = (t @ w_router).astype(jnp.float32)
    top_vals, top_idx = lax.top_k(logits, TOP_K)
    top_w = jax.nn.softmax(top_vals, axis=-1)
    combine = jnp.sum(jax.nn.one_hot(top_idx, N_EXPERTS, dtype=jnp.float32)
                      * top_w[..., None], axis=1).astype(t.dtype)
    out = jnp.zeros_like(t)
    for e in range(N_EXPERTS):
        y = swiglu(t, w_gate_e[e], w_up_e[e], w_down_e[e])
        out = out + combine[:, e:e + 1] * y
    return out.reshape(b, s, d)

def setup_inputs(seed: int = 0) -> dict:
    key = jax.random.key(seed)
    keys = iter(jax.random.split(key, 64))

    def w(shape, fan_in):
        return jax.random.normal(next(keys), shape, jnp.float32) * (fan_in ** -0.5)

    def gain(shape):
        return 1.0 + 0.02 * jax.random.normal(next(keys), shape, jnp.float32)

    def small(shape, std):
        return std * jax.random.normal(next(keys), shape, jnp.float32)

    L = DEPTH
    return {
        "x": jax.random.normal(next(keys), (BATCH, SEQ, D_MODEL), jnp.float32),
        "positions": jnp.broadcast_to(jnp.arange(SEQ, dtype=jnp.int32), (BATCH, SEQ)),
        "attn_norm_g": gain((L, D_MODEL)),
        "w_in": w((L, D_MODEL, D_IN), D_MODEL),
        "w_gate": w((L, D_MODEL, 2 * D_MODEL), D_MODEL),
        "mla_q_norm_g": gain((L, MLA_Q_LORA)),
        "mla_kv_norm_g": gain((L, MLA_KV_LORA)),
        "mla_w_uq": w((L, MLA_Q_LORA, MLA_HEADS * (MLA_NOPE + MLA_ROPE)), MLA_Q_LORA),
        "mla_w_ukv": w((L, MLA_KV_LORA, MLA_HEADS * (MLA_NOPE + MLA_V)), MLA_KV_LORA),
        "mla_qn_nope_g": gain((L, MLA_NOPE)),
        "mla_qn_rope_g": gain((L, MLA_ROPE)),
        "mla_kn_nope_g": gain((L, MLA_NOPE)),
        "mla_kn_rope_g": gain((L, MLA_ROPE)),
        "diff_qn_g": gain((L, DIFF_HEAD_DIM)),
        "diff_kn_g": gain((L, DIFF_HEAD_DIM)),
        "diff_lam_q1": small((L, DIFF_HEAD_DIM), 0.1),
        "diff_lam_k1": small((L, DIFF_HEAD_DIM), 0.1),
        "diff_lam_q2": small((L, DIFF_HEAD_DIM), 0.1),
        "diff_lam_k2": small((L, DIFF_HEAD_DIM), 0.1),
        "diff_subln_g": gain((L, 2 * DIFF_HEAD_DIM)),
        "w_branch_a": w((L, MLA_OUT, D_MODEL), MLA_OUT),
        "w_branch_b": w((L, DIFF_OUT, D_MODEL), DIFF_OUT),
        "w_out": w((L, D_MODEL, D_MODEL), D_MODEL),
        "ffn_norm_g": gain((L, D_MODEL)),
        "dense_w_gate": w((N_DENSE, D_MODEL, D_FF_DENSE), D_MODEL),
        "dense_w_up": w((N_DENSE, D_MODEL, D_FF_DENSE), D_MODEL),
        "dense_w_down": w((N_DENSE, D_FF_DENSE, D_MODEL), D_FF_DENSE),
        "moe_w_router": w((N_MOE, D_MODEL, N_EXPERTS), D_MODEL),
        "moe_w_gate": w((N_MOE, N_EXPERTS, D_MODEL, D_FF_EXPERT), D_MODEL),
        "moe_w_up": w((N_MOE, N_EXPERTS, D_MODEL, D_FF_EXPERT), D_MODEL),
        "moe_w_down": w((N_MOE, N_EXPERTS, D_FF_EXPERT, D_MODEL), D_FF_EXPERT),
    }

def reference(x, positions, attn_norm_g, w_in, w_gate, mla_q_norm_g, mla_kv_norm_g,
              mla_w_uq, mla_w_ukv, mla_qn_nope_g, mla_qn_rope_g, mla_kn_nope_g,
              mla_kn_rope_g, diff_qn_g, diff_kn_g, diff_lam_q1, diff_lam_k1,
              diff_lam_q2, diff_lam_k2, diff_subln_g, w_branch_a, w_branch_b, w_out,
              ffn_norm_g, dense_w_gate, dense_w_up, dense_w_down, moe_w_router,
              moe_w_gate, moe_w_up, moe_w_down):
    splits = [W_CQ, W_CQ + W_CKV, W_CQ + W_CKV + W_KR, W_CQ + W_CKV + W_KR + W_DQ,
              W_CQ + W_CKV + W_KR + W_DQ + W_DK]
    for layer in range(DEPTH):
        h = rms_norm(x, attn_norm_g[layer])
        c_q, c_kv, k_rope, dq, dk, dv = jnp.split(h @ w_in[layer], splits, axis=-1)
        o_a = mla_attention(c_q, c_kv, k_rope, positions,
                            mla_q_norm_g[layer], mla_kv_norm_g[layer],
                            mla_w_uq[layer], mla_w_ukv[layer],
                            mla_qn_nope_g[layer], mla_qn_rope_g[layer],
                            mla_kn_nope_g[layer], mla_kn_rope_g[layer])
        lambda_init = 0.8 - 0.6 * math.exp(-0.3 * layer)
        o_b = diff_attention(dq, dk, dv, positions, diff_qn_g[layer], diff_kn_g[layer],
                             diff_lam_q1[layer], diff_lam_k1[layer],
                             diff_lam_q2[layer], diff_lam_k2[layer],
                             diff_subln_g[layer], lambda_init)
        g_a, g_b = jnp.split(jax.nn.sigmoid(h @ w_gate[layer]), 2, axis=-1)
        merged = g_a * (o_a @ w_branch_a[layer]) + g_b * (o_b @ w_branch_b[layer])
        x = x + merged @ w_out[layer]
        h = rms_norm(x, ffn_norm_g[layer])
        j = layer // 2
        if layer % 2 == 0:
            x = x + swiglu(h, dense_w_gate[j], dense_w_up[j], dense_w_down[j])
        else:
            x = x + moe_swiglu(h, moe_w_router[j], moe_w_gate[j], moe_w_up[j], moe_w_down[j])
    return x


_drawn_inputs = setup_inputs


def setup_inputs(seed=0):
    import zlib

    import numpy as np

    out = dict(_drawn_inputs(seed))
    spreads = {}
    factors = {'mla_q_norm_g': 8.0,
     'mla_kv_norm_g': 8.0,
     'mla_qn_nope_g': 8.0,
     'mla_qn_rope_g': 8.0,
     'mla_kn_nope_g': 8.0,
     'mla_kn_rope_g': 4.492,
     'diff_qn_g': 2.972,
     'diff_subln_g': 3.701}
    for name, (base, spread) in spreads.items():
        noise = np.random.default_rng([zlib.crc32(name.encode()), seed]).standard_normal(out[name].shape)
        drawn = base * np.exp(spread * noise) if base else spread * noise
        out[name] = __import__('jax').numpy.asarray(drawn.astype(out[name].dtype))
    for name, factor in factors.items():
        out[name] = (out[name] * factor).astype(out[name].dtype)
    return out
```

```python
from contextlib import ExitStack

import numpy as np

import concourse.bass as bass
from concourse import mybir

F32 = mybir.dt.float32
I32 = mybir.dt.int32
ALU = mybir.AluOpType
ACT = mybir.ActivationFunctionType
AX = mybir.AxisListType

P = 128
T = 256
TT = T // P
D = 1024
DB = D // P
DEPTH = 2
HEADS = 8
PAIRS = HEADS // 2
QLB, KLB = 4, 2
ROPE = 64
EPS = 1e-6
MLA_SCALE = float((128 + 64) ** -0.5)
DIFF_SCALE = float(64 ** -0.5)
DENSE_CHUNKS = 2816 // 256
EXPERTS = 8
EXP_CHUNKS = 3584 // 512
CAP = 96
MAX_ROUNDS = -(-T // CAP)
SLOT = 4096
TWO_PI_HI, TWO_PI_MID = 6.28125, 0.0019350051879882812
TWO_PI_LO = float(2 * np.pi - 6.28125 - 0.0019350051879882812)
PI_IN = 3.1415925
ROUND = 12582912.0

LAMBDA_INIT = [0.8 - 0.6 * float(np.exp(-0.3 * l)) for l in range(DEPTH)]

CONST = {}
_at = 0
for _name, _n in (("ident", P), ("ones", P), ("half_ones", P), ("rot", P), ("before", P),
                  ("slot_no", CAP), ("first_wins", EXPERTS), ("inv_freq", 1), ("slope", HEADS)):
    CONST[_name] = (_at, _at + _n)
    _at += _n
CONST_COLS = _at

GAIN = {}
_at = 0
for _name, _n in (("attn", DB), ("ffn", DB), ("q_lat", QLB), ("kv_lat", KLB), ("qn", 1), ("qr", 1),
                  ("kn", 1), ("kr", 1), ("dq", 1), ("dk", 1), ("sub", 1)):
    GAIN[_name] = (_at, _at + _n)
    _at += _n
GAIN_COLS = _at

BANKS = ("proj0", "proj1", "stat", "score0", "score1", "trans", "ctx", "val")
PHASES = []
for _l in range(DEPTH):
    PHASES += [
        (("norm", _l, 0), 1, dict(stat=1, sq=2, rs=1, h=DB)),
        (("latent", _l), 1, dict(proj0=2, proj1=2, stat=3, val=1, sq=4, rs=3, lat=3, kr=1, s4=1, s5=1)),
        (("pair", _l), PAIRS, dict(proj0=4, proj1=3, stat=5, score0=3, score1=3, trans=4, ctx=4, val=3,
                                   sq=5, rs=5, qk=6, v=2, mx=2, dmx=2, p=2, pd=2, pn=2, w=2, pt=4,
                                   gate=2, s0=1, s1=1, s2=1, s3=1)),
        (("merge", _l), 1, dict(proj0=6, proj1=6, stat=4, sq=1, rs=4, ob=4, sig=1, mg=4, x=4,
                                s0=1, s1=1, s2=1, s3=1, s4=1, s5=1)),
        (("norm", _l, 1), 1, dict(stat=1, sq=2, rs=1, h=DB)),
    ]
    if _l % 2 == 0:
        PHASES += [
            (("dense0", _l), 1, dict(proj0=1, proj1=1, silu=1, hid=1, s0=1)),
            (("dense", _l), DENSE_CHUNKS // 2, dict(proj0=2, proj1=2, score0=2, score1=2, trans=2, ctx=2,
                                                    silu=2, hid=2, x=8, s0=1, s1=1, s2=1, s3=1)),
            (("dense1", _l), 1, dict(score0=1, score1=1, trans=1, ctx=1, x=4, s1=1)),
        ]
    else:
        PHASES += [
            (("route", _l), 1, dict(val=2, trans=2, ctx=2, score0=2, score1=2, htok=4, xtok=4)),
        ]
START, _c = {}, {}
for _key, _trips, _per in PHASES:
    START[_key] = dict(_c)
    for _s, _n in _per.items():
        _c[_s] = _c.get(_s, 0) + _trips * _n
PER = {k: p for k, _, p in PHASES}
MOE_START = dict(_c)
MOE_EXPERT = dict(proj0=7, proj1=7, score0=7, score1=7, trans=3, ctx=2, val=2, stat=2, silu=7, hid=7, yadd=7,
                  g=1, he=1, st=1, y=1, comb=1)
MOE_SLOTS = 7


def count(phase, name, k, i=0):
    start, per = START[phase].get(name, 0), PER[phase][name]
    return i * per + (start + k) if not isinstance(i, int) else start + i * per + k


def moe_count(name, k, rnd, pair, par, j=0, per_j=0):
    n = MOE_EXPERT[name]
    v = MOE_START.get(name, 0) + par * n + k
    for reg, per in ((rnd, EXPERTS * n), (pair, 2 * n), (j, per_j)):
        v = v + reg * per if isinstance(reg, int) else reg * per + v
    return v


def slot_count(slot, k, rnd, pair, j=0):
    v = MOE_START.get(f"s{slot}", 0) + k
    for reg, per in ((rnd, EXPERTS // 2 * MOE_SLOTS), (pair, MOE_SLOTS), (j, 1)):
        v = v + reg * per if isinstance(reg, int) else reg * per + v
    return v


def build(nc, x_t, pos_row, pos_col, const, gains, lam_vecs, w_lat, w_heads, w_dqk, w_dv, w_gates, w_merge,
          w_gu, w_dn, w_router, w_exp, out):
    with ExitStack() as ctx:
        def sb(name, shape, dt=F32):
            return ctx.enter_context(nc.sbuf_tensor(name, [P] + shape, dt))

        def sem(name):
            return ctx.enter_context(nc.semaphore(name))

        slots = [sb(f"slot{s}", [SLOT]) for s in range(6)]
        xT = sb("xT", [DB, T])
        hT = sb("hT", [DB, T])
        merged = sb("merged", [DB, T])
        gates = sb("gates", [2 * DB, T])
        latN = sb("latN", [QLB + KLB, T])
        krT = sb("krT", [T])
        cosT, sinT = sb("cosT", [T]), sb("sinT", [T])
        dist = sb("dist", [TT, T])
        cst = sb("cst", [CONST_COLS])
        gn = sb("gn", [DEPTH, GAIN_COLS])
        lamv = sb("lamv", [DEPTH, 4, 64])
        lams = sb("lams", [DEPTH, 8])
        posr, posc = sb("posr", [T], I32), sb("posc", [TT], I32)
        poscf = sb("poscf", [TT])
        eps = sb("eps", [1])
        marks = sb("marks", [16])
        tmp = sb("tmp", [2, T])
        qk = sb("qk", [5, 2 * T])
        flat_mg = merged[:].rearrange("p a b -> p (a b)")
        sqp = flat_mg[:, 0:4 * T].rearrange("p (a b) -> p a b", a=2)
        rsp = sb("rsp", [2, 2 * T])
        msp = sb("msp", [2, 2 * T])
        v_mla, v_diff = (flat_mg[:, n * 2 * T:(n + 1) * 2 * T].rearrange("p (a b) -> p a b", a=TT) for n in (2, 3))
        prob = sb("prob", [2, TT, T])
        dprob = sb("dprob", [2, 2, TT, T])
        probT = sb("probT", [2, TT, T])
        oaT, obT = sb("oaT", [DB, T]), sb("obT", [DB, T])
        mx, nmx, sums = sb("mx", [12]), sb("nmx", [12]), sb("sums", [12])
        rcp = sb("rcp", [12])
        htok = gates[:, 0:8].rearrange("p a b -> p (a b)").rearrange("p (t d) -> p t d", t=TT)
        acc = gates[:, 8:16].rearrange("p a b -> p (a b)").rearrange("p (t d) -> p t d", t=TT)
        flat_oa = oaT[:].rearrange("p a b -> p (a b)")
        flat_ob = obT[:].rearrange("p a b -> p (a b)")
        hTe = [flat_oa[:, i * DB * CAP:(i + 1) * DB * CAP] for i in range(2)]
        yT = flat_ob[:, 0:DB * CAP]
        yrow = flat_mg[:, 0:D]
        G = [flat_mg[:, D + i * TT * CAP:D + (i + 1) * TT * CAP].rearrange("p (t c) -> p t c", t=TT) for i in range(2)]
        Gw = flat_ob[:, 1024:1024 + TT * CAP].rearrange("p (t c) -> p t c", t=TT)
        S = flat_ob[:, 1280:1280 + T]
        silu = prob[:].rearrange("p a b c -> p (a b c)")
        hid = [dprob[:, i].rearrange("p a b c -> p (a b c)") for i in range(2)]
        wr = probT[:].rearrange("p a b c -> p (a b c)")[:, 0:DB * EXPERTS]
        rt = sb("rt", [16, TT, EXPERTS])
        sc1 = sb("sc1", [16, TT])
        cnt = sb("cnt", [EXPERTS + 8])
        nrnd = sb("nrnd", [1], I32)

        ps = {b: ctx.enter_context(nc.psum_tensor(f"ps_{b}", [P, 2 * T], F32)) for b in BANKS}
        full = {b: sem(f"{b}_full") for b in BANKS}
        free = {b: sem(f"{b}_free") for b in BANKS}
        slot_full = [sem(f"slot{s}_full") for s in range(6)]
        slot_free = [sem(f"slot{s}_free") for s in range(6)]
        const_in = sem("const_in")
        x_in = sem("x_in")
        router_in = sem("router_in")
        eps_set = sem("eps_set")
        angle_ready = sem("angle_ready")
        sin_ready = sem("sin_ready")
        lam_dot = sem("lam_dot")
        lam_exp = sem("lam_exp")
        x_ready = sem("x_ready")
        sq_ready = sem("sq_ready")
        rs_ready = sem("rs_ready")
        h_ready = sem("h_ready")
        lat_ready = sem("lat_ready")
        kr_ready = sem("kr_ready")
        qk_ready = sem("qk_ready")
        v_ready = sem("v_ready")
        mla_max = sem("mla_max")
        diff_max = sem("diff_max")
        mla_exp = sem("mla_exp")
        diff_exp = sem("diff_exp")
        mla_prob = sem("mla_prob")
        diff_prob = sem("diff_prob")
        probT_ready = sem("probT_ready")
        gate_raw = sem("gate_raw")
        ob_ready = sem("ob_ready")
        gate_ready = sem("gate_ready")
        merged_ready = sem("merged_ready")
        silu_ready = sem("silu_ready")
        hid_ready = sem("hid_ready")
        route_exp_in = sem("route_exp_in")
        route_exp_out = sem("route_exp_out")
        sel_ready = sem("sel_ready")
        htok_ready = sem("htok_ready")
        xtok_ready = sem("xtok_ready")
        rounds_ready = sem("rounds_ready")
        gather_ready = sem("gather_ready")
        he_ready = sem("he_ready")
        scatter_ready = sem("scatter_ready")
        yadd_done = sem("yadd_done")
        y_ready = sem("y_ready")
        comb_done = sem("comb_done")
        out_ready = sem("out_ready")
        out_sent = sem("out_sent")

        def c_(name):
            a, b = CONST[name]
            return cst[:, a:b]

        def g_(l, name, j=0):
            a = GAIN[name][0] + j
            return gn[:, l, a:a + 1]

        def blk(ap, b, n=P):
            return ap[:, b * n:(b + 1) * n]

        block = ctx.enter_context(nc.Block())

        @block.sync
        def _(sp):
            sp.dma_start(xT[:], x_t).then_inc(x_in, 16)
            for dst, src in ((cst[:], const), (gn[:], gains), (lamv[:], lam_vecs), (posr[:], pos_row),
                             (posc[:], pos_col)):
                sp.dma_start(dst, src).then_inc(const_in, 16)

            def load(slot, before, src, width=SLOT):
                sp.wait_ge(slot_free[slot], before + 1)
                sp.dma_start(slots[slot][:, 0:width], src).then_inc(slot_full[slot], 16)

            def one(arr, i):
                return arr[bass.ds(i, 1)].rearrange("a p n -> p (a n)")

            for l in range(DEPTH):
                load(4, count(("latent", l), "s4", 0), w_lat[l, :, 0:4096])
                load(5, count(("latent", l), "s5", 0), w_lat[l, :, 4096:4096 + 3072], 3072)
                with sp.Fori(0, PAIRS) as i:
                    for s, arr in enumerate((w_heads, w_dqk, w_dv, w_gates)):
                        load(s, count(("pair", l), f"s{s}", 0, i), one(arr, i + l * PAIRS), arr.shape[2])
                for s, piece in ((4, 0), (5, 1), (0, 2), (1, 3), (2, 4), (3, 5)):
                    load(s, count(("merge", l), f"s{s}", 0), w_merge[l, piece])
                if l % 2 == 0:
                    load(0, count(("dense0", l), "s0", 0), w_gu[0])
                    load(1, count(("dense", l), "s1", 0), w_dn[0], 2048)
                    with sp.Fori(0, DENSE_CHUNKS // 2) as i:
                        load(2, count(("dense", l), "s2", 0, i), one(w_gu, i * 2 + 1))
                        load(3, count(("dense", l), "s3", 0, i), one(w_dn, i * 2 + 1), 2048)
                        load(0, count(("dense", l), "s0", 0, i), one(w_gu, i * 2 + 2))
                        load(1, count(("dense", l), "s1", 1, i), one(w_dn, i * 2 + 2), 2048)

            sp.wait_ge(x_ready, count(("merge", 1), "x", 4))
            sp.dma_start(wr, w_router).then_inc(router_in, 16)

            def experts(rnd):
                with sp.Fori(0, EXPERTS // 2) as pair:
                    for par in range(2):
                        def chunk(c0, used, j=0):
                            base = 3 * ((par + c0) % 2)
                            for m in range(3):
                                at = (par * EXP_CHUNKS + c0) * 3 + m
                                idx = pair * (2 * EXP_CHUNKS * 3) + at
                                if not isinstance(j, int):
                                    idx = pair * (2 * EXP_CHUNKS * 3) + j * 6 + at
                                load(base + m, slot_count(base + m, used, rnd, pair, j), one(w_exp, idx))
                        before = [0, 0] if par == 0 else [4, 3]
                        chunk(0, before[par % 2])
                        with sp.Fori(0, EXP_CHUNKS // 2) as j:
                            chunk(1, before[(par + 1) % 2], j)
                            chunk(2, before[par % 2] + 1, j)

            experts(0)
            sp.wait_ge(rounds_ready, 1)
            n = sp.value_load(nrnd[0:1, 0:1], min_val=1, max_val=MAX_ROUNDS)
            with sp.If(n > 1):
                with sp.Fori(1, n) as rnd:
                    experts(rnd)
            sp.wait_ge(out_ready, 1)
            sp.dma_start(out.rearrange("(t p) d -> p t d", p=P), acc).then_inc(out_sent, 16)
            sp.wait_ge(out_sent, 16)

        @block.tensor
        def _(pe):
            def take(bank, n):
                pe.wait_ge(free[bank], n + 1)
                return ps[bank]

            def need(slot, before):
                pe.wait_ge(slot_full[slot], before * 16 + 16)

            def mm(out_, lhsT, rhs, k, n, **kw):
                return nc.tensor.matmul(out_, lhsT, rhs, start=(k == 0), stop=(k == n - 1), **kw)

            def norm(l, which):
                ph = ("norm", l, which)
                o = take("stat", count(ph, "stat", 0))
                for k in range(DB):
                    if k % 4 == 0:
                        pe.wait_ge(sq_ready, count(ph, "sq", k // 4 + 1))
                    m = mm(o[:, 0:T], c_("ones"), merged[:, k], k, DB)
                m.then_inc(full["stat"], 1)

            def latent(l):
                ph = ("latent", l)
                need(4, count(ph, "s4", 0))
                for job in range(2):
                    o = take(f"proj{job}", count(ph, f"proj{job}", 0))
                    for b in range(2):
                        for k in range(DB):
                            if job == 0 and b == 0:
                                pe.wait_ge(h_ready, count(("norm", l, 0), "h", k + 1))
                            c = (k * 4 + job * 2 + b) * P
                            m = mm(o[:, b * T:(b + 1) * T], slots[4][:, c:c + P], hT[:, k], k, DB)
                    m.then_inc(full[f"proj{job}"], 1)
                nc.tensor.drain().then_inc(slot_free[4], 1)
                need(5, count(ph, "s5", 0))
                for job in range(2):
                    o = take(f"proj{job}", count(ph, f"proj{job}", 1))
                    for b in range(2 - job):
                        for k in range(DB):
                            c = (k * 3 + job * 2 + b) * P
                            m = mm(o[:, b * T:(b + 1) * T], slots[5][:, c:c + P], hT[:, k], k, DB)
                    m.then_inc(full[f"proj{job}"], 1)
                nc.tensor.drain().then_inc(slot_free[5], 1)
                for s, (sq_n, ones, blocks) in enumerate(((2, "ones", range(0, 4)), (3, "ones", range(4, 6)),
                                                          (4, "half_ones", range(6, 7)))):
                    pe.wait_ge(sq_ready, count(ph, "sq", sq_n))
                    o = take("stat", count(ph, "stat", s))
                    for k, b in enumerate(blocks):
                        m = mm(o[:, 0:T], c_(ones), gates[:, b], k, len(blocks))
                    m.then_inc(full["stat"], 1)
                pe.wait_ge(lat_ready, count(ph, "lat", 3))
                o = take("val", count(ph, "val", 0))
                mm(o[:, 0:T], c_("rot"), gates[:, 14], 0, 1).then_inc(full["val"], 1)

            def pair(l, i):
                ph = ("pair", l)

                def cn(name, k):
                    return count(ph, name, k, i)

                def stat(g):
                    pe.wait_ge(sq_ready, cn("sq", g + 1))
                    o = take("stat", cn("stat", g))
                    w = T if g == 2 else 2 * T
                    mm(o[:, 0:w], c_("ones" if g < 2 else "half_ones"), sqp[:, g % 2, 0:w], 0, 1)\
                        .then_inc(full["stat"], 1)

                heads = slots[0][:, 0:2560]
                uq = heads[:, 0:1536].rearrange("p (k c) -> p k c", k=QLB)
                ukv = heads[:, 1536:2560].rearrange("p (k c) -> p k c", k=KLB)
                need(0, cn("s0", 0))
                pe.wait_ge(lat_ready, count(("latent", l), "lat", 2))
                o = take("proj0", cn("proj0", 0))
                for h in range(2):
                    for k in range(QLB):
                        m = mm(o[:, h * T:(h + 1) * T], blk(uq[:, k], h), latN[:, k], k, QLB)
                m.then_inc(full["proj0"], 1)
                o = take("proj1", cn("proj1", 0))
                for h in range(2):
                    for k in range(KLB):
                        m = mm(o[:, h * T:(h + 1) * T], blk(ukv[:, k], h), latN[:, QLB + k], k, KLB)
                m.then_inc(full["proj1"], 1)
                o = take("proj0", cn("proj0", 1))
                for k in range(QLB):
                    m = mm(o[:, 0:T], blk(uq[:, k], 2), latN[:, k], k, QLB)
                m.then_inc(full["proj0"], 1)
                o = take("val", cn("val", 0))
                for t in range(TT):
                    for k in range(KLB):
                        m = mm(o[:, t * T:(t + 1) * T], latN[:, QLB + k, t * P:(t + 1) * P],
                               ukv[:, k, 2 * P:4 * P], k, KLB)
                m.then_inc(full["val"], 1)
                nc.tensor.drain().then_inc(slot_free[0], 1)
                stat(0)

                dqk = slots[1][:].rearrange("p (m k c) -> p m k c", m=2, k=DB)
                need(1, cn("s1", 0))
                for m_, bank, job in ((0, "proj1", 1), (1, "proj0", 2)):
                    o = take(bank, cn(bank, job))
                    for h in range(2):
                        for k in range(DB):
                            m = mm(o[:, h * T:(h + 1) * T], blk(dqk[:, m_, k], h), hT[:, k], k, DB)
                    m.then_inc(full[bank], 1)
                    stat(1 + m_)
                nc.tensor.drain().then_inc(slot_free[1], 1)

                dv = slots[2][:, 0:2048].rearrange("p (k c) -> p k c", k=DB)
                need(2, cn("s2", 0))
                o = take("val", cn("val", 1))
                for t in range(TT):
                    for k in range(DB):
                        m = mm(o[:, t * T:(t + 1) * T], hT[:, k, t * P:(t + 1) * P], dv[:, k], k, DB)
                m.then_inc(full["val"], 1)
                nc.tensor.drain().then_inc(slot_free[2], 1)
                stat(3)

                pe.wait_ge(qk_ready, cn("qk", 3))
                o = take("val", cn("val", 2))
                mm(o[:, 0:T], c_("rot"), qk[:, 2, 0:T], 0, 1).then_inc(full["val"], 1)
                stat(4)

                gw = slots[3][:].rearrange("p (k c) -> p k c", k=DB)

                def gate(bank, job, b0):
                    o = take(bank, cn(bank, job))
                    for b in range(2):
                        for k in range(DB):
                            m = mm(o[:, b * T:(b + 1) * T], blk(gw[:, k], b0 + b), hT[:, k], k, DB)
                    m.then_inc(full[bank], 1)

                pe.wait_ge(qk_ready, cn("qk", 5))
                pe.wait_ge(kr_ready, count(("latent", l), "kr", 1))
                for h in range(2):
                    o = take(f"score{h}", cn(f"score{h}", 0))
                    for q in range(TT):
                        mm(o[:, q * T:(q + 1) * T], qk[:, 0, h * T + q * P:h * T + (q + 1) * P],
                           qk[:, 1, h * T:(h + 1) * T], 0, 2)
                        m = mm(o[:, q * T:(q + 1) * T], qk[64 * h:64 * h + 64, 2, T + q * P:T + (q + 1) * P],
                               krT[64 * h:64 * h + 64, :], 1, 2)
                    m.then_inc(full[f"score{h}"], 1)

                need(3, cn("s3", 0))
                gate("proj1", 2, 0)

                def diff_scores(h):
                    if h == 0:
                        pe.wait_ge(qk_ready, cn("qk", 6))
                    for c in range(2):
                        o = take(f"score{c}", cn(f"score{c}", 1 + h))
                        for q in range(TT):
                            r = slice(64 * c, 64 * c + 64)
                            m = mm(o[:, q * T:(q + 1) * T], qk[r, 3, h * T + q * P:h * T + (q + 1) * P],
                                   qk[r, 4, h * T:(h + 1) * T], 0, 1)
                        m.then_inc(full[f"score{c}"], 1)

                def turn(n, src, ready, value):
                    pe.wait_ge(ready, value)
                    o = take("trans", cn("trans", n))
                    for k in range(TT):
                        for q in range(TT):
                            m = nc.tensor.transpose(o[:, k * T + q * P:k * T + (q + 1) * P],
                                                    src[:, q, k * P:(k + 1) * P], c_("ident"))
                    m.then_inc(full["trans"], 1)

                def weigh(n, v, ready):
                    pe.wait_ge(v_ready, ready)
                    pe.wait_ge(probT_ready, cn("pt", n + 1))
                    o = take("ctx", cn("ctx", n))
                    for k in range(TT):
                        m = mm(o[:, 0:T], v[:, k], probT[:, n % 2, k], k, TT)
                    m.then_inc(full["ctx"], 1)

                diff_scores(0)
                for h in range(2):
                    turn(h, prob[:, h], mla_prob, cn("pn", h + 1))
                for h in range(2):
                    weigh(h, v_mla[:, :, h * P:(h + 1) * P], cn("v", 1))
                diff_scores(1)
                gate("proj0", 3, 2)
                nc.tensor.drain().then_inc(slot_free[3], 1)
                for h in range(2):
                    turn(2 + h, dprob[:, h, 0], diff_prob, cn("w", h + 1))
                for h in range(2):
                    weigh(2 + h, v_diff[:, :, h * P:(h + 1) * P], cn("v", 2))

            def merge(l):
                ph = ("merge", l)
                jobs = [0, 0]

                def product(slot, b0, src, bank):
                    w = slots[slot][:].rearrange("p (k c) -> p k c", k=DB)
                    o = take(f"proj{bank}", count(ph, f"proj{bank}", jobs[bank]))
                    jobs[bank] += 1
                    for b in range(2):
                        for k in range(DB):
                            m = mm(o[:, b * T:(b + 1) * T], blk(w[:, k], b0 + b), src[:, k], k, DB)
                    m.then_inc(full[f"proj{bank}"], 1)

                pe.wait_ge(free["ctx"], count(("pair", l), "ctx", 4, PAIRS - 1) + 1)
                need(4, count(ph, "s4", 0))
                product(4, 0, oaT, 0)
                product(4, 2, oaT, 1)
                nc.tensor.drain().then_inc(slot_free[4], 1)
                pe.wait_ge(sq_ready, count(ph, "sq", 1))
                for g in range(4):
                    o = take("stat", count(ph, "stat", g))
                    mm(o[:], c_("ones"), merged[:, 2 * g:2 * g + 2].rearrange("p a b -> p (a b)"), 0, 1)\
                        .then_inc(full["stat"], 1)
                pe.wait_ge(ob_ready, count(ph, "ob", 4))
                need(5, count(ph, "s5", 0))
                product(5, 0, obT, 0)
                product(5, 2, obT, 1)
                nc.tensor.drain().then_inc(slot_free[5], 1)
                for slot, src in ((0, oaT), (1, obT)):
                    need(slot, count(ph, f"s{slot}", 0))
                    product(slot, 0, src, 0)
                    product(slot, 2, src, 1)
                    nc.tensor.drain().then_inc(slot_free[slot], 1)
                pe.wait_ge(merged_ready, count(ph, "mg", 4))
                for slot in (2, 3):
                    need(slot, count(ph, f"s{slot}", 0))
                    product(slot, 0, merged, 0)
                    product(slot, 2, merged, 1)
                    nc.tensor.drain().then_inc(slot_free[slot], 1)

            def dense(l):
                def gate_up(ph, i, slot, kslot, job):
                    w = slots[slot][:].rearrange("p (m k c) -> p m k c", m=2, k=DB)
                    need(slot, count(ph, f"s{slot}", kslot, i))
                    for m_ in range(2):
                        o = take(f"proj{m_}", count(ph, f"proj{m_}", job, i))
                        for b in range(2):
                            for k in range(DB):
                                if ph[0] == "dense0" and m_ == 0 and b == 0:
                                    pe.wait_ge(h_ready, count(("norm", l, 1), "h", k + 1))
                                m = mm(o[:, b * T:(b + 1) * T], blk(w[:, m_, k], b), hT[:, k], k, DB)
                        m.then_inc(full[f"proj{m_}"], 1)
                    nc.tensor.drain().then_inc(slot_free[slot], 1)

                def down(ph, i, slot, kslot, job, hid_n, parity):
                    w = slots[slot][:, 0:2048].rearrange("p (f c) -> p f c", f=2)
                    h = hid[parity][:, 0:2 * T].rearrange("p (f t) -> p f t", f=2)
                    need(slot, kslot)
                    pe.wait_ge(hid_ready, hid_n)
                    for q, bank in enumerate(("score0", "score1", "trans", "ctx")):
                        o = take(bank, count(ph, bank, job, i))
                        for b in range(2):
                            for f in range(2):
                                m = mm(o[:, b * T:(b + 1) * T], blk(w[:, f], 2 * q + b), h[:, f], f, 2)
                        m.then_inc(full[bank], 1)
                    nc.tensor.drain().then_inc(slot_free[slot], 1)

                first, loop, last = ("dense0", l), ("dense", l), ("dense1", l)
                gate_up(first, 0, 0, 0, 0)
                with pe.Fori(0, DENSE_CHUNKS // 2) as i:
                    gate_up(loop, i, 2, 0, 0)
                    down(loop, i, 1, count(loop, "s1", 0, i), 0, count(loop, "hid", 0, i), 0)
                    gate_up(loop, i, 0, 0, 1)
                    down(loop, i, 3, count(loop, "s3", 0, i), 1, count(loop, "hid", 1, i), 1)
                down(last, 0, 1, count(last, "s1", 0), 0, count(last, "x", 0) * 0 + START[last]["hid"], 0)

            def route(l):
                ph = ("route", l)
                pe.wait_ge(router_in, 16)
                o = take("val", count(ph, "val", 0))
                for t in range(TT):
                    for k in range(DB):
                        if t == 0:
                            pe.wait_ge(h_ready, count(("norm", l, 1), "h", k + 1))
                        m = mm(o[:, t * EXPERTS:(t + 1) * EXPERTS], hT[:, k, t * P:(t + 1) * P],
                               wr[:, k * EXPERTS:(k + 1) * EXPERTS], k, DB)
                m.then_inc(full["val"], 1)
                for src, banks in ((hT, ("trans", "ctx")), (xT, ("score0", "score1"))):
                    for t in range(TT):
                        for half, bank in enumerate(banks):
                            o = take(bank, count(ph, bank, t))
                            for k in range(4):
                                m = nc.tensor.transpose(o[:, k * P:(k + 1) * P],
                                                        src[:, half * 4 + k, t * P:(t + 1) * P], c_("ident"))
                            m.then_inc(full[bank], 1)
                pe.wait_ge(sel_ready, 1)
                o = take("val", count(ph, "val", 1))
                E = EXPERTS
                mm(o[:, 0:E], c_("before"), rt[:, 0, 0], 0, 1)
                mm(o[:, E:2 * E], c_("before"), rt[:, 0, 1], 0, 2)
                mm(o[:, E:2 * E], c_("ones"), rt[:, 0, 0], 1, 2)
                mm(o[:, 2 * E:3 * E], c_("ones"), rt[:, 0, 0], 0, 2)
                mm(o[:, 2 * E:3 * E], c_("ones"), rt[:, 0, 1], 1, 2).then_inc(full["val"], 1)

            def experts(rnd):
                with pe.Fori(0, EXPERTS // 2) as pair_:
                    for par in range(2):
                        def cn(name, k, j=0, per_j=0):
                            return moe_count(name, k, rnd, pair_, par, j, per_j)

                        before = [0, 0] if par == 0 else [4, 3]
                        pe.wait_ge(gather_ready, cn("g", 1))
                        for half, bank in enumerate(("trans", "ctx")):
                            o = take(bank, cn(bank, 0))
                            for b in range(4):
                                for t in range(TT):
                                    c = (half * 4 + b) * P
                                    m = mm(o[:, b * CAP:(b + 1) * CAP], htok[:, t, c:c + P], G[par][:, t], t, TT)
                            m.then_inc(full[bank], 1)
                        o = take("trans", cn("trans", 1))
                        for t in range(TT):
                            m = nc.tensor.transpose(o[0:CAP, t * P:(t + 1) * P], Gw[:, t], c_("ident"))
                        m.then_inc(full["trans"], 1)
                        he = hTe[par].rearrange("p (k c) -> p k c", k=DB)

                        def gate_up(c0, job, j=0):
                            sset = (par + c0) % 2
                            for m_ in range(2):
                                s = 3 * sset + m_
                                w = slots[s][:].rearrange("p (k c) -> p k c", k=DB)
                                used = before[sset] + c0 // 2
                                need(s, slot_count(s, used, rnd, pair_, j))
                                o = take(f"proj{m_}", cn(f"proj{m_}", job, j, 2))
                                for f in range(4):
                                    for k in range(DB):
                                        m = mm(o[:, f * CAP:(f + 1) * CAP], blk(w[:, k], f), he[:, k], k, DB)
                                m.then_inc(full[f"proj{m_}"], 1)
                                nc.tensor.drain().then_inc(slot_free[s], 1)

                        def down(c0, job, j=0):
                            sset = (par + c0) % 2
                            s = 3 * sset + 2
                            w = slots[s][:].rearrange("p (f c) -> p f c", f=4)
                            h = hid[(par + c0) % 2][:, 0:4 * CAP].rearrange("p (f c) -> p f c", f=4)
                            used = before[sset] + c0 // 2
                            need(s, slot_count(s, used, rnd, pair_, j))
                            pe.wait_ge(hid_ready, cn("hid", job + 1, j, 2))
                            for half in range(2):
                                o = take(f"score{half}", cn(f"score{half}", job, j, 2))
                                for b in range(4):
                                    for f in range(4):
                                        m = mm(o[:, b * CAP:(b + 1) * CAP], blk(w[:, f], half * 4 + b), h[:, f], f, 4)
                                m.then_inc(full[f"score{half}"], 1)
                            nc.tensor.drain().then_inc(slot_free[s], 1)

                        pe.wait_ge(he_ready, cn("he", 1))
                        gate_up(0, 0)
                        with pe.Fori(0, EXP_CHUNKS // 2) as j:
                            gate_up(1, 1, j)
                            down(0, 0, j)
                            gate_up(2, 2, j)
                            down(1, 1, j)
                        down(6, 6)
                        pe.wait_ge(yadd_done, cn("yadd", 7))
                        for half, (bank, job) in enumerate((("ctx", 1), ("trans", 2))):
                            o = take(bank, cn(bank, job))
                            for b in range(4):
                                c = (half * 4 + b) * CAP
                                m = nc.tensor.transpose(o[0:CAP, b * P:(b + 1) * P], yT[:, c:c + CAP], c_("ident"))
                            m.then_inc(full[bank], 1)
                        pe.wait_ge(scatter_ready, cn("st", 1))
                        pe.wait_ge(y_ready, cn("y", 1))
                        for t in range(TT):
                            for half, bank in enumerate(("val", "stat")):
                                o = take(bank, cn(bank, t))
                                mm(o[:], S[0:CAP, t * P:(t + 1) * P], yrow[0:CAP, half * 512:(half + 1) * 512], 0, 1)\
                                    .then_inc(full[bank], 1)

            pe.wait_ge(const_in, 80)
            for l in range(DEPTH):
                norm(l, 0)
                latent(l)
                with pe.Fori(0, PAIRS) as i:
                    pair(l, i)
                merge(l)
                norm(l, 1)
                if l % 2 == 0:
                    dense(l)
                else:
                    route(l)
            experts(0)
            pe.wait_ge(rounds_ready, 1)
            n = pe.value_load(nrnd[0:1, 0:1], min_val=1, max_val=MAX_ROUNDS)
            with pe.If(n > 1):
                with pe.Fori(1, n) as rnd:
                    experts(rnd)

        @block.scalar
        def _(act):
            def fresh(bank, n):
                act.wait_ge(full[bank], n + 1)
                return ps[bank]

            A = nc.scalar.activation

            def rsqrt(bank_n, at, width, mean):
                o = fresh("stat", bank_n)
                h, c = at
                out_, ms = rsp[:, h, c:c + width], msp[:, h, c:c + width]
                A(ms, o[:, 0:width], ACT.Identity, bias=eps[:, 0:1], scale=mean)
                A(out_, o[:, 0:width], ACT.Ln, bias=eps[:, 0:1], scale=mean)
                act.drain().then_inc(free["stat"], 1)
                A(out_, out_, ACT.Exp, scale=-0.5).then_inc(rs_ready, 1)

            def norm(l, which, x_value):
                ph = ("norm", l, which)
                if x_value:
                    act.wait_ge(x_ready, x_value)
                for half in range(2):
                    A(merged[:, half * 4:half * 4 + 4], xT[:, half * 4:half * 4 + 4], ACT.Square)\
                        .then_inc(sq_ready, 1)
                rsqrt(count(ph, "stat", 0), (0, 0), T, 1.0 / D)

            def latent(l):
                ph = ("latent", l)
                for g, (bank, job, b0, nb) in enumerate((("proj0", 0, 0, 2), ("proj1", 0, 2, 2),
                                                         ("proj0", 1, 4, 2), ("proj1", 1, 6, 1))):
                    o = fresh(bank, count(ph, bank, job))[:, 0:nb * T].rearrange("p (b t) -> p b t", t=T)
                    A(gates[:, 8 + b0:8 + b0 + nb], o, ACT.Copy)
                    A(gates[:, b0:b0 + nb], o, ACT.Square).then_inc(sq_ready, 1)
                    act.drain().then_inc(free[bank], 1)
                for s, n in enumerate((4 * P, 2 * P, ROPE)):
                    if s == 0:
                        act.wait_ge(h_ready, count(("norm", l, 0), "h", DB))
                    rsqrt(count(ph, "stat", s), (s // 2, (s % 2) * T), T, 1.0 / n)

            def pair(l, i):
                ph = ("pair", l)

                def cn(name, k):
                    return count(ph, name, k, i)

                def take(g, bank, job):
                    o = fresh(bank, cn(bank, job))
                    w = T if g == 2 else 2 * T
                    A(qk[:, g, 0:w], o[:, 0:w], ACT.Copy)
                    if g >= 2:
                        act.wait_ge(full["stat"], cn("stat", g - 1))
                    A(sqp[:, g % 2, 0:w], o[:, 0:w], ACT.Square).then_inc(sq_ready, 1)
                    act.drain().then_inc(free[bank], 1)

                def factors(g):
                    w = T if g == 2 else 2 * T
                    if g >= 2:
                        act.wait_ge(qk_ready, cn("qk", (1, 2, 3)[g - 2]))
                    rsqrt(cn("stat", g), (g % 2, 0), w, 1.0 / (P if g < 2 else ROPE))

                take(0, "proj0", 0)
                take(1, "proj1", 0)
                factors(0)
                take(2, "proj0", 1)
                factors(1)
                take(3, "proj1", 1)
                factors(2)
                take(4, "proj0", 2)
                factors(3)
                factors(4)

                for h in range(2):
                    act.wait_ge(mla_max, cn("mx", h + 1))
                    o = fresh(f"score{h}", cn(f"score{h}", 0))
                    for q in range(TT):
                        m = A(prob[:, h, q], o[:, q * T:(q + 1) * T], ACT.Exp, bias=nmx[:, 2 * h + q:2 * h + q + 1],
                              scale=MLA_SCALE, accum_out=sums[:, 2 * h + q:2 * h + q + 1])
                    m.then_inc(mla_exp, 1)
                    act.drain().then_inc(free[f"score{h}"], 1)

                def turned(n):
                    o = fresh("trans", cn("trans", n))
                    if n >= 2:
                        act.wait_ge(full["ctx"], cn("ctx", n - 1))
                    A(probT[:, n % 2].rearrange("p a b -> p (a b)"), o[:], ACT.Copy).then_inc(probT_ready, 1)
                    act.drain().then_inc(free["trans"], 1)

                def diff_exps(h):
                    act.wait_ge(diff_max, cn("dmx", h + 1))
                    for c in range(2):
                        for q in range(TT):
                            n = 4 + 4 * h + 2 * c + q
                            m = A(dprob[:, h, c, q], dprob[:, h, c, q], ACT.Exp, bias=nmx[:, n:n + 1],
                                  scale=DIFF_SCALE, accum_out=sums[:, n:n + 1])
                    m.then_inc(diff_exp, 1)

                diff_exps(0)
                turned(0)
                turned(1)
                diff_exps(1)
                turned(2)
                turned(3)

            def merge(l):
                ph = ("merge", l)
                act.wait_ge(free["ctx"], count(("pair", l), "ctx", 4, PAIRS - 1) + 1)
                A(merged[:], obT[:], ACT.Square).then_inc(sq_ready, 1)
                for g in range(4):
                    if g >= 2:
                        act.wait_ge(ob_ready, count(ph, "ob", g - 1))
                    rsqrt(count(ph, "stat", g), (g % 2, 0), 2 * T, 1.0 / P)
                A(gates[:], gates[:], ACT.Sigmoid).then_inc(gate_ready, 1)

            def dense(l):
                def chunk(ph, job, i=0):
                    o = fresh("proj0", count(ph, "proj0", job, i))
                    act.wait_ge(hid_ready, count(ph, "hid", job, i))
                    A(silu[:, 0:2 * T], o[:], ACT.Silu).then_inc(silu_ready, 1)
                    act.drain().then_inc(free["proj0"], 1)

                chunk(("dense0", l), 0)
                with act.Fori(0, DENSE_CHUNKS // 2) as i:
                    chunk(("dense", l), 0, i)
                    chunk(("dense", l), 1, i)

            def route(l):
                ph = ("route", l)
                for name, banks, dst, ready in (("h", ("trans", "ctx"), htok, htok_ready),
                                                ("x", ("score0", "score1"), acc, xtok_ready)):
                    for t in range(TT):
                        for half, bank in enumerate(banks):
                            o = fresh(bank, count(ph, bank, t))
                            A(dst[:, t, half * 512:(half + 1) * 512], o[:], ACT.Copy).then_inc(ready, 1)
                            act.drain().then_inc(free[bank], 1)
                act.wait_ge(route_exp_in, 1)
                A(sc1[:, 4], sc1[:, 3], ACT.Exp).then_inc(route_exp_out, 1)

            def experts(rnd):
                with act.Fori(0, EXPERTS // 2) as pair_:
                    for par in range(2):
                        def cn(name, k, j=0, per_j=0):
                            return moe_count(name, k, rnd, pair_, par, j, per_j)

                        for half, bank in enumerate(("trans", "ctx")):
                            o = fresh(bank, cn(bank, 0))
                            n = 4 * CAP
                            m = A(hTe[par][:, half * n:(half + 1) * n], o[:, 0:n], ACT.Copy)
                            if half:
                                m.then_inc(he_ready, 1)
                            act.drain().then_inc(free[bank], 1)
                        o = fresh("trans", cn("trans", 1))
                        act.wait_ge(comb_done, cn("comb", 0) + 1)
                        A(S[0:CAP, :], o[0:CAP, 0:T], ACT.Copy).then_inc(scatter_ready, 1)
                        act.drain().then_inc(free["trans"], 1)

                        def chunk(job, j=0):
                            o = fresh("proj0", cn("proj0", job, j, 2))
                            act.wait_ge(hid_ready, cn("hid", job, j, 2))
                            A(silu[:, 0:4 * CAP], o[:, 0:4 * CAP], ACT.Silu).then_inc(silu_ready, 1)
                            act.drain().then_inc(free["proj0"], 1)

                        chunk(0)
                        with act.Fori(0, EXP_CHUNKS // 2) as j:
                            chunk(1, j)
                            chunk(2, j)
                        for half, (bank, job) in enumerate((("ctx", 1), ("trans", 2))):
                            o = fresh(bank, cn(bank, job))
                            m = A(yrow[0:CAP, half * 512:(half + 1) * 512], o[0:CAP, :], ACT.Copy)
                            if half:
                                m.then_inc(y_ready, 1)
                            act.drain().then_inc(free[bank], 1)

            exp_ln = "natural_log_exp_and_others"
            act.wait_ge(angle_ready, 1)
            A(sinT[:], tmp[:, 0], ACT.Sin)
            A(cosT[:], tmp[:, 1], ACT.Sin).then_inc(sin_ready, 1)
            act.preload_act_table_set(exp_ln)
            act.wait_ge(lam_dot, 1)
            for l in range(DEPTH):
                m = A(lams[:, l, 2:4], lams[:, l, 0:2], ACT.Exp)
            m.then_inc(lam_exp, 1)
            act.wait_ge(x_in, 16)
            act.wait_ge(eps_set, 1)
            for l in range(DEPTH):
                norm(l, 0, START[("norm", l, 0)].get("x", 0))
                latent(l)
                act.wait_ge(lat_ready, count(("latent", l), "lat", 3))
                with act.Fori(0, PAIRS) as i:
                    pair(l, i)
                merge(l)
                act.preload_act_table_set(exp_ln)
                norm(l, 1, count(("merge", l), "x", 4))
                if l % 2 == 0:
                    dense(l)
                    act.preload_act_table_set(exp_ln)
                else:
                    route(l)
            experts(0)
            act.wait_ge(rounds_ready, 1)
            n = act.value_load(nrnd[0:1, 0:1], min_val=1, max_val=MAX_ROUNDS)
            with act.If(n > 1):
                with act.Fori(1, n) as rnd:
                    experts(rnd)

        @block.vector
        def _(dve):
            V = nc.vector

            def fresh(bank, n):
                dve.wait_ge(full[bank], n + 1)
                return ps[bank]

            def then(*ops):
                for op in ops:
                    op()
                    dve.drain()

            def setup():
                V.memset(eps[:], EPS).then_inc(eps_set, 1)
                for n, s in enumerate(slot_free + list(free.values()) + [comb_done]):
                    V.memset(marks[:, n:n + 1], 0.0).then_inc(s, 1)
                dve.wait_ge(const_in, 80)
                V.tensor_copy(tmp[:, 0], posr[:])
                V.tensor_copy(poscf[:], posc[:])
                dve.drain()
                for q in range(TT):
                    V.tensor_scalar(dist[:, q], tmp[:, 0], poscf[:, q:q + 1], None, ALU.subtract)
                dve.drain()
                V.tensor_scalar(probT[:, 0], dist[:], -1.0, None, ALU.mult)
                dve.drain()
                V.tensor_tensor(dist[:], dist[:], probT[:, 0], ALU.max)
                ang, turns = tmp[:, 0], tmp[:, 1]
                then(lambda: V.tensor_scalar(ang, tmp[:, 0], c_("inv_freq"), None, ALU.mult),
                     lambda: V.tensor_scalar(turns, ang, float(0.5 / np.pi), None, ALU.mult),
                     lambda: V.tensor_scalar(turns, turns, ROUND, -ROUND, ALU.add, ALU.add),
                     lambda: V.scalar_tensor_tensor(ang, turns, -TWO_PI_HI, ang, ALU.mult, ALU.add),
                     lambda: V.scalar_tensor_tensor(ang, turns, -TWO_PI_MID, ang, ALU.mult, ALU.add),
                     lambda: V.scalar_tensor_tensor(ang, turns, -TWO_PI_LO, ang, ALU.mult, ALU.add),
                     lambda: V.tensor_scalar(turns, ang, float(np.pi / 2), float(np.pi), ALU.add, ALU.is_gt),
                     lambda: V.tensor_scalar(turns, turns, float(-2 * np.pi), float(np.pi / 2), ALU.mult, ALU.add),
                     lambda: V.tensor_tensor(turns, turns, ang, ALU.add),
                     lambda: V.tensor_scalar(ang, ang, PI_IN, -PI_IN, ALU.min, ALU.max))
                V.tensor_scalar(turns, turns, PI_IN, -PI_IN, ALU.min, ALU.max).then_inc(angle_ready, 1)
                for l in range(DEPTH):
                    V.tensor_tensor(lamv[:, l, 0:4:2], lamv[:, l, 0:4:2], lamv[:, l, 1:4:2], ALU.mult)
                    V.tensor_scalar(g_(l, "sub"), g_(l, "sub"), 1.0 - LAMBDA_INIT[l], None, ALU.mult)
                dve.drain()
                for l in range(DEPTH):
                    m = V.tensor_reduce(lams[:, l, 0:2], lamv[:, l, 0:4:2], AX.X, ALU.add)
                m.then_inc(lam_dot, 1)
                dve.wait_ge(lam_exp, 1)
                for l in range(DEPTH):
                    V.tensor_tensor(lams[:, l, 4:5], lams[:, l, 3:4], lams[:, l, 2:3], ALU.subtract)
                dve.drain()
                for l in range(DEPTH):
                    V.tensor_scalar(lams[:, l, 5:6], lams[:, l, 4:5], -LAMBDA_INIT[l], None, ALU.add)
                dve.wait_ge(sin_ready, 1)
                dve.wait_ge(x_in, 16)
                dve.drain()

            def root(value, at, width):
                dve.wait_ge(rs_ready, value)
                h, c = at
                y, m_ = rsp[:, h, c:c + width], msp[:, h, c:c + width]
                V.scalar_tensor_tensor(m_, m_, -0.5, y, ALU.mult, ALU.mult)
                dve.drain()
                V.tensor_tensor(m_, m_, y, ALU.mult)
                dve.drain()
                V.scalar_tensor_tensor(y, m_, 1.5, y, ALU.add, ALU.mult)
                dve.drain()
                return y

            def norm(l, which):
                ph = ("norm", l, which)
                y = root(count(ph, "rs", 1), (0, 0), T)
                for b in range(DB):
                    V.scalar_tensor_tensor(hT[:, b], xT[:, b], g_(l, "attn" if which == 0 else "ffn", b),
                                           y, ALU.mult, ALU.mult).then_inc(h_ready, 1)

            def latent(l):
                ph = ("latent", l)
                for s, (name, blocks) in enumerate((("q_lat", range(0, 4)), ("kv_lat", range(4, 6)), ("kr", range(6, 7)))):
                    r = root(count(ph, "rs", s + 1), (s // 2, (s % 2) * T), T)
                    for j, b in enumerate(blocks):
                        dst = latN[:, b] if s < 2 else gates[:, 14]
                        m = V.scalar_tensor_tensor(dst, gates[:, 8 + b], g_(l, name, j), r, ALU.mult, ALU.mult)
                    m.then_inc(lat_ready, 1)
                dve.drain()
                o = fresh("val", count(ph, "val", 0))
                V.tensor_tensor(tmp[:, 0], o[:, 0:T], sinT[:], ALU.mult).then_inc(free["val"], 1)
                V.tensor_tensor(tmp[:, 1], gates[:, 14], cosT[:], ALU.mult)
                dve.drain()
                V.tensor_tensor(krT[:], tmp[:, 0], tmp[:, 1], ALU.add).then_inc(kr_ready, 1)

            def pair(l, i):
                ph = ("pair", l)

                def cn(name, k):
                    return count(ph, name, k, i)

                def scale(g, name):
                    w = T if g == 2 else 2 * T
                    y = root(cn("rs", g + 1), (g % 2, 0), w)
                    V.scalar_tensor_tensor(qk[:, g, 0:w], qk[:, g, 0:w], g_(l, name), y,
                                           ALU.mult, ALU.mult).then_inc(qk_ready, 1)

                def values(dst, job):
                    o = fresh("val", cn("val", job))
                    V.tensor_copy(dst.rearrange("p a b -> p (a b)"), o[:]).then_inc(v_ready, 1)
                    dve.drain().then_inc(free["val"], 1)

                values(v_mla, 0)
                scale(0, "qn")
                scale(1, "kn")
                scale(2, "qr")
                values(v_diff, 1)
                scale(3, "dq")
                dve.drain()
                o = fresh("val", cn("val", 2))
                V.tensor_tensor(tmp[:, 0], o[:, 0:T], sinT[:], ALU.mult).then_inc(free["val"], 1)
                V.tensor_tensor(tmp[:, 1], qk[:, 2, 0:T], cosT[:], ALU.mult)
                dve.drain()
                V.tensor_tensor(qk[:, 2, T:2 * T], tmp[:, 0], tmp[:, 1], ALU.add).then_inc(qk_ready, 1)
                scale(4, "dk")

                for h in range(2):
                    o = fresh(f"score{h}", cn(f"score{h}", 0))
                    V.tensor_reduce(mx[:, 2 * h:2 * h + 2], o[:].rearrange("p (q t) -> p q t", t=T), AX.X, ALU.max)
                    dve.drain()
                    V.tensor_scalar(nmx[:, 2 * h:2 * h + 2], mx[:, 2 * h:2 * h + 2], -MLA_SCALE, None, ALU.mult)\
                        .then_inc(mla_max, 1)

                def diff_logits(h):
                    for c in range(2):
                        o = fresh(f"score{c}", cn(f"score{c}", 1 + h))
                        V.scalar_tensor_tensor(dprob[:, h, c].rearrange("p a b -> p (a b)"),
                                               dist[:].rearrange("p a b -> p (a b)"),
                                               cst[:, bass.ds(i * 2 + (CONST["slope"][0] + h), 1)], o[:],
                                               ALU.mult, ALU.add).then_inc(free[f"score{c}"], 1)
                    dve.drain()
                    n = 4 + 4 * h
                    V.tensor_reduce(mx[:, n:n + 4], dprob[:, h].rearrange("p c q t -> p (c q) t"), AX.X, ALU.max)
                    dve.drain()
                    V.tensor_scalar(nmx[:, n:n + 4], mx[:, n:n + 4], -DIFF_SCALE, None, ALU.mult).then_inc(diff_max, 1)

                def gate(bank, job, b0):
                    o = fresh(bank, cn(bank, job))
                    V.tensor_scalar(gates[:, bass.ds(i * 4 + b0, 2)], o[:].rearrange("p (b t) -> p b t", t=T),
                                    1.0, None, ALU.mult).then_inc(free[bank], 1)

                gate("proj1", 2, 0)
                diff_logits(0)
                for h in range(2):
                    dve.wait_ge(mla_exp, cn("p", h + 1))
                    V.reciprocal(rcp[:, 2 * h:2 * h + 2], sums[:, 2 * h:2 * h + 2])
                    dve.drain()
                    for q in range(TT):
                        m = V.tensor_scalar(prob[:, h, q], prob[:, h, q], rcp[:, 2 * h + q:2 * h + q + 1], None, ALU.mult)
                    m.then_inc(mla_prob, 1)

                def context(n, dst, h):
                    o = fresh("ctx", cn("ctx", n))
                    V.tensor_scalar(dst[:, bass.ds(i * 2 + h, 1)].rearrange("p a b -> p (a b)"), o[:, 0:T], 1.0, None,
                                    ALU.mult)\
                        .then_inc(free["ctx"], 1)

                for h in range(2):
                    context(h, oaT, h)
                diff_logits(1)
                gate("proj0", 3, 2)
                for h in range(2):
                    dve.wait_ge(diff_exp, cn("pd", h + 1))
                    n = 4 + 4 * h
                    V.reciprocal(rcp[:, n:n + 4], sums[:, n:n + 4])
                    dve.drain()
                    V.tensor_scalar(rcp[:, n + 2:n + 4], rcp[:, n + 2:n + 4], lams[:, l, 5:6], None, ALU.mult)
                    for q in range(TT):
                        V.tensor_scalar(dprob[:, h, 0, q], dprob[:, h, 0, q], rcp[:, n + q:n + q + 1], None, ALU.mult)
                    dve.drain()
                    for q in range(TT):
                        m = V.scalar_tensor_tensor(dprob[:, h, 0, q], dprob[:, h, 1, q], rcp[:, n + 2 + q:n + 3 + q],
                                                   dprob[:, h, 0, q], ALU.mult, ALU.add)
                    m.then_inc(diff_prob, 1)
                for h in range(2):
                    context(2 + h, obT, h)
                dve.drain()

            def merge(l):
                ph = ("merge", l)
                jobs = [0, 0]

                def job(bank):
                    o = fresh(f"proj{bank}", count(ph, f"proj{bank}", jobs[bank]))
                    jobs[bank] += 1
                    return o

                def two(ap, b):
                    return ap[:, b:b + 2].rearrange("p a b -> p (a b)")

                for g in range(4):
                    y = root(count(ph, "rs", g + 1), (g % 2, 0), 2 * T)
                    V.scalar_tensor_tensor(two(obT, 2 * g), two(obT, 2 * g), g_(l, "sub"), y,
                                           ALU.mult, ALU.mult).then_inc(ob_ready, 1)
                dve.wait_ge(gate_ready, count(ph, "sig", 1))
                for half in range(2):
                    for bank in range(2):
                        b = 4 * half + 2 * bank
                        V.tensor_tensor(two(merged, b), job(bank)[:], two(gates, b), ALU.mult)\
                            .then_inc(free[f"proj{bank}"], 1)
                    for bank in range(2):
                        b = 4 * half + 2 * bank
                        V.tensor_tensor(tmp[:].rearrange("p a b -> p (a b)"), job(bank)[:], two(gates, DB + b), ALU.mult)\
                            .then_inc(free[f"proj{bank}"], 1)
                        dve.drain()
                        V.tensor_tensor(two(merged, b), two(merged, b), tmp[:].rearrange("p a b -> p (a b)"), ALU.add)\
                            .then_inc(merged_ready, 1)
                        dve.drain()
                for half in range(2):
                    for bank in range(2):
                        b = 4 * half + 2 * bank
                        V.tensor_tensor(two(xT, b), two(xT, b), job(bank)[:], ALU.add).then_inc(x_ready, 1)
                        dve.drain().then_inc(free[f"proj{bank}"], 1)

            def dense(l):
                def hidden(ph, job, i, parity):
                    o = fresh("proj1", count(ph, "proj1", job, i))
                    dve.wait_ge(silu_ready, count(ph, "silu", job + 1, i))
                    V.tensor_tensor(hid[parity][:, 0:2 * T], o[:], silu[:, 0:2 * T], ALU.mult).then_inc(hid_ready, 1)
                    dve.drain().then_inc(free["proj1"], 1)

                def add(ph, job, i):
                    for q, bank in enumerate(("score0", "score1", "trans", "ctx")):
                        o = fresh(bank, count(ph, bank, job, i))
                        x2 = xT[:, 2 * q:2 * q + 2].rearrange("p a b -> p (a b)")
                        V.tensor_tensor(x2, x2, o[:], ALU.add).then_inc(x_ready, 1)
                        dve.drain().then_inc(free[bank], 1)

                first, loop, last = ("dense0", l), ("dense", l), ("dense1", l)
                hidden(first, 0, 0, 0)
                with dve.Fori(0, DENSE_CHUNKS // 2) as i:
                    hidden(loop, 0, i, 1)
                    add(loop, 0, i)
                    hidden(loop, 1, i, 0)
                    add(loop, 1, i)
                add(last, 0, 0)

            def route(l):
                ph = ("route", l)
                lg, oh1, l2, oh2, sc = (rt[:, n] for n in range(1, 6))
                sel, wt = rt[:, 0], rt[:, 6]
                o = fresh("val", count(ph, "val", 0))
                V.tensor_copy(lg.rearrange("p a b -> p (a b)"), o[:, 0:TT * EXPERTS]).then_inc(free["val"], 1)
                dve.drain()

                def best(src, m_, f_, onehot):
                    V.tensor_reduce(sc1[:, m_], src, AX.X, ALU.max)
                    dve.drain()
                    for t in range(TT):
                        V.scalar_tensor_tensor(sc[:, t], src[:, t], sc1[:, m_, t:t + 1], c_("first_wins"),
                                               ALU.is_equal, ALU.mult)
                    dve.drain()
                    V.tensor_reduce(sc1[:, f_], sc, AX.X, ALU.max)
                    dve.drain()
                    for t in range(TT):
                        V.tensor_scalar(onehot[:, t], c_("first_wins"), sc1[:, f_, t:t + 1], None, ALU.is_equal)
                    dve.drain()

                best(lg, 0, 1, oh1)
                V.scalar_tensor_tensor(l2, oh1, -3.0e38, lg, ALU.mult, ALU.add)
                dve.drain()
                best(l2, 2, 1, oh2)
                V.tensor_tensor(sel, oh1, oh2, ALU.add).then_inc(sel_ready, 1)
                V.tensor_tensor(sc1[:, 3], sc1[:, 2], sc1[:, 0], ALU.subtract).then_inc(route_exp_in, 1)
                dve.wait_ge(route_exp_out, 1)
                V.tensor_scalar(sc1[:, 5], sc1[:, 4], 1.0, None, ALU.add)
                dve.drain()
                V.reciprocal(sc1[:, 6], sc1[:, 5])
                dve.drain()
                V.tensor_tensor(sc1[:, 7], sc1[:, 6], sc1[:, 4], ALU.mult)
                dve.drain()
                for t in range(TT):
                    V.tensor_scalar(wt[:, t], oh1[:, t], sc1[:, 6, t:t + 1], None, ALU.mult)
                dve.drain()
                for t in range(TT):
                    V.scalar_tensor_tensor(wt[:, t], oh2[:, t], sc1[:, 7, t:t + 1], wt[:, t], ALU.mult, ALU.add)
                o = fresh("val", count(ph, "val", 1))
                E = EXPERTS
                place = rt[:, 7]
                V.tensor_copy(place.rearrange("p a b -> p (a b)"), o[:, 0:2 * E])
                V.tensor_reduce(cnt[:, E:E + 1], o[:, 2 * E:3 * E], AX.X, ALU.max)
                dve.drain().then_inc(free["val"], 1)
                V.tensor_scalar(sc, sel, -1.0e6, 1.0e6, ALU.mult, ALU.add)
                for r in range(MAX_ROUNDS):
                    V.tensor_scalar(cnt[:, r:r + 1], cnt[:, E:E + 1], float(CAP * r), None, ALU.is_gt)
                dve.drain()
                V.tensor_tensor(place, place, sc, ALU.add)
                V.tensor_reduce(cnt[:, E + 1:E + 2], cnt[:, 0:MAX_ROUNDS], AX.X, ALU.add)
                dve.drain()
                V.tensor_copy(nrnd[:], cnt[:, E + 1:E + 2]).then_inc(rounds_ready, 1)
                dve.drain()
                dve.wait_ge(xtok_ready, 4)
                dve.wait_ge(htok_ready, 4)

            def experts(rnd):
                place, wt = rt[:, 7], rt[:, 6]
                with dve.Fori(0, EXPERTS // 2) as pair_:
                    for par in range(2):
                        def cn(name, k, j=0, per_j=0):
                            return moe_count(name, k, rnd, pair_, par, j, per_j)

                        dve.wait_ge(comb_done, cn("comb", 0) + 1)
                        e = pair_ * 2 + par
                        for t in range(TT):
                            V.tensor_scalar(G[par][:, t], c_("slot_no"), place[:, t, bass.ds(e, 1)], None, ALU.is_equal)
                            m = V.tensor_scalar(Gw[:, t], c_("slot_no"), place[:, t, bass.ds(e, 1)],
                                                wt[:, t, bass.ds(e, 1)], ALU.is_equal, ALU.mult)
                        m.then_inc(gather_ready, 1)
                        V.memset(yT, 0.0)
                        dve.drain()

                        def hidden(c0, job, j=0):
                            o = fresh("proj1", cn("proj1", job, j, 2))
                            dve.wait_ge(silu_ready, cn("silu", job + 1, j, 2))
                            V.tensor_tensor(hid[(par + c0) % 2][:, 0:4 * CAP], o[:, 0:4 * CAP], silu[:, 0:4 * CAP],
                                            ALU.mult).then_inc(hid_ready, 1)
                            dve.drain().then_inc(free["proj1"], 1)

                        def add(job, j=0):
                            for half in range(2):
                                o = fresh(f"score{half}", cn(f"score{half}", job, j, 2))
                                y = yT[:, half * 4 * CAP:(half + 1) * 4 * CAP]
                                m = V.tensor_tensor(y, y, o[:, 0:4 * CAP], ALU.add)
                                if half:
                                    m.then_inc(yadd_done, 1)
                                dve.drain().then_inc(free[f"score{half}"], 1)

                        hidden(0, 0)
                        with dve.Fori(0, EXP_CHUNKS // 2) as j:
                            hidden(1, 1, j)
                            add(0, j)
                            hidden(2, 2, j)
                            add(1, j)
                        add(6)
                        for t in range(TT):
                            for half, bank in enumerate(("val", "stat")):
                                o = fresh(bank, cn(bank, t))
                                a = acc[:, t, half * 512:(half + 1) * 512]
                                m = V.tensor_tensor(a, a, o[:], ALU.add)
                                if t and half:
                                    m.then_inc(comb_done, 1)
                                dve.drain().then_inc(free[bank], 1)
                V.tensor_scalar(place, place, float(-CAP), None, ALU.add)
                dve.drain()

            setup()
            for l in range(DEPTH):
                norm(l, 0)
                latent(l)
                with dve.Fori(0, PAIRS) as i:
                    pair(l, i)
                merge(l)
                norm(l, 1)
                if l % 2 == 0:
                    dense(l)
                else:
                    route(l)
            experts(0)
            n = dve.value_load(nrnd[0:1, 0:1], min_val=1, max_val=MAX_ROUNDS)
            with dve.If(n > 1):
                with dve.Fori(1, n) as rnd:
                    experts(rnd)
            dve.drain().then_inc(out_ready, 1)


def constants():
    c = np.zeros((P, CONST_COLS), np.float32)

    def put(name, a):
        c[:, CONST[name][0]:CONST[name][1]] = a

    p = np.arange(P)
    put("ident", np.eye(P))
    put("ones", 1.0)
    put("half_ones", p[:, None] // 64 == p[None, :] // 64)
    rot = np.zeros((P, P))
    for m in range(P):
        rot[m + 32 if m % 64 < 32 else m - 32, m] = -1.0 if m % 64 < 32 else 1.0
    put("rot", rot)
    put("before", p[:, None] < p[None, :])
    put("slot_no", np.arange(CAP)[None])
    put("first_wins", np.arange(EXPERTS, 0, -1)[None])
    half = ROPE // 2
    freq = np.float32(10000.0) ** (-np.arange(half, dtype=np.float32) / np.float32(half))
    put("inv_freq", freq[p % half][:, None])
    put("slope", -(2.0 ** -(np.arange(1, HEADS + 1))) * (1 / DIFF_SCALE))
    return c


def layout(a):
    f = {k: np.asarray(v) for k, v in a.items()}
    L = DEPTH

    def kp(w, blocks):
        return np.moveaxis(w.reshape(w.shape[:-2] + (blocks, P, w.shape[-1])), -3, -2)

    def cols(v):
        return v.reshape(L, -1, P).transpose(2, 0, 1)

    def twice(v):
        return cols(np.concatenate([v, v], axis=1))

    gains = np.concatenate([cols(f["attn_norm_g"]), cols(f["ffn_norm_g"]), cols(f["mla_q_norm_g"]),
                            cols(f["mla_kv_norm_g"]), cols(f["mla_qn_nope_g"]), twice(f["mla_qn_rope_g"]),
                            cols(f["mla_kn_nope_g"]), twice(f["mla_kn_rope_g"]), twice(f["diff_qn_g"]),
                            twice(f["diff_kn_g"]), cols(f["diff_subln_g"])], axis=2)
    lam = np.stack([f["diff_lam_q1"], f["diff_lam_k1"], f["diff_lam_q2"], f["diff_lam_k2"]], axis=1)
    w_in = kp(f["w_in"], DB)
    kr = w_in[..., 768:832]
    w_lat = np.concatenate([w_in[..., 0:512].reshape(L, P, -1),
                            np.concatenate([w_in[..., 512:768], kr, kr], axis=-1).reshape(L, P, -1)], axis=2)

    def by_pair(w, n):
        return np.moveaxis(w.reshape(w.shape[:3] + (PAIRS, n)), 3, 1).reshape(L * PAIRS, P, w.shape[2], n)

    uq = by_pair(kp(f["mla_w_uq"], QLB), 384)
    ukv = by_pair(kp(f["mla_w_ukv"], KLB), 512)
    w_heads = np.concatenate([
        np.concatenate([uq[..., 0:128], uq[..., 192:320], uq[..., 128:192], uq[..., 320:384]], -1).reshape(L * PAIRS, P, -1),
        np.concatenate([ukv[..., 0:128], ukv[..., 256:384], ukv[..., 128:256], ukv[..., 384:512]], -1).reshape(L * PAIRS, P, -1)],
        axis=2)
    dq, dk, dv = (by_pair(w_in[..., 832 + n * 1024:832 + (n + 1) * 1024], 256).reshape(L * PAIRS, P, -1) for n in range(3))
    w_dqk = np.concatenate([dq, dk], axis=2)
    w_gates = by_pair(kp(f["w_gate"], DB), 512).reshape(L * PAIRS, P, -1)
    wa, wb, wo = (kp(f[n], DB) for n in ("w_branch_a", "w_branch_b", "w_out"))
    w_merge = np.stack([w[..., h * 512:(h + 1) * 512].reshape(L, P, -1)
                        for w, h in ((wa, 0), (wb, 0), (wa, 1), (wb, 1), (wo, 0), (wo, 1))], axis=1)
    C = DENSE_CHUNKS
    g, u = (np.moveaxis(kp(f[n][0], DB).reshape(P, DB, C, 256), 2, 0).reshape(C, P, -1)
            for n in ("dense_w_gate", "dense_w_up"))
    w_gu = np.concatenate([g, u], axis=2)
    w_dn = f["dense_w_down"][0].reshape(C, 2, P, D).transpose(0, 2, 1, 3).reshape(C, P, -1)
    w_router = kp(f["moe_w_router"][0], DB).reshape(P, -1)
    E, C = EXPERTS, EXP_CHUNKS
    g, u = (np.moveaxis(kp(f[n][0], DB).reshape(E, P, DB, C, 512), 3, 1).reshape(E, C, P, SLOT)
            for n in ("moe_w_gate", "moe_w_up"))
    d = f["moe_w_down"][0].reshape(E, C, 4, P, D).transpose(0, 1, 3, 2, 4).reshape(E, C, P, SLOT)
    w_exp = np.stack([g, u, d], axis=2).reshape(E * C * 3, P, SLOT)
    pos = f["positions"]
    return dict(
        x_t=f["x"][0].T.reshape(DB, P, T).transpose(1, 0, 2), pos_row=np.repeat(pos, P, axis=0),
        pos_col=pos.reshape(TT, P).T, const=constants(), gains=gains,
        lam_vecs=np.broadcast_to(lam[None], (P, L, 4, 64)), w_lat=w_lat, w_heads=w_heads, w_dqk=w_dqk, w_dv=dv,
        w_gates=w_gates, w_merge=w_merge, w_gu=w_gu, w_dn=w_dn, w_router=w_router, w_exp=w_exp)


def kernel(**inputs):
    import concourse.bacc as bacc
    from concourse.bass_utils import run_bass_kernel_spmd

    nc = bacc.Bacc("TRN2", target_bir_lowering=False, num_devices=1)
    arrays = {f"in_{k}": np.ascontiguousarray(v) for k, v in layout(inputs).items()}
    args = [nc.dram_tensor(k, v.shape, mybir.dt.from_np(v.dtype), kind="ExternalInput").ap() for k, v in arrays.items()]
    out = nc.dram_tensor("out_rows", (T, D), F32, kind="ExternalOutput").ap()
    build(nc, *args, out)
    r = run_bass_kernel_spmd(nc, [arrays], core_ids=[0])
    return r.results[0]["out_rows"].reshape(1, T, D)
```

```python
from contextlib import ExitStack

import numpy as np

import concourse.bass as bass
from concourse import mybir

F32 = mybir.dt.float32
F32R = mybir.dt.float32r
I32 = mybir.dt.int32
ALU = mybir.AluOpType
ACT = mybir.ActivationFunctionType
AX = mybir.AxisListType

P = 128
T = 256
TT = T // P
D = 1024
DB = D // P
DEPTH = 2
HEADS = 8
PAIRS = HEADS // 2
QLB, KLB = 4, 2
ROPE = 64
EPS = 1e-6
MLA_SCALE = float((128 + 64) ** -0.5)
DIFF_SCALE = float(64 ** -0.5)
DENSE_CHUNKS = 2816 // 256
EXPERTS = 8
EXP_CHUNKS = 3584 // 512
CAP = P
MAX_ROUNDS = -(-T // CAP)
SLOT = 4096
TWO_PI_HI, TWO_PI_MID = 6.28125, 0.0019350051879882812
TWO_PI_LO = float(2 * np.pi - 6.28125 - 0.0019350051879882812)
PI_IN = 3.1415925
ROUND = 12582912.0

LAMBDA_INIT = [0.8 - 0.6 * float(np.exp(-0.3 * l)) for l in range(DEPTH)]

CONST = {}
_at = 0
for _name, _n in (("ident", P), ("ones", P), ("half_ones", P), ("rot", P), ("before", P),
                  ("slot_no", CAP), ("first_wins", EXPERTS), ("inv_freq", 1), ("slope", HEADS)):
    CONST[_name] = (_at, _at + _n)
    _at += _n
CONST_COLS = _at

GAIN = {}
_at = 0
for _name, _n in (("attn", DB), ("ffn", DB), ("q_lat", QLB), ("kv_lat", KLB), ("qn", 1), ("qr", 1),
                  ("kn", 1), ("kr", 1), ("dq", 1), ("dk", 1), ("sub", 1)):
    GAIN[_name] = (_at, _at + _n)
    _at += _n
GAIN_COLS = _at

BANKS = ("proj0", "proj1", "stat", "score0", "score1", "trans", "ctx", "val")
PHASES = []
for _l in range(DEPTH):
    PHASES += [
        (("norm", _l, 0), 1, dict(stat=1, sq=2, rs=1, h=DB)),
        (("latent", _l), 1, dict(proj0=2, proj1=2, stat=3, val=1, sq=4, rs=3, lat=3, kr=1, s4=1, s5=1)),
        (("pair", _l), PAIRS, dict(proj0=4, proj1=3, stat=5, score0=3, score1=3, trans=4, ctx=4, val=3,
                                   sq=5, rs=5, qk=6, v=2, mx=2, dmx=2, p=2, pd=2, pn=2, w=2, pt=4,
                                   gate=2, s0=1, s1=1, s2=1, s3=1)),
        (("merge", _l), 1, dict(proj0=6, proj1=6, stat=4, sq=1, rs=4, ob=4, sig=1, mg=4, x=4,
                                s0=1, s1=1, s2=1, s3=1, s4=1, s5=1)),
        (("norm", _l, 1), 1, dict(stat=1, sq=2, rs=1, h=DB)),
    ]
    if _l % 2 == 0:
        PHASES += [
            (("dense0", _l), 1, dict(proj0=1, proj1=1, silu=1, hid=1, s0=1)),
            (("dense", _l), DENSE_CHUNKS // 2, dict(proj0=2, proj1=2, score0=2, score1=2, trans=2, ctx=2,
                                                    silu=2, hid=2, x=8, s0=1, s1=1, s2=1, s3=1)),
            (("dense1", _l), 1, dict(score0=1, score1=1, trans=1, ctx=1, x=4, s1=1)),
        ]
    else:
        PHASES += [
            (("route", _l), 1, dict(val=2, trans=2, ctx=2, score0=2, score1=2, htok=4, xtok=4)),
        ]
START, _c = {}, {}
for _key, _trips, _per in PHASES:
    START[_key] = dict(_c)
    for _s, _n in _per.items():
        _c[_s] = _c.get(_s, 0) + _trips * _n
PER = {k: p for k, _, p in PHASES}
MOE_START = dict(_c)
def count(phase, name, k, i=0):
    start, per = START[phase].get(name, 0), PER[phase][name]
    return i * per + (start + k) if not isinstance(i, int) else start + i * per + k


MOE_PAIR = dict(proj0=14, proj1=14, trans=14, score0=2, score1=2, ctx=6, val=6, stat=2, hi=84, split=84, used=84,
                silu=14, hid=14, hthi=14, ht=14, g=2, hehi=4, he=2, st=2, y=2, comb=2, zero=0)
MOE_SLOTS = 7
GRAN = SLOT // 2
RING = 4


MOE_OPEN = dict(ctx=1, val=1, hehi=2, he=1, g=1, stat=1, st=1, score0=1, score1=1, zero=1)
MOE_CLOSE = dict(ctx=2, val=2, y=1, comb=1)


def moe_count(name, k, rnd, pair, j=0, per_j=0, opening=False):
    n, own = MOE_PAIR[name], MOE_OPEN.get(name, 0)
    v = MOE_START.get(name, 0) + k + (0 if opening else own)
    for reg, per in ((rnd, EXPERTS // 2 * n + own + MOE_CLOSE.get(name, 0)), (pair, n), (j, per_j)):
        v = v + reg * per if isinstance(reg, int) else reg * per + v
    return v


def slot_count(slot, k, rnd, pair, j=0):
    v = MOE_START.get(f"s{slot}", 0) + k
    for reg, per in ((rnd, EXPERTS // 2 * MOE_SLOTS), (pair, MOE_SLOTS), (j, 1)):
        v = v + reg * per if isinstance(reg, int) else reg * per + v
    return v


def step_items(t):
    s = t % 2
    gate, up = (("gate", t, 3 * s, t // 2), ("up", t, 3 * s + 1, t // 2))
    down = ("down", t - 1, 3 * s + 2, t // 2 - (1 - s))
    if t == 0:
        return [gate, up]
    if t == EXP_CHUNKS:
        return [down, gate, up]
    if t == 2 * EXP_CHUNKS:
        return [down]
    return [gate, up, down]


def granules_before(t):
    return 0 if t == 0 else 6 * t - 2


def build(nc, x_t, pos_row, pos_col, const, gains, lam_vecs, w_lat, w_heads, w_dqk, w_dv, w_gates, w_merge,
          w_gu, w_dn, w_router, w_exp, out):
    with ExitStack() as ctx:
        def sb(name, shape, dt=F32):
            return ctx.enter_context(nc.sbuf_tensor(name, [P] + shape, dt))

        def sem(name):
            return ctx.enter_context(nc.semaphore(name))

        slots = [sb(f"slot{s}", [SLOT]) for s in range(6)]
        gates = sb("gates", [2 * DB, T])
        cst = sb("cst", [CONST_COLS])
        gn = sb("gn", [DEPTH, GAIN_COLS])
        lams = sb("lams", [DEPTH, 8])
        poscf = sb("poscf", [TT])
        eps = sb("eps", [1])
        marks = sb("marks", [24])
        mx, nmx, sums = sb("mx", [12]), sb("nmx", [12]), sb("sums", [12])
        rcp = sb("rcp", [12])
        rt = sb("rt", [16, TT, EXPERTS])
        sc1 = sb("sc1", [16, TT])
        cnt = sb("cnt", [EXPERTS + 8])
        nrnd = sb("nrnd", [1], I32)
        place = sb("place", [TT, EXPERTS + 2])
        wt = sb("wt", [TT, EXPERTS + 2])

        shared = ExitStack()

        def sa(name, shape, dt=F32):
            return shared.enter_context(nc.sbuf_tensor(name, [P] + shape, dt))

        qk = sa("qk", [5, 2 * T])
        oaT, obT = sa("oaT", [DB, T]), sa("obT", [DB, T])
        latN = sa("latN", [QLB + KLB, T])
        prob = sa("prob", [2, TT, T])
        dprob = sa("dprob", [2, 2, TT, T])
        krT = sa("krT", [T])
        cosT, sinT = sa("cosT", [T]), sa("sinT", [T])
        dist = sa("dist", [TT, T])
        lamv = sa("lamv", [DEPTH, 4, 64])
        posr, posc = sa("posr", [T], I32), sa("posc", [TT], I32)
        tmp = sa("tmp", [2, T])
        rsp = sa("rsp", [2, 2 * T])
        msp = sa("msp", [2, 2 * T])
        probT = sa("probT", [2, TT, T])
        xT = sa("xT", [DB, T])
        hT = sa("hT", [DB, T])
        merged = sa("merged", [DB, T])
        flat_mg = merged[:].rearrange("p a b -> p (a b)")
        sqp = flat_mg[:, 0:4 * T].rearrange("p (a b) -> p a b", a=2)
        v_mla, v_diff = (flat_mg[:, n * 2 * T:(n + 1) * 2 * T].rearrange("p (a b) -> p a b", a=TT) for n in (2, 3))
        silu = prob[:].rearrange("p a b c -> p (a b c)")
        hid = [dprob[:, i].rearrange("p a b c -> p (a b c)") for i in range(2)]
        wr = probT[:].rearrange("p a b c -> p (a b c)")[:, 0:DB * EXPERTS]
        htok = gates[:, 0:8].rearrange("p a b -> p (a b)").rearrange("p (t d) -> p t d", t=TT)
        acc = gates[:, 8:16].rearrange("p a b -> p (a b)").rearrange("p (t d) -> p t d", t=TT)
        shared.close()
        w_hi = [sb(f"w_hi{n}", [GRAN], F32R) for n in range(RING)]
        w_lo = [sb(f"w_lo{n}", [GRAN], F32R) for n in range(RING)]
        he_hi = sb("he_hi", [DB, CAP], F32R)
        he_lo = sb("he_lo", [DB, CAP], F32R)
        hidT_hi, hidT_lo = sb("hidT_hi", [4, CAP], F32R), sb("hidT_lo", [4, CAP], F32R)
        silu_e, hid_e = sb("silu_e", [4 * P]), sb("hid_e", [4 * P])
        yrow = sb("yrow", [D])
        G = [sb(f"G{n}", [TT, CAP]) for n in range(2)]
        Gw = sb("Gw", [TT, CAP])
        S = [sb(f"S{n}", [T]) for n in range(2)]

        ps = {b: ctx.enter_context(nc.psum_tensor(f"ps_{b}", [P, 2 * T], F32)) for b in BANKS}
        full = {b: sem(f"{b}_full") for b in BANKS}
        free = {b: sem(f"{b}_free") for b in BANKS}
        slot_full = [sem(f"slot{s}_full") for s in range(6)]
        slot_free = [sem(f"slot{s}_free") for s in range(6)]
        const_in = sem("const_in")
        x_in = sem("x_in")
        router_in = sem("router_in")
        eps_set = sem("eps_set")
        angle_ready = sem("angle_ready")
        sin_ready = sem("sin_ready")
        lam_dot = sem("lam_dot")
        lam_exp = sem("lam_exp")
        x_ready = sem("x_ready")
        sq_ready = sem("sq_ready")
        rs_ready = sem("rs_ready")
        h_ready = sem("h_ready")
        lat_ready = sem("lat_ready")
        kr_ready = sem("kr_ready")
        qk_ready = sem("qk_ready")
        v_ready = sem("v_ready")
        mla_max = sem("mla_max")
        diff_max = sem("diff_max")
        mla_exp = sem("mla_exp")
        diff_exp = sem("diff_exp")
        mla_prob = sem("mla_prob")
        diff_prob = sem("diff_prob")
        probT_ready = sem("probT_ready")
        gate_raw = sem("gate_raw")
        ob_ready = sem("ob_ready")
        gate_ready = sem("gate_ready")
        merged_ready = sem("merged_ready")
        silu_ready = sem("silu_ready")
        hid_ready = sem("hid_ready")
        route_exp_in = sem("route_exp_in")
        route_exp_out = sem("route_exp_out")
        sel_ready = sem("sel_ready")
        htok_ready = sem("htok_ready")
        xtok_ready = sem("xtok_ready")
        rounds_ready = sem("rounds_ready")
        gather_ready = sem("gather_ready")
        hi_ready = sem("hi_ready")
        split_ready = sem("split_ready")
        split_free = sem("split_free")
        he_hi_ready = sem("he_hi_ready")
        he_ready = sem("he_ready")
        hidT_hi_ready = sem("hidT_hi_ready")
        hidT_ready = sem("hidT_ready")
        scatter_ready = sem("scatter_ready")
        y_ready = sem("y_ready")
        comb_done = sem("comb_done")
        zero_ready = sem("zero_ready")
        out_ready = sem("out_ready")
        out_sent = sem("out_sent")

        def c_(name):
            a, b = CONST[name]
            return cst[:, a:b]

        def g_(l, name, j=0):
            a = GAIN[name][0] + j
            return gn[:, l, a:a + 1]

        def blk(ap, b, n=P):
            return ap[:, b * n:(b + 1) * n]

        block = ctx.enter_context(nc.Block())

        @block.sync
        def _(sp):
            sp.dma_start(xT[:], x_t).then_inc(x_in, 16)
            for dst, src in ((cst[:], const), (gn[:], gains), (lamv[:], lam_vecs), (posr[:], pos_row),
                             (posc[:], pos_col)):
                sp.dma_start(dst, src).then_inc(const_in, 16)

            def load(slot, before, src, width=SLOT):
                sp.wait_ge(slot_free[slot], before + 1)
                sp.dma_start(slots[slot][:, 0:width], src).then_inc(slot_full[slot], 16)

            def one(arr, i):
                return arr[bass.ds(i, 1)].rearrange("a p n -> p (a n)")

            for l in range(DEPTH):
                load(4, count(("latent", l), "s4", 0), w_lat[l, :, 0:4096])
                load(5, count(("latent", l), "s5", 0), w_lat[l, :, 4096:4096 + 3072], 3072)
                with sp.Fori(0, PAIRS) as i:
                    for s, arr in enumerate((w_heads, w_dqk, w_dv, w_gates)):
                        load(s, count(("pair", l), f"s{s}", 0, i), one(arr, i + l * PAIRS), arr.shape[2])
                for s, piece in ((4, 0), (5, 1), (0, 2), (1, 3), (2, 4), (3, 5)):
                    load(s, count(("merge", l), f"s{s}", 0), w_merge[l, piece])
                if l % 2 == 0:
                    load(0, count(("dense0", l), "s0", 0), w_gu[0])
                    load(1, count(("dense", l), "s1", 0), w_dn[0], 2048)
                    with sp.Fori(0, DENSE_CHUNKS // 2) as i:
                        load(2, count(("dense", l), "s2", 0, i), one(w_gu, i * 2 + 1))
                        load(3, count(("dense", l), "s3", 0, i), one(w_dn, i * 2 + 1), 2048)
                        load(0, count(("dense", l), "s0", 0, i), one(w_gu, i * 2 + 2))
                        load(1, count(("dense", l), "s1", 1, i), one(w_dn, i * 2 + 2), 2048)

            sp.wait_ge(x_ready, count(("merge", 1), "x", 4))
            sp.dma_start(wr, w_router).then_inc(router_in, 16)

            def experts(rnd):
                with sp.Fori(0, EXPERTS // 2) as pair:
                    def step(t, j=0):
                        for kind, chunk, slot, used in step_items(t):
                            at = chunk * 3 + ("gate", "up", "down").index(kind)
                            idx = pair * (2 * EXP_CHUNKS * 3)
                            idx = idx + at if isinstance(j, int) else idx + j * 6 + at
                            load(slot, slot_count(slot, used, rnd, pair, j), one(w_exp, idx))

                    step(0)
                    for t0 in (1, EXP_CHUNKS + 1):
                        with sp.Fori(0, EXP_CHUNKS // 2) as j:
                            step(t0, j)
                            step(t0 + 1, j)
                        step(t0 + EXP_CHUNKS - 1)

            experts(0)
            sp.wait_ge(rounds_ready, 1)
            n = sp.value_load(nrnd[0:1, 0:1], min_val=1, max_val=MAX_ROUNDS)
            with sp.If(n > 1):
                with sp.Fori(1, n) as rnd:
                    experts(rnd)
            sp.wait_ge(out_ready, 1)
            sp.dma_start(out.rearrange("(t p) d -> p t d", p=P), acc).then_inc(out_sent, 16)
            sp.wait_ge(out_sent, 16)

        @block.tensor
        def _(pe):
            def take(bank, n):
                pe.wait_ge(free[bank], n + 1)
                return ps[bank]

            def need(slot, before):
                pe.wait_ge(slot_full[slot], before * 16 + 16)

            owed = []

            def release(sem_):
                owed.append(sem_)

            def settle():
                while owed:
                    nc.tensor.drain().then_inc(owed.pop(0), 1)

            def mm(out_, lhsT, rhs, k, n):
                m = nc.tensor.matmul(out_, lhsT, rhs, start=(k == 0), stop=(k == n - 1))
                if owed and k < n - 1:
                    m.then_inc(owed.pop(0), 1)
                return m

            def norm(l, which):
                ph = ("norm", l, which)
                o = take("stat", count(ph, "stat", 0))
                for k in range(DB):
                    if k % 4 == 0:
                        pe.wait_ge(sq_ready, count(ph, "sq", k // 4 + 1))
                    m = mm(o[:, 0:T], c_("ones"), merged[:, k], k, DB)
                m.then_inc(full["stat"], 1)

            def latent(l):
                ph = ("latent", l)
                need(4, count(ph, "s4", 0))
                for job in range(2):
                    o = take(f"proj{job}", count(ph, f"proj{job}", 0))
                    for b in range(2):
                        for k in range(DB):
                            if job == 0 and b == 0:
                                pe.wait_ge(h_ready, count(("norm", l, 0), "h", k + 1))
                            c = (k * 4 + job * 2 + b) * P
                            m = mm(o[:, b * T:(b + 1) * T], slots[4][:, c:c + P], hT[:, k], k, DB)
                    m.then_inc(full[f"proj{job}"], 1)
                release(slot_free[4])
                need(5, count(ph, "s5", 0))
                for job in range(2):
                    o = take(f"proj{job}", count(ph, f"proj{job}", 1))
                    for b in range(2 - job):
                        for k in range(DB):
                            c = (k * 3 + job * 2 + b) * P
                            m = mm(o[:, b * T:(b + 1) * T], slots[5][:, c:c + P], hT[:, k], k, DB)
                    m.then_inc(full[f"proj{job}"], 1)
                release(slot_free[5])
                for s, (sq_n, ones, blocks) in enumerate(((2, "ones", range(0, 4)), (3, "ones", range(4, 6)),
                                                          (4, "half_ones", range(6, 7)))):
                    pe.wait_ge(sq_ready, count(ph, "sq", sq_n))
                    o = take("stat", count(ph, "stat", s))
                    for k, b in enumerate(blocks):
                        m = mm(o[:, 0:T], c_(ones), gates[:, b], k, len(blocks))
                    m.then_inc(full["stat"], 1)
                pe.wait_ge(lat_ready, count(ph, "lat", 3))
                o = take("val", count(ph, "val", 0))
                mm(o[:, 0:T], c_("rot"), gates[:, 14], 0, 1).then_inc(full["val"], 1)

            def pair(l, i):
                ph = ("pair", l)

                def cn(name, k):
                    return count(ph, name, k, i)

                def stat(g):
                    pe.wait_ge(sq_ready, cn("sq", g + 1))
                    o = take("stat", cn("stat", g))
                    w = T if g == 2 else 2 * T
                    mm(o[:, 0:w], c_("ones" if g < 2 else "half_ones"), sqp[:, g % 2, 0:w], 0, 1)\
                        .then_inc(full["stat"], 1)

                heads = slots[0][:, 0:2560]
                uq = heads[:, 0:1536].rearrange("p (k c) -> p k c", k=QLB)
                ukv = heads[:, 1536:2560].rearrange("p (k c) -> p k c", k=KLB)
                need(0, cn("s0", 0))
                pe.wait_ge(lat_ready, count(("latent", l), "lat", 2))
                o = take("proj0", cn("proj0", 0))
                for h in range(2):
                    for k in range(QLB):
                        m = mm(o[:, h * T:(h + 1) * T], blk(uq[:, k], h), latN[:, k], k, QLB)
                m.then_inc(full["proj0"], 1)
                o = take("proj1", cn("proj1", 0))
                for h in range(2):
                    for k in range(KLB):
                        m = mm(o[:, h * T:(h + 1) * T], blk(ukv[:, k], h), latN[:, QLB + k], k, KLB)
                m.then_inc(full["proj1"], 1)
                stat(0)
                o = take("proj0", cn("proj0", 1))
                for k in range(QLB):
                    m = mm(o[:, 0:T], blk(uq[:, k], 2), latN[:, k], k, QLB)
                m.then_inc(full["proj0"], 1)
                stat(1)
                o = take("val", cn("val", 0))
                for t in range(TT):
                    for k in range(KLB):
                        m = mm(o[:, t * T:(t + 1) * T], latN[:, QLB + k, t * P:(t + 1) * P],
                               ukv[:, k, 2 * P:4 * P], k, KLB)
                m.then_inc(full["val"], 1)
                release(slot_free[0])

                dqk = slots[1][:].rearrange("p (m k c) -> p m k c", m=2, k=DB)

                def diff_head(o, m_, h):
                    for k in range(DB):
                        m = mm(o[:, h * T:(h + 1) * T], blk(dqk[:, m_, k], h), hT[:, k], k, DB)
                    return m

                need(1, cn("s1", 0))
                o = take("proj1", cn("proj1", 1))
                diff_head(o, 0, 0)
                stat(2)
                diff_head(o, 0, 1).then_inc(full["proj1"], 1)
                o = take("proj0", cn("proj0", 2))
                diff_head(o, 1, 0)
                stat(3)
                pe.wait_ge(qk_ready, cn("qk", 3))
                rot = take("val", cn("val", 1))
                mm(rot[:, 0:T], c_("rot"), qk[:, 2, 0:T], 0, 1).then_inc(full["val"], 1)
                diff_head(o, 1, 1).then_inc(full["proj0"], 1)
                release(slot_free[1])

                dv = slots[2][:, 0:2048].rearrange("p (k c) -> p k c", k=DB)
                need(2, cn("s2", 0))
                o = take("val", cn("val", 2))
                for t in range(TT):
                    for k in range(DB):
                        m = mm(o[:, t * T:(t + 1) * T], hT[:, k, t * P:(t + 1) * P], dv[:, k], k, DB)
                    if t == 0:
                        stat(4)
                m.then_inc(full["val"], 1)
                release(slot_free[2])

                gw = slots[3][:].rearrange("p (k c) -> p k c", k=DB)

                def gate(o, b, ks=range(DB)):
                    for k in ks:
                        m = mm(o[:, b % 2 * T:(b % 2 + 1) * T], blk(gw[:, k], b), hT[:, k], k, DB)
                    return m

                pe.wait_ge(qk_ready, cn("qk", 4))
                pe.wait_ge(kr_ready, count(("latent", l), "kr", 1))
                for h in range(2):
                    o = take(f"score{h}", cn(f"score{h}", 0))
                    for q in range(TT):
                        mm(o[:, q * T:(q + 1) * T], qk[:, 0, h * T + q * P:h * T + (q + 1) * P],
                           qk[:, 1, h * T:(h + 1) * T], 0, 2)
                        m = mm(o[:, q * T:(q + 1) * T], qk[64 * h:64 * h + 64, 2, T + q * P:T + (q + 1) * P],
                               krT[64 * h:64 * h + 64, :], 1, 2)
                    m.then_inc(full[f"score{h}"], 1)

                def diff_scores(h):
                    if h == 0:
                        pe.wait_ge(qk_ready, cn("qk", 6))
                    for c in range(2):
                        o = take(f"score{c}", cn(f"score{c}", 1 + h))
                        for q in range(TT):
                            r = slice(64 * c, 64 * c + 64)
                            m = mm(o[:, q * T:(q + 1) * T], qk[r, 3, h * T + q * P:h * T + (q + 1) * P],
                                   qk[r, 4, h * T:(h + 1) * T], 0, 1)
                        m.then_inc(full[f"score{c}"], 1)

                def turn(n, src, ready, value):
                    pe.wait_ge(ready, value)
                    o = take("trans", cn("trans", n))
                    for k in range(TT):
                        for q in range(TT):
                            m = nc.tensor.transpose(o[:, k * T + q * P:k * T + (q + 1) * P],
                                                    src[:, q, k * P:(k + 1) * P], c_("ident"))
                    m.then_inc(full["trans"], 1)

                def weigh(n, v, ready):
                    pe.wait_ge(v_ready, ready)
                    pe.wait_ge(probT_ready, cn("pt", n + 1))
                    o = take("ctx", cn("ctx", n))
                    for k in range(TT):
                        m = mm(o[:, 0:T], v[:, k], probT[:, n % 2, k], k, TT)
                    m.then_inc(full["ctx"], 1)

                need(3, cn("s3", 0))
                g = take("proj1", cn("proj1", 2))
                gate(g, 0)
                diff_scores(0)
                for h in range(2):
                    turn(h, prob[:, h], mla_prob, cn("pn", h + 1))
                gate(g, 1).then_inc(full["proj1"], 1)
                for h in range(2):
                    weigh(h, v_mla[:, :, h * P:(h + 1) * P], cn("v", 1))
                diff_scores(1)
                g = take("proj0", cn("proj0", 3))
                gate(g, 2)
                turn(2, dprob[:, 0, 0], diff_prob, cn("w", 1))
                gate(g, 3, range(DB // 2))
                turn(3, dprob[:, 1, 0], diff_prob, cn("w", 2))
                gate(g, 3, range(DB // 2, DB)).then_inc(full["proj0"], 1)
                release(slot_free[3])
                for h in range(2):
                    weigh(2 + h, v_diff[:, :, h * P:(h + 1) * P], cn("v", 2))

            def merge(l):
                ph = ("merge", l)
                jobs = [0, 0]

                def product(slot, b0, src, bank):
                    w = slots[slot][:].rearrange("p (k c) -> p k c", k=DB)
                    o = take(f"proj{bank}", count(ph, f"proj{bank}", jobs[bank]))
                    jobs[bank] += 1
                    for b in range(2):
                        for k in range(DB):
                            m = mm(o[:, b * T:(b + 1) * T], blk(w[:, k], b0 + b), src[:, k], k, DB)
                    m.then_inc(full[f"proj{bank}"], 1)

                pe.wait_ge(free["ctx"], count(("pair", l), "ctx", 4, PAIRS - 1) + 1)
                need(4, count(ph, "s4", 0))
                product(4, 0, oaT, 0)
                product(4, 2, oaT, 1)
                release(slot_free[4])
                pe.wait_ge(sq_ready, count(ph, "sq", 1))
                for g in range(4):
                    o = take("stat", count(ph, "stat", g))
                    mm(o[:], c_("ones"), merged[:, 2 * g:2 * g + 2].rearrange("p a b -> p (a b)"), 0, 1)\
                        .then_inc(full["stat"], 1)
                pe.wait_ge(ob_ready, count(ph, "ob", 4))
                need(5, count(ph, "s5", 0))
                product(5, 0, obT, 0)
                product(5, 2, obT, 1)
                release(slot_free[5])
                for slot, src in ((0, oaT), (1, obT)):
                    need(slot, count(ph, f"s{slot}", 0))
                    product(slot, 0, src, 0)
                    product(slot, 2, src, 1)
                    release(slot_free[slot])
                pe.wait_ge(merged_ready, count(ph, "mg", 4))
                for slot in (2, 3):
                    need(slot, count(ph, f"s{slot}", 0))
                    product(slot, 0, merged, 0)
                    product(slot, 2, merged, 1)
                    release(slot_free[slot])

            def dense(l):
                def gate_up(ph, i, slot, kslot, job):
                    w = slots[slot][:].rearrange("p (m k c) -> p m k c", m=2, k=DB)
                    need(slot, count(ph, f"s{slot}", kslot, i))
                    for m_ in range(2):
                        o = take(f"proj{m_}", count(ph, f"proj{m_}", job, i))
                        for b in range(2):
                            for k in range(DB):
                                if ph[0] == "dense0" and m_ == 0 and b == 0:
                                    pe.wait_ge(h_ready, count(("norm", l, 1), "h", k + 1))
                                m = mm(o[:, b * T:(b + 1) * T], blk(w[:, m_, k], b), hT[:, k], k, DB)
                        m.then_inc(full[f"proj{m_}"], 1)
                    release(slot_free[slot])

                def down(ph, i, slot, kslot, job, hid_n, parity):
                    w = slots[slot][:, 0:2048].rearrange("p (f c) -> p f c", f=2)
                    h = hid[parity][:, 0:2 * T].rearrange("p (f t) -> p f t", f=2)
                    need(slot, kslot)
                    pe.wait_ge(hid_ready, hid_n)
                    for q, bank in enumerate(("score0", "score1", "trans", "ctx")):
                        o = take(bank, count(ph, bank, job, i))
                        for b in range(2):
                            for f in range(2):
                                m = mm(o[:, b * T:(b + 1) * T], blk(w[:, f], 2 * q + b), h[:, f], f, 2)
                        m.then_inc(full[bank], 1)
                    release(slot_free[slot])

                first, loop, last = ("dense0", l), ("dense", l), ("dense1", l)
                gate_up(first, 0, 0, 0, 0)
                settle()
                with pe.Fori(0, DENSE_CHUNKS // 2) as i:
                    gate_up(loop, i, 2, 0, 0)
                    down(loop, i, 1, count(loop, "s1", 0, i), 0, count(loop, "hid", 0, i), 0)
                    gate_up(loop, i, 0, 0, 1)
                    down(loop, i, 3, count(loop, "s3", 0, i), 1, count(loop, "hid", 1, i), 1)
                    settle()
                down(last, 0, 1, count(last, "s1", 0), 0, count(last, "x", 0) * 0 + START[last]["hid"], 0)

            def route(l):
                ph = ("route", l)
                pe.wait_ge(router_in, 16)
                o = take("val", count(ph, "val", 0))
                for t in range(TT):
                    for k in range(DB):
                        if t == 0:
                            pe.wait_ge(h_ready, count(("norm", l, 1), "h", k + 1))
                        m = mm(o[:, t * EXPERTS:(t + 1) * EXPERTS], hT[:, k, t * P:(t + 1) * P],
                               wr[:, k * EXPERTS:(k + 1) * EXPERTS], k, DB)
                m.then_inc(full["val"], 1)
                for src, banks in ((hT, ("trans", "ctx")), (xT, ("score0", "score1"))):
                    for t in range(TT):
                        for half, bank in enumerate(banks):
                            o = take(bank, count(ph, bank, t))
                            for k in range(4):
                                m = nc.tensor.transpose(o[:, k * P:(k + 1) * P],
                                                        src[:, half * 4 + k, t * P:(t + 1) * P], c_("ident"))
                            m.then_inc(full[bank], 1)
                pe.wait_ge(sel_ready, 1)
                o = take("val", count(ph, "val", 1))
                E = EXPERTS
                mm(o[:, 0:E], c_("before"), rt[:, 0, 0], 0, 1)
                mm(o[:, E:2 * E], c_("before"), rt[:, 0, 1], 0, 2)
                mm(o[:, E:2 * E], c_("ones"), rt[:, 0, 0], 1, 2)
                mm(o[:, 2 * E:3 * E], c_("ones"), rt[:, 0, 0], 0, 2)
                mm(o[:, 2 * E:3 * E], c_("ones"), rt[:, 0, 1], 1, 2).then_inc(full["val"], 1)

            def gather(par, half, g_value, value):
                if half == 0:
                    pe.wait_ge(gather_ready, g_value)
                bank = ("ctx", "val")[half]
                o = take(bank, value)
                for b in range(4):
                    for t in range(TT):
                        c = (half * 4 + b) * P
                        m = mm(o[:, b * CAP:(b + 1) * CAP], htok[:, t, c:c + P], G[par][:, t], t, TT)
                m.then_inc(full[bank], 1)

            def scatter_matrix(value):
                o = take("stat", value)
                for t in range(TT):
                    m = nc.tensor.transpose(o[:, t * P:(t + 1) * P], Gw[:, t], c_("ident"))
                    if owed and t == 0:
                        m.then_inc(owed.pop(0), 1)
                m.then_inc(full["stat"], 1)

            def combine(t, par, y_value, st_value, bank_value):
                if t == 0:
                    pe.wait_ge(y_ready, y_value)
                    pe.wait_ge(scatter_ready, st_value + 1)
                for half, bank in enumerate(("ctx", "val")):
                    o = take(bank, bank_value(bank) + t)
                    mm(o[:], S[par][:, t * P:(t + 1) * P], yrow[:, half * 512:(half + 1) * 512], 0, 1)\
                        .then_inc(full[bank], 1)

            def experts(rnd):
                def opening(name, k=0):
                    return moe_count(name, k, rnd, 0, opening=True)

                pe.wait_ge(zero_ready, opening("zero", 1))
                for bank in ("score0", "score1"):
                    o = take(bank, opening(bank))
                    mm(o[:], S[1][:, 0:P], cst[:, 0:2 * T], 0, 1).then_inc(full[bank], 1)
                for half, bank in enumerate(("ctx", "val")):
                    gather(0, half, opening("g", 1), opening(bank))
                scatter_matrix(opening("stat"))
                settle()
                with pe.Fori(0, EXPERTS // 2) as pair_:
                    def cn(name, k, j=0, per_j=0):
                        return moe_count(name, k, rnd, pair_, j, per_j)

                    def gather_next(par):
                        for half, bank in enumerate(("ctx", "val")):
                            gather(par, half, cn("g", 2 - par), cn(bank, 5 - 3 * par))
                        scatter_matrix(cn("stat", 1 - par))

                    def combine_last(t, n):
                        combine(t, 1 - n, cn("y", n + 1), cn("st", n), lambda bank: cn(bank, 3 * n))

                    def exact(o, a_hi, a_lo, w_h, w_l, first, last):
                        m = nc.tensor.matmul(o, a_hi, w_h, start=first, stop=False)
                        if owed:
                            m.then_inc(owed.pop(0), 1)
                        nc.tensor.matmul(o, a_hi, w_l, start=False, stop=False)
                        return nc.tensor.matmul(o, a_lo, w_h, start=False, stop=last)

                    def step(t, j=0):
                        par = 0 if t < EXP_CHUNKS else 1

                        def granule(n):
                            n = n + granules_before(t)
                            pe.wait_ge(split_ready, cn("split", n + 1, j, 12))
                            return w_hi[n % RING][:], w_lo[n % RING][:]

                        def gate_up(m_, n0):
                            o = take(f"proj{m_}", cn(f"proj{m_}", t, j, 2))
                            if t in (0, EXP_CHUNKS) and m_ == 0:
                                pe.wait_ge(he_ready, cn("he", par))
                            for half in range(2):
                                h, lo_ = granule(n0 + half)
                                for k in range(4):
                                    kk = half * 4 + k
                                    m = exact(o[:], he_hi[:, kk], he_lo[:, kk], blk(h, k, 512),
                                              blk(lo_, k, 512), kk == 0, kk == DB - 1)
                                if half == 0:
                                    m.then_inc(split_free, 1)
                            m.then_inc(full[f"proj{m_}"], 1)
                            release(split_free)

                        def turn():
                            pe.wait_ge(hid_ready, cn("hid", t, j, 2))
                            o = take("trans", cn("trans", t - 1, j, 2))
                            for f in range(4):
                                m = nc.tensor.transpose(o[:, f * CAP:(f + 1) * CAP], hid_e[:, f * P:(f + 1) * P],
                                                        c_("ident"))
                                if owed and f < 3:
                                    m.then_inc(owed.pop(0), 1)
                            m.then_inc(full["trans"], 1)

                        def down(n0):
                            own, c = divmod(t - 1, EXP_CHUNKS)
                            looped = not isinstance(j, int)
                            if c == 0 and not looped:
                                for b in range(2):
                                    take(f"score{b}", cn(f"score{b}", own))
                            pe.wait_ge(hidT_ready, cn("ht", t, j, 2))
                            for half in range(2):
                                h, lo_ = granule(n0 + half)
                                for k in range(2):
                                    f = half * 2 + k
                                    for b in range(2):
                                        m = exact(ps[f"score{b}"][:], hidT_hi[:, f], hidT_lo[:, f],
                                                  h[:, k * D + b * 512:k * D + (b + 1) * 512],
                                                  lo_[:, k * D + b * 512:k * D + (b + 1) * 512],
                                                  c == 0 and f == 0 and not looped, c == EXP_CHUNKS - 1 and f == 3)
                                        if c == EXP_CHUNKS - 1 and f == 3:
                                            m.then_inc(full[f"score{b}"], 1)
                                if half == 0 or c < EXP_CHUNKS - 1:
                                    m.then_inc(split_free, 1)
                                else:
                                    release(split_free)

                        if t == 0:
                            gate_up(0, 0)
                            combine_last(0, 0)
                            combine_last(1, 0)
                            gate_up(1, 2)
                        elif t % EXP_CHUNKS == 0:
                            turn()
                            gather_next(1 if t == EXP_CHUNKS else 0)
                            down(0)
                            if t == EXP_CHUNKS:
                                gate_up(0, 2)
                                gate_up(1, 4)
                        else:
                            after_first = t == EXP_CHUNKS + 1 and isinstance(j, int)
                            gate_up(0, 0)
                            if after_first:
                                combine_last(0, 1)
                            turn()
                            if after_first:
                                combine_last(1, 1)
                            gate_up(1, 2)
                            down(4)

                    step(0)
                    for t0 in (1, EXP_CHUNKS + 1):
                        step(t0)
                        step(t0 + 1)
                        settle()
                        with pe.Fori(1, EXP_CHUNKS // 2) as j:
                            step(t0, j)
                            step(t0 + 1, j)
                            settle()
                        step(t0 + EXP_CHUNKS - 1)
                    settle()
                end = EXPERTS // 2
                for t in range(TT):
                    combine(t, 1, moe_count("y", 1, rnd, end), moe_count("st", 0, rnd, end),
                            lambda bank: moe_count(bank, 0, rnd, end))

            pe.wait_ge(const_in, 80)
            for l in range(DEPTH):
                norm(l, 0)
                latent(l)
                settle()
                with pe.Fori(0, PAIRS) as i:
                    pair(l, i)
                    settle()
                merge(l)
                norm(l, 1)
                if l % 2 == 0:
                    dense(l)
                else:
                    route(l)
            settle()
            experts(0)
            pe.wait_ge(rounds_ready, 1)
            n = pe.value_load(nrnd[0:1, 0:1], min_val=1, max_val=MAX_ROUNDS)
            with pe.If(n > 1):
                with pe.Fori(1, n) as rnd:
                    experts(rnd)

        @block.scalar
        def _(act):
            def fresh(bank, n):
                act.wait_ge(full[bank], n + 1)
                return ps[bank]

            A = nc.scalar.activation

            def rsqrt(bank_n, at, width, mean):
                o = fresh("stat", bank_n)
                h, c = at
                out_, ms = rsp[:, h, c:c + width], msp[:, h, c:c + width]
                A(ms, o[:, 0:width], ACT.Identity, bias=eps[:, 0:1], scale=mean)
                A(out_, o[:, 0:width], ACT.Ln, bias=eps[:, 0:1], scale=mean)
                act.drain().then_inc(free["stat"], 1)
                A(out_, out_, ACT.Exp, scale=-0.5).then_inc(rs_ready, 1)

            def norm(l, which, x_value):
                ph = ("norm", l, which)
                if x_value:
                    act.wait_ge(x_ready, x_value)
                for half in range(2):
                    A(merged[:, half * 4:half * 4 + 4], xT[:, half * 4:half * 4 + 4], ACT.Square)\
                        .then_inc(sq_ready, 1)
                rsqrt(count(ph, "stat", 0), (0, 0), T, 1.0 / D)

            def latent(l):
                ph = ("latent", l)
                for g, (bank, job, b0, nb) in enumerate((("proj0", 0, 0, 2), ("proj1", 0, 2, 2),
                                                         ("proj0", 1, 4, 2), ("proj1", 1, 6, 1))):
                    o = fresh(bank, count(ph, bank, job))[:, 0:nb * T].rearrange("p (b t) -> p b t", t=T)
                    A(gates[:, 8 + b0:8 + b0 + nb], o, ACT.Copy)
                    A(gates[:, b0:b0 + nb], o, ACT.Square).then_inc(sq_ready, 1)
                    act.drain().then_inc(free[bank], 1)
                for s, n in enumerate((4 * P, 2 * P, ROPE)):
                    if s == 0:
                        act.wait_ge(h_ready, count(("norm", l, 0), "h", DB))
                    rsqrt(count(ph, "stat", s), (s // 2, (s % 2) * T), T, 1.0 / n)

            def pair(l, i):
                ph = ("pair", l)

                def cn(name, k):
                    return count(ph, name, k, i)

                def take(g, bank, job):
                    o = fresh(bank, cn(bank, job))
                    w = T if g == 2 else 2 * T
                    A(qk[:, g, 0:w], o[:, 0:w], ACT.Copy)
                    if g >= 2:
                        act.wait_ge(full["stat"], cn("stat", g - 1))
                    A(sqp[:, g % 2, 0:w], o[:, 0:w], ACT.Square).then_inc(sq_ready, 1)
                    act.drain().then_inc(free[bank], 1)

                def factors(g):
                    w = T if g == 2 else 2 * T
                    if g >= 2:
                        act.wait_ge(qk_ready, cn("qk", (1, 2, 3)[g - 2]))
                    rsqrt(cn("stat", g), (g % 2, 0), w, 1.0 / (P if g < 2 else ROPE))

                take(0, "proj0", 0)
                take(1, "proj1", 0)
                factors(0)
                take(2, "proj0", 1)
                factors(1)
                factors(2)
                take(3, "proj1", 1)
                factors(3)
                take(4, "proj0", 2)
                factors(4)

                for h in range(2):
                    act.wait_ge(mla_max, cn("mx", h + 1))
                    o = fresh(f"score{h}", cn(f"score{h}", 0))
                    for q in range(TT):
                        m = A(prob[:, h, q], o[:, q * T:(q + 1) * T], ACT.Exp, bias=nmx[:, 2 * h + q:2 * h + q + 1],
                              scale=MLA_SCALE, accum_out=sums[:, 2 * h + q:2 * h + q + 1])
                    m.then_inc(mla_exp, 1)
                    act.drain().then_inc(free[f"score{h}"], 1)

                def turned(n):
                    o = fresh("trans", cn("trans", n))
                    if n >= 2:
                        act.wait_ge(full["ctx"], cn("ctx", n - 1))
                    A(probT[:, n % 2].rearrange("p a b -> p (a b)"), o[:], ACT.Copy).then_inc(probT_ready, 1)
                    act.drain().then_inc(free["trans"], 1)

                def diff_exps(h):
                    act.wait_ge(diff_max, cn("dmx", h + 1))
                    for c in range(2):
                        for q in range(TT):
                            n = 4 + 4 * h + 2 * c + q
                            m = A(dprob[:, h, c, q], dprob[:, h, c, q], ACT.Exp, bias=nmx[:, n:n + 1],
                                  scale=DIFF_SCALE, accum_out=sums[:, n:n + 1])
                    m.then_inc(diff_exp, 1)

                turned(0)
                turned(1)
                diff_exps(0)
                diff_exps(1)
                turned(2)
                turned(3)

            def merge(l):
                ph = ("merge", l)
                act.wait_ge(free["ctx"], count(("pair", l), "ctx", 4, PAIRS - 1) + 1)
                A(merged[:], obT[:], ACT.Square).then_inc(sq_ready, 1)
                for g in range(4):
                    if g >= 2:
                        act.wait_ge(ob_ready, count(ph, "ob", g - 1))
                    rsqrt(count(ph, "stat", g), (g % 2, 0), 2 * T, 1.0 / P)
                A(gates[:], gates[:], ACT.Sigmoid).then_inc(gate_ready, 1)

            def dense(l):
                def chunk(ph, job, i=0):
                    o = fresh("proj0", count(ph, "proj0", job, i))
                    act.wait_ge(hid_ready, count(ph, "hid", job, i))
                    A(silu[:, 0:2 * T], o[:], ACT.Silu).then_inc(silu_ready, 1)
                    act.drain().then_inc(free["proj0"], 1)

                act.preload_act_table(ACT.Silu)
                chunk(("dense0", l), 0)
                with act.Fori(0, DENSE_CHUNKS // 2) as i:
                    chunk(("dense", l), 0, i)
                    chunk(("dense", l), 1, i)

            def route(l):
                ph = ("route", l)
                for name, banks, dst, ready in (("h", ("trans", "ctx"), htok, htok_ready),
                                                ("x", ("score0", "score1"), acc, xtok_ready)):
                    for t in range(TT):
                        for half, bank in enumerate(banks):
                            o = fresh(bank, count(ph, bank, t))
                            A(dst[:, t, half * 512:(half + 1) * 512], o[:], ACT.Copy).then_inc(ready, 1)
                            act.drain().then_inc(free[bank], 1)
                act.wait_ge(route_exp_in, 1)
                A(sc1[:, 4], sc1[:, 3], ACT.Exp).then_inc(route_exp_out, 1)

            def gathered_half(half, value):
                o = fresh(("ctx", "val")[half], value)
                A(he_hi[:, half * 4:half * 4 + 4].rearrange("p a b -> p (a b)"), o[:], ACT.Copy).then_inc(he_hi_ready, 1)

            def scatter_matrix(par, stat_value, comb_value):
                o = fresh("stat", stat_value)
                act.wait_ge(comb_done, comb_value + 1)
                A(S[par][:], o[:, 0:T], ACT.Copy).then_inc(scatter_ready, 1)
                act.drain().then_inc(free["stat"], 1)

            def outputs(comb_value, score_value):
                act.wait_ge(comb_done, comb_value + 1)
                for b in range(2):
                    o = fresh(f"score{b}", score_value(f"score{b}"))
                    m = A(yrow[:, b * 512:(b + 1) * 512], o[:], ACT.Copy)
                    if b:
                        m.then_inc(y_ready, 1)
                    act.drain().then_inc(free[f"score{b}"], 1)

            def experts(rnd):
                def opening(name, k=0):
                    return moe_count(name, k, rnd, 0, opening=True)

                for half, bank in enumerate(("ctx", "val")):
                    gathered_half(half, opening(bank))
                scatter_matrix(0, opening("stat"), opening("comb"))
                with act.Fori(0, EXPERTS // 2) as pair_:
                    def cn(name, k, j=0, per_j=0):
                        return moe_count(name, k, rnd, pair_, j, per_j)

                    def gathered(par):
                        for half, bank in enumerate(("ctx", "val")):
                            gathered_half(half, cn(bank, 5 - 3 * par))
                        scatter_matrix(par, cn("stat", 1 - par), cn("comb", 2 - par))

                    def outputs_last(n):
                        outputs(cn("comb", n), lambda bank: cn(bank, n - 1))

                    def step(t, j=0):
                        items = step_items(t)

                        def high(n):
                            kind, chunk, slot, used = items[n // 2]
                            if n % 2 == 0:
                                act.wait_ge(slot_full[slot], slot_count(slot, used, rnd, pair_, j) * 16 + 16)
                            g = granules_before(t) + n
                            act.wait_ge(split_free, cn("used", g + 1, j, 12))
                            A(w_hi[g % RING][:], slots[slot][:, n % 2 * GRAN:(n % 2 + 1) * GRAN], ACT.Copy)\
                                .then_inc(hi_ready, 1)

                        def turned():
                            o = fresh("trans", cn("trans", t - 1, j, 2))
                            A(hidT_hi[:].rearrange("p a b -> p (a b)"), o[:], ACT.Copy).then_inc(hidT_hi_ready, 1)

                        def silu_of_gate():
                            o = fresh("proj0", cn("proj0", t, j, 2))
                            act.wait_ge(hid_ready, cn("hid", t, j, 2))
                            A(silu_e[:], o[:], ACT.Silu).then_inc(silu_ready, 1)
                            act.drain().then_inc(free["proj0"], 1)

                        if t == 0:
                            high(0)
                            high(1)
                            outputs_last(0)
                            high(2)
                            high(3)
                            silu_of_gate()
                        elif t == EXP_CHUNKS:
                            high(0)
                            high(1)
                            high(2)
                            high(3)
                            turned()
                            gathered(1)
                            high(4)
                            high(5)
                            outputs_last(1)
                            silu_of_gate()
                        elif t == 2 * EXP_CHUNKS:
                            high(0)
                            high(1)
                            turned()
                            gathered(0)
                        else:
                            high(0)
                            high(1)
                            high(2)
                            high(3)
                            turned()
                            silu_of_gate()
                            high(4)
                            high(5)

                    step(0)
                    for t0 in (1, EXP_CHUNKS + 1):
                        with act.Fori(0, EXP_CHUNKS // 2) as j:
                            step(t0, j)
                            step(t0 + 1, j)
                        step(t0 + EXP_CHUNKS - 1)
                end = EXPERTS // 2
                outputs(moe_count("comb", 0, rnd, end), lambda bank: moe_count(bank, -1, rnd, end))

            exp_ln = "natural_log_exp_and_others"
            act.wait_ge(angle_ready, 1)
            A(sinT[:], tmp[:, 0], ACT.Sin)
            A(cosT[:], tmp[:, 1], ACT.Sin).then_inc(sin_ready, 1)
            act.preload_act_table_set(exp_ln)
            act.wait_ge(lam_dot, 1)
            for l in range(DEPTH):
                m = A(lams[:, l, 2:4], lams[:, l, 0:2], ACT.Exp)
            m.then_inc(lam_exp, 1)
            act.wait_ge(x_in, 16)
            act.wait_ge(eps_set, 1)
            for l in range(DEPTH):
                norm(l, 0, START[("norm", l, 0)].get("x", 0))
                latent(l)
                act.wait_ge(lat_ready, count(("latent", l), "lat", 3))
                with act.Fori(0, PAIRS) as i:
                    pair(l, i)
                merge(l)
                act.preload_act_table_set(exp_ln)
                norm(l, 1, count(("merge", l), "x", 4))
                if l % 2 == 0:
                    dense(l)
                    act.preload_act_table_set(exp_ln)
                else:
                    route(l)
            act.preload_act_table(ACT.Silu)
            experts(0)
            act.wait_ge(rounds_ready, 1)
            n = act.value_load(nrnd[0:1, 0:1], min_val=1, max_val=MAX_ROUNDS)
            with act.If(n > 1):
                with act.Fori(1, n) as rnd:
                    experts(rnd)

        @block.vector
        def _(dve):
            V = nc.vector

            def fresh(bank, n):
                dve.wait_ge(full[bank], n + 1)
                return ps[bank]

            def then(*ops):
                for op in ops:
                    op()
                    dve.drain()

            def setup():
                V.memset(eps[:], EPS).then_inc(eps_set, 1)
                for n, s in enumerate(slot_free + list(free.values()) + [comb_done, scatter_ready] + [split_free] * RING):
                    V.memset(marks[:, n:n + 1], 0.0).then_inc(s, 1)
                dve.wait_ge(const_in, 80)
                V.tensor_copy(tmp[:, 0], posr[:])
                V.tensor_copy(poscf[:], posc[:])
                dve.drain()
                for q in range(TT):
                    V.tensor_scalar(dist[:, q], tmp[:, 0], poscf[:, q:q + 1], None, ALU.subtract)
                dve.drain()
                V.tensor_scalar(probT[:, 0], dist[:], -1.0, None, ALU.mult)
                dve.drain()
                V.tensor_tensor(dist[:], dist[:], probT[:, 0], ALU.max)
                ang, turns = tmp[:, 0], tmp[:, 1]
                then(lambda: V.tensor_scalar(ang, tmp[:, 0], c_("inv_freq"), None, ALU.mult),
                     lambda: V.tensor_scalar(turns, ang, float(0.5 / np.pi), None, ALU.mult),
                     lambda: V.tensor_scalar(turns, turns, ROUND, -ROUND, ALU.add, ALU.add),
                     lambda: V.scalar_tensor_tensor(ang, turns, -TWO_PI_HI, ang, ALU.mult, ALU.add),
                     lambda: V.scalar_tensor_tensor(ang, turns, -TWO_PI_MID, ang, ALU.mult, ALU.add),
                     lambda: V.scalar_tensor_tensor(ang, turns, -TWO_PI_LO, ang, ALU.mult, ALU.add),
                     lambda: V.tensor_scalar(turns, ang, float(np.pi / 2), float(np.pi), ALU.add, ALU.is_gt),
                     lambda: V.tensor_scalar(turns, turns, float(-2 * np.pi), float(np.pi / 2), ALU.mult, ALU.add),
                     lambda: V.tensor_tensor(turns, turns, ang, ALU.add),
                     lambda: V.tensor_scalar(ang, ang, PI_IN, -PI_IN, ALU.min, ALU.max))
                V.tensor_scalar(turns, turns, PI_IN, -PI_IN, ALU.min, ALU.max).then_inc(angle_ready, 1)
                for l in range(DEPTH):
                    V.tensor_tensor(lamv[:, l, 0:4:2], lamv[:, l, 0:4:2], lamv[:, l, 1:4:2], ALU.mult)
                    V.tensor_scalar(g_(l, "sub"), g_(l, "sub"), 1.0 - LAMBDA_INIT[l], None, ALU.mult)
                dve.drain()
                for l in range(DEPTH):
                    m = V.tensor_reduce(lams[:, l, 0:2], lamv[:, l, 0:4:2], AX.X, ALU.add)
                m.then_inc(lam_dot, 1)
                dve.wait_ge(lam_exp, 1)
                for l in range(DEPTH):
                    V.tensor_tensor(lams[:, l, 4:5], lams[:, l, 3:4], lams[:, l, 2:3], ALU.subtract)
                dve.drain()
                for l in range(DEPTH):
                    V.tensor_scalar(lams[:, l, 5:6], lams[:, l, 4:5], -LAMBDA_INIT[l], None, ALU.add)
                dve.wait_ge(sin_ready, 1)
                dve.wait_ge(x_in, 16)
                dve.drain()

            def root(value, at, width):
                dve.wait_ge(rs_ready, value)
                h, c = at
                y, m_ = rsp[:, h, c:c + width], msp[:, h, c:c + width]
                V.scalar_tensor_tensor(m_, m_, -0.5, y, ALU.mult, ALU.mult)
                dve.drain()
                V.tensor_tensor(m_, m_, y, ALU.mult)
                dve.drain()
                V.scalar_tensor_tensor(y, m_, 1.5, y, ALU.add, ALU.mult)
                dve.drain()
                return y

            def norm(l, which):
                ph = ("norm", l, which)
                y = root(count(ph, "rs", 1), (0, 0), T)
                for b in range(DB):
                    V.scalar_tensor_tensor(hT[:, b], xT[:, b], g_(l, "attn" if which == 0 else "ffn", b),
                                           y, ALU.mult, ALU.mult).then_inc(h_ready, 1)

            def latent(l):
                ph = ("latent", l)
                for s, (name, blocks) in enumerate((("q_lat", range(0, 4)), ("kv_lat", range(4, 6)), ("kr", range(6, 7)))):
                    r = root(count(ph, "rs", s + 1), (s // 2, (s % 2) * T), T)
                    for j, b in enumerate(blocks):
                        dst = latN[:, b] if s < 2 else gates[:, 14]
                        m = V.scalar_tensor_tensor(dst, gates[:, 8 + b], g_(l, name, j), r, ALU.mult, ALU.mult)
                    m.then_inc(lat_ready, 1)
                dve.drain()
                o = fresh("val", count(ph, "val", 0))
                V.tensor_tensor(tmp[:, 0], o[:, 0:T], sinT[:], ALU.mult).then_inc(free["val"], 1)
                V.tensor_tensor(tmp[:, 1], gates[:, 14], cosT[:], ALU.mult)
                dve.drain()
                V.tensor_tensor(krT[:], tmp[:, 0], tmp[:, 1], ALU.add).then_inc(kr_ready, 1)

            def pair(l, i):
                ph = ("pair", l)

                def cn(name, k):
                    return count(ph, name, k, i)

                def scale(g, name):
                    w = T if g == 2 else 2 * T
                    y = root(cn("rs", g + 1), (g % 2, 0), w)
                    V.scalar_tensor_tensor(qk[:, g, 0:w], qk[:, g, 0:w], g_(l, name), y,
                                           ALU.mult, ALU.mult).then_inc(qk_ready, 1)

                def values(dst, job):
                    o = fresh("val", cn("val", job))
                    V.tensor_copy(dst.rearrange("p a b -> p (a b)"), o[:]).then_inc(v_ready, 1)
                    dve.drain().then_inc(free["val"], 1)

                values(v_mla, 0)
                scale(0, "qn")
                scale(1, "kn")
                scale(2, "qr")
                dve.drain()
                o = fresh("val", cn("val", 1))
                V.tensor_tensor(tmp[:, 0], o[:, 0:T], sinT[:], ALU.mult).then_inc(free["val"], 1)
                V.tensor_tensor(tmp[:, 1], qk[:, 2, 0:T], cosT[:], ALU.mult)
                dve.drain()
                V.tensor_tensor(qk[:, 2, T:2 * T], tmp[:, 0], tmp[:, 1], ALU.add).then_inc(qk_ready, 1)
                scale(3, "dq")
                scale(4, "dk")
                values(v_diff, 2)

                for h in range(2):
                    o = fresh(f"score{h}", cn(f"score{h}", 0))
                    V.tensor_reduce(mx[:, 2 * h:2 * h + 2], o[:].rearrange("p (q t) -> p q t", t=T), AX.X, ALU.max)
                    dve.drain()
                    V.tensor_scalar(nmx[:, 2 * h:2 * h + 2], mx[:, 2 * h:2 * h + 2], -MLA_SCALE, None, ALU.mult)\
                        .then_inc(mla_max, 1)

                def diff_logits(h):
                    for c in range(2):
                        o = fresh(f"score{c}", cn(f"score{c}", 1 + h))
                        V.scalar_tensor_tensor(dprob[:, h, c].rearrange("p a b -> p (a b)"),
                                               dist[:].rearrange("p a b -> p (a b)"),
                                               cst[:, bass.ds(i * 2 + (CONST["slope"][0] + h), 1)], o[:],
                                               ALU.mult, ALU.add).then_inc(free[f"score{c}"], 1)
                    dve.drain()
                    n = 4 + 4 * h
                    V.tensor_reduce(mx[:, n:n + 4], dprob[:, h].rearrange("p c q t -> p (c q) t"), AX.X, ALU.max)
                    dve.drain()
                    V.tensor_scalar(nmx[:, n:n + 4], mx[:, n:n + 4], -DIFF_SCALE, None, ALU.mult).then_inc(diff_max, 1)

                def gate(bank, job, b0):
                    o = fresh(bank, cn(bank, job))
                    V.tensor_scalar(gates[:, bass.ds(i * 4 + b0, 2)], o[:].rearrange("p (b t) -> p b t", t=T),
                                    1.0, None, ALU.mult).then_inc(free[bank], 1)

                def context(n, dst, h):
                    o = fresh("ctx", cn("ctx", n))
                    V.tensor_scalar(dst[:, bass.ds(i * 2 + h, 1)].rearrange("p a b -> p (a b)"), o[:, 0:T], 1.0, None,
                                    ALU.mult)\
                        .then_inc(free["ctx"], 1)

                def diff_weights(h):
                    dve.wait_ge(diff_exp, cn("pd", h + 1))
                    n = 4 + 4 * h
                    V.reciprocal(rcp[:, n:n + 4], sums[:, n:n + 4])
                    dve.drain()
                    V.tensor_scalar(rcp[:, n + 2:n + 4], rcp[:, n + 2:n + 4], lams[:, l, 5:6], None, ALU.mult)
                    for q in range(TT):
                        V.tensor_scalar(dprob[:, h, 0, q], dprob[:, h, 0, q], rcp[:, n + q:n + q + 1], None, ALU.mult)
                    dve.drain()
                    for q in range(TT):
                        m = V.scalar_tensor_tensor(dprob[:, h, 0, q], dprob[:, h, 1, q], rcp[:, n + 2 + q:n + 3 + q],
                                                   dprob[:, h, 0, q], ALU.mult, ALU.add)
                    m.then_inc(diff_prob, 1)

                for h in range(2):
                    dve.wait_ge(mla_exp, cn("p", h + 1))
                    V.reciprocal(rcp[:, 2 * h:2 * h + 2], sums[:, 2 * h:2 * h + 2])
                    dve.drain()
                    for q in range(TT):
                        m = V.tensor_scalar(prob[:, h, q], prob[:, h, q], rcp[:, 2 * h + q:2 * h + q + 1], None, ALU.mult)
                    m.then_inc(mla_prob, 1)
                diff_logits(0)
                gate("proj1", 2, 0)
                diff_weights(0)
                for h in range(2):
                    context(h, oaT, h)
                diff_logits(1)
                diff_weights(1)
                gate("proj0", 3, 2)
                for h in range(2):
                    context(2 + h, obT, h)
                dve.drain()

            def merge(l):
                ph = ("merge", l)
                jobs = [0, 0]

                def job(bank):
                    o = fresh(f"proj{bank}", count(ph, f"proj{bank}", jobs[bank]))
                    jobs[bank] += 1
                    return o

                def two(ap, b):
                    return ap[:, b:b + 2].rearrange("p a b -> p (a b)")

                for g in range(4):
                    y = root(count(ph, "rs", g + 1), (g % 2, 0), 2 * T)
                    V.scalar_tensor_tensor(two(obT, 2 * g), two(obT, 2 * g), g_(l, "sub"), y,
                                           ALU.mult, ALU.mult).then_inc(ob_ready, 1)
                dve.wait_ge(gate_ready, count(ph, "sig", 1))
                for half in range(2):
                    for bank in range(2):
                        b = 4 * half + 2 * bank
                        V.tensor_tensor(two(merged, b), job(bank)[:], two(gates, b), ALU.mult)\
                            .then_inc(free[f"proj{bank}"], 1)
                    for bank in range(2):
                        b = 4 * half + 2 * bank
                        V.tensor_tensor(tmp[:].rearrange("p a b -> p (a b)"), job(bank)[:], two(gates, DB + b), ALU.mult)\
                            .then_inc(free[f"proj{bank}"], 1)
                        dve.drain()
                        V.tensor_tensor(two(merged, b), two(merged, b), tmp[:].rearrange("p a b -> p (a b)"), ALU.add)\
                            .then_inc(merged_ready, 1)
                        dve.drain()
                for half in range(2):
                    for bank in range(2):
                        b = 4 * half + 2 * bank
                        V.tensor_tensor(two(xT, b), two(xT, b), job(bank)[:], ALU.add).then_inc(x_ready, 1)
                        dve.drain().then_inc(free[f"proj{bank}"], 1)

            def dense(l):
                def hidden(ph, job, i, parity):
                    o = fresh("proj1", count(ph, "proj1", job, i))
                    dve.wait_ge(silu_ready, count(ph, "silu", job + 1, i))
                    V.tensor_tensor(hid[parity][:, 0:2 * T], o[:], silu[:, 0:2 * T], ALU.mult).then_inc(hid_ready, 1)
                    dve.drain().then_inc(free["proj1"], 1)

                def add(ph, job, i):
                    for q, bank in enumerate(("score0", "score1", "trans", "ctx")):
                        o = fresh(bank, count(ph, bank, job, i))
                        x2 = xT[:, 2 * q:2 * q + 2].rearrange("p a b -> p (a b)")
                        V.tensor_tensor(x2, x2, o[:], ALU.add).then_inc(x_ready, 1)
                        dve.drain().then_inc(free[bank], 1)

                first, loop, last = ("dense0", l), ("dense", l), ("dense1", l)
                hidden(first, 0, 0, 0)
                with dve.Fori(0, DENSE_CHUNKS // 2) as i:
                    hidden(loop, 0, i, 1)
                    add(loop, 0, i)
                    hidden(loop, 1, i, 0)
                    add(loop, 1, i)
                add(last, 0, 0)

            def route(l):
                ph = ("route", l)
                lg, oh1, l2, oh2, sc = (rt[:, n] for n in range(1, 6))
                sel, w8, place8 = rt[:, 0], wt[:, :, 0:EXPERTS], place[:, :, 0:EXPERTS]
                V.memset(place[:, :, EXPERTS:], 1.0e6)
                V.memset(wt[:, :, EXPERTS:], 0.0)
                o = fresh("val", count(ph, "val", 0))
                V.tensor_copy(lg.rearrange("p a b -> p (a b)"), o[:, 0:TT * EXPERTS]).then_inc(free["val"], 1)
                dve.drain()

                def best(src, m_, f_, onehot):
                    V.tensor_reduce(sc1[:, m_], src, AX.X, ALU.max)
                    dve.drain()
                    for t in range(TT):
                        V.scalar_tensor_tensor(sc[:, t], src[:, t], sc1[:, m_, t:t + 1], c_("first_wins"),
                                               ALU.is_equal, ALU.mult)
                    dve.drain()
                    V.tensor_reduce(sc1[:, f_], sc, AX.X, ALU.max)
                    dve.drain()
                    for t in range(TT):
                        V.tensor_scalar(onehot[:, t], c_("first_wins"), sc1[:, f_, t:t + 1], None, ALU.is_equal)
                    dve.drain()

                best(lg, 0, 1, oh1)
                V.scalar_tensor_tensor(l2, oh1, -3.0e38, lg, ALU.mult, ALU.add)
                dve.drain()
                best(l2, 2, 1, oh2)
                V.tensor_tensor(sel, oh1, oh2, ALU.add).then_inc(sel_ready, 1)
                V.tensor_tensor(sc1[:, 3], sc1[:, 2], sc1[:, 0], ALU.subtract).then_inc(route_exp_in, 1)
                dve.wait_ge(route_exp_out, 1)
                V.tensor_scalar(sc1[:, 5], sc1[:, 4], 1.0, None, ALU.add)
                dve.drain()
                V.reciprocal(sc1[:, 6], sc1[:, 5])
                dve.drain()
                V.tensor_tensor(sc1[:, 7], sc1[:, 6], sc1[:, 4], ALU.mult)
                dve.drain()
                for t in range(TT):
                    V.tensor_scalar(w8[:, t], oh1[:, t], sc1[:, 6, t:t + 1], None, ALU.mult)
                dve.drain()
                for t in range(TT):
                    V.scalar_tensor_tensor(w8[:, t], oh2[:, t], sc1[:, 7, t:t + 1], w8[:, t], ALU.mult, ALU.add)
                o = fresh("val", count(ph, "val", 1))
                E = EXPERTS
                V.tensor_copy(place8, o[:, 0:2 * E].rearrange("p (a b) -> p a b", a=TT))
                V.tensor_reduce(cnt[:, E:E + 1], o[:, 2 * E:3 * E], AX.X, ALU.max)
                dve.drain().then_inc(free["val"], 1)
                V.tensor_scalar(sc, sel, -1.0e6, 1.0e6, ALU.mult, ALU.add)
                for r in range(MAX_ROUNDS):
                    V.tensor_scalar(cnt[:, r:r + 1], cnt[:, E:E + 1], float(CAP * r), None, ALU.is_gt)
                dve.drain()
                V.tensor_tensor(place8, place8, sc, ALU.add)
                V.tensor_reduce(cnt[:, E + 1:E + 2], cnt[:, 0:MAX_ROUNDS], AX.X, ALU.add)
                dve.drain()
                V.tensor_copy(nrnd[:], cnt[:, E + 1:E + 2]).then_inc(rounds_ready, 1)
                dve.drain()
                dve.wait_ge(xtok_ready, 4)
                dve.wait_ge(htok_ready, 4)

            def one_hot(par, e, turned_before):
                dve.wait_ge(scatter_ready, turned_before + 1)
                for t in range(TT):
                    V.tensor_scalar(G[par][:, t], c_("slot_no"), place[:, t, bass.ds(e, 1)], None, ALU.is_equal)
                    m = V.tensor_scalar(Gw[:, t], c_("slot_no"), place[:, t, bass.ds(e, 1)],
                                        wt[:, t, bass.ds(e, 1)], ALU.is_equal, ALU.mult)
                m.then_inc(gather_ready, 1)

            def gathered_half(half, value):
                dve.wait_ge(he_hi_ready, value)
                h = he_hi[:, half * 4:half * 4 + 4].rearrange("p a b -> p (a b)")
                bank = ("ctx", "val")[half]
                m = V.tensor_tensor(he_lo[:, half * 4:half * 4 + 4].rearrange("p a b -> p (a b)"),
                                    ps[bank][:], h.bitcast(F32), ALU.subtract)
                if half:
                    m.then_inc(he_ready, 1)
                dve.drain().then_inc(free[bank], 1)

            def combined(t, bank_value):
                for half, bank in enumerate(("ctx", "val")):
                    o = fresh(bank, bank_value(bank) + t)
                    a = acc[:, t, half * 512:(half + 1) * 512]
                    m = V.tensor_tensor(a, a, o[:], ALU.add)
                    if t and half:
                        m.then_inc(comb_done, 1)
                    dve.drain().then_inc(free[bank], 1)

            def experts(rnd):
                def opening(name, k=0):
                    return moe_count(name, k, rnd, 0, opening=True)

                V.memset(S[1][:], 0.0).then_inc(zero_ready, 1)
                one_hot(0, 0, opening("st"))
                for half in range(2):
                    gathered_half(half, opening("hehi", half + 1))
                with dve.Fori(0, EXPERTS // 2) as pair_:
                    def cn(name, k, j=0, per_j=0):
                        return moe_count(name, k, rnd, pair_, j, per_j)

                    def gathered(par):
                        for half in range(2):
                            gathered_half(half, cn("hehi", 2 * (1 - par) + half + 1))

                    def combined_last(t, n):
                        combined(t, lambda bank: cn(bank, 3 * n))

                    def step(t, j=0):
                        items = step_items(t)

                        def low(n):
                            kind, chunk, slot, used = items[n // 2]
                            g = granules_before(t) + n
                            dve.wait_ge(hi_ready, cn("hi", g + 1, j, 12))
                            V.tensor_tensor(w_lo[g % RING][:], slots[slot][:, n % 2 * GRAN:(n % 2 + 1) * GRAN],
                                            w_hi[g % RING][:].bitcast(F32), ALU.subtract).then_inc(split_ready, 1)
                            if n % 2:
                                dve.drain().then_inc(slot_free[slot], 1)

                        def turned():
                            dve.wait_ge(hidT_hi_ready, cn("hthi", t, j, 2))
                            V.tensor_tensor(hidT_lo[:].rearrange("p a b -> p (a b)"), ps["trans"][:],
                                            hidT_hi[:].rearrange("p a b -> p (a b)").bitcast(F32), ALU.subtract)\
                                .then_inc(hidT_ready, 1)
                            dve.drain().then_inc(free["trans"], 1)

                        def hidden(c=t):
                            o = fresh("proj1", cn("proj1", c, j, 2))
                            dve.wait_ge(silu_ready, cn("silu", c + 1, j, 2))
                            V.tensor_tensor(hid_e[:], o[:], silu_e[:], ALU.mult).then_inc(hid_ready, 1)
                            dve.drain().then_inc(free["proj1"], 1)

                        if t == 0:
                            low(0)
                            low(1)
                            low(2)
                            low(3)
                            combined_last(0, 0)
                            combined_last(1, 0)
                        elif t == EXP_CHUNKS:
                            low(0)
                            low(1)
                            low(2)
                            low(3)
                            turned()
                            gathered(1)
                            low(4)
                            low(5)
                        elif t == 2 * EXP_CHUNKS:
                            low(0)
                            low(1)
                            turned()
                            gathered(0)
                        elif isinstance(j, int) and t % EXP_CHUNKS == 1:
                            n = t // EXP_CHUNKS
                            low(0)
                            low(1)
                            hidden(t - 1)
                            low(2)
                            low(3)
                            if n:
                                combined_last(0, n)
                            turned()
                            if n:
                                combined_last(1, n)
                            low(4)
                            low(5)
                            hidden()
                            one_hot(1 - n, pair_ * 2 + (n + 1), cn("st", n))
                        else:
                            low(0)
                            low(1)
                            low(2)
                            low(3)
                            turned()
                            low(4)
                            low(5)
                            hidden()

                    step(0)
                    for t0 in (1, EXP_CHUNKS + 1):
                        step(t0)
                        step(t0 + 1)
                        with dve.Fori(1, EXP_CHUNKS // 2) as j:
                            step(t0, j)
                            step(t0 + 1, j)
                        step(t0 + EXP_CHUNKS - 1)
                end = EXPERTS // 2
                for t in range(TT):
                    combined(t, lambda bank: moe_count(bank, 0, rnd, end))
                place8 = place[:, :, 0:EXPERTS]
                dve.drain()
                V.tensor_scalar(place8, place8, float(-CAP), None, ALU.add)
                dve.drain()

            setup()
            for l in range(DEPTH):
                norm(l, 0)
                latent(l)
                with dve.Fori(0, PAIRS) as i:
                    pair(l, i)
                merge(l)
                norm(l, 1)
                if l % 2 == 0:
                    dense(l)
                else:
                    route(l)
            experts(0)
            n = dve.value_load(nrnd[0:1, 0:1], min_val=1, max_val=MAX_ROUNDS)
            with dve.If(n > 1):
                with dve.Fori(1, n) as rnd:
                    experts(rnd)
            dve.drain().then_inc(out_ready, 1)


def constants():
    c = np.zeros((P, CONST_COLS), np.float32)

    def put(name, a):
        c[:, CONST[name][0]:CONST[name][1]] = a

    p = np.arange(P)
    put("ident", np.eye(P))
    put("ones", 1.0)
    put("half_ones", p[:, None] // 64 == p[None, :] // 64)
    rot = np.zeros((P, P))
    for m in range(P):
        rot[m + 32 if m % 64 < 32 else m - 32, m] = -1.0 if m % 64 < 32 else 1.0
    put("rot", rot)
    put("before", p[:, None] < p[None, :])
    put("slot_no", np.arange(CAP)[None])
    put("first_wins", np.arange(EXPERTS, 0, -1)[None])
    half = ROPE // 2
    freq = np.float32(10000.0) ** (-np.arange(half, dtype=np.float32) / np.float32(half))
    put("inv_freq", freq[p % half][:, None])
    put("slope", -(2.0 ** -(np.arange(1, HEADS + 1))) * (1 / DIFF_SCALE))
    return c


def layout(a):
    f = {k: np.asarray(v) for k, v in a.items()}
    L = DEPTH

    def kp(w, blocks):
        return np.moveaxis(w.reshape(w.shape[:-2] + (blocks, P, w.shape[-1])), -3, -2)

    def cols(v):
        return v.reshape(L, -1, P).transpose(2, 0, 1)

    def twice(v):
        return cols(np.concatenate([v, v], axis=1))

    gains = np.concatenate([cols(f["attn_norm_g"]), cols(f["ffn_norm_g"]), cols(f["mla_q_norm_g"]),
                            cols(f["mla_kv_norm_g"]), cols(f["mla_qn_nope_g"]), twice(f["mla_qn_rope_g"]),
                            cols(f["mla_kn_nope_g"]), twice(f["mla_kn_rope_g"]), twice(f["diff_qn_g"]),
                            twice(f["diff_kn_g"]), cols(f["diff_subln_g"])], axis=2)
    lam = np.stack([f["diff_lam_q1"], f["diff_lam_k1"], f["diff_lam_q2"], f["diff_lam_k2"]], axis=1)
    w_in = kp(f["w_in"], DB)
    kr = w_in[..., 768:832]
    w_lat = np.concatenate([w_in[..., 0:512].reshape(L, P, -1),
                            np.concatenate([w_in[..., 512:768], kr, kr], axis=-1).reshape(L, P, -1)], axis=2)

    def by_pair(w, n):
        return np.moveaxis(w.reshape(w.shape[:3] + (PAIRS, n)), 3, 1).reshape(L * PAIRS, P, w.shape[2], n)

    uq = by_pair(kp(f["mla_w_uq"], QLB), 384)
    ukv = by_pair(kp(f["mla_w_ukv"], KLB), 512)
    w_heads = np.concatenate([
        np.concatenate([uq[..., 0:128], uq[..., 192:320], uq[..., 128:192], uq[..., 320:384]], -1).reshape(L * PAIRS, P, -1),
        np.concatenate([ukv[..., 0:128], ukv[..., 256:384], ukv[..., 128:256], ukv[..., 384:512]], -1).reshape(L * PAIRS, P, -1)],
        axis=2)
    dq, dk, dv = (by_pair(w_in[..., 832 + n * 1024:832 + (n + 1) * 1024], 256).reshape(L * PAIRS, P, -1) for n in range(3))
    w_dqk = np.concatenate([dq, dk], axis=2)
    w_gates = by_pair(kp(f["w_gate"], DB), 512).reshape(L * PAIRS, P, -1)
    wa, wb, wo = (kp(f[n], DB) for n in ("w_branch_a", "w_branch_b", "w_out"))
    w_merge = np.stack([w[..., h * 512:(h + 1) * 512].reshape(L, P, -1)
                        for w, h in ((wa, 0), (wb, 0), (wa, 1), (wb, 1), (wo, 0), (wo, 1))], axis=1)
    C = DENSE_CHUNKS
    g, u = (np.moveaxis(kp(f[n][0], DB).reshape(P, DB, C, 256), 2, 0).reshape(C, P, -1)
            for n in ("dense_w_gate", "dense_w_up"))
    w_gu = np.concatenate([g, u], axis=2)
    w_dn = f["dense_w_down"][0].reshape(C, 2, P, D).transpose(0, 2, 1, 3).reshape(C, P, -1)
    w_router = kp(f["moe_w_router"][0], DB).reshape(P, -1)
    E, C = EXPERTS, EXP_CHUNKS
    g, u = (np.moveaxis(kp(f[n][0], DB).reshape(E, P, DB, C, 512), 3, 1).reshape(E, C, P, SLOT)
            for n in ("moe_w_gate", "moe_w_up"))
    d = f["moe_w_down"][0].reshape(E, C, 4, P, D).transpose(0, 1, 3, 2, 4).reshape(E, C, P, SLOT)
    w_exp = np.stack([g, u, d], axis=2).reshape(E * C * 3, P, SLOT)
    pos = f["positions"]
    return dict(
        x_t=f["x"][0].T.reshape(DB, P, T).transpose(1, 0, 2), pos_row=np.repeat(pos, P, axis=0),
        pos_col=pos.reshape(TT, P).T, const=constants(), gains=gains,
        lam_vecs=np.broadcast_to(lam[None], (P, L, 4, 64)), w_lat=w_lat, w_heads=w_heads, w_dqk=w_dqk, w_dv=dv,
        w_gates=w_gates, w_merge=w_merge, w_gu=w_gu, w_dn=w_dn, w_router=w_router, w_exp=w_exp)


def kernel(**inputs):
    import concourse.bacc as bacc
    from concourse.bass_utils import run_bass_kernel_spmd

    nc = bacc.Bacc("TRN2", target_bir_lowering=False, num_devices=1)
    arrays = {f"in_{k}": np.ascontiguousarray(v) for k, v in layout(inputs).items()}
    args = [nc.dram_tensor(k, v.shape, mybir.dt.from_np(v.dtype), kind="ExternalInput").ap() for k, v in arrays.items()]
    out = nc.dram_tensor("out_rows", (T, D), F32, kind="ExternalOutput").ap()
    build(nc, *args, out)
    r = run_bass_kernel_spmd(nc, [arrays], core_ids=[0])
    return r.results[0]["out_rows"].reshape(1, T, D)
```

```python
from contextlib import ExitStack

import numpy as np

import concourse.bass as bass
from concourse import mybir

F32 = mybir.dt.float32
F32R = mybir.dt.float32r
I32 = mybir.dt.int32
ALU = mybir.AluOpType
ACT = mybir.ActivationFunctionType
AX = mybir.AxisListType

P = 128
T = 256
TT = T // P
D = 1024
DB = D // P
DEPTH = 2
HEADS = 8
PAIRS = HEADS // 2
QLB, KLB = 4, 2
ROPE = 64
EPS = 1e-6
MLA_SCALE = float((128 + 64) ** -0.5)
DIFF_SCALE = float(64 ** -0.5)
DENSE_CHUNKS = 2816 // 256
EXPERTS = 8
EXP_CHUNKS = 3584 // 512
CAP = P
MAX_ROUNDS = -(-T // CAP)
SLOT = 4096
TWO_PI_HI, TWO_PI_MID = 6.28125, 0.0019350051879882812
TWO_PI_LO = float(2 * np.pi - 6.28125 - 0.0019350051879882812)
PI_IN = 3.1415925
ROUND = 12582912.0

LAMBDA_INIT = [0.8 - 0.6 * float(np.exp(-0.3 * l)) for l in range(DEPTH)]

CONST = {}
_at = 0
for _name, _n in (("ident", P), ("ones", P), ("half_ones", P), ("rot", P), ("before", P),
                  ("slot_no", CAP), ("first_wins", EXPERTS), ("inv_freq", 1), ("slope", HEADS)):
    CONST[_name] = (_at, _at + _n)
    _at += _n
CONST_COLS = _at

GAIN = {}
_at = 0
for _name, _n in (("attn", DB), ("ffn", DB), ("q_lat", QLB), ("kv_lat", KLB), ("qn", 1), ("qr", 1),
                  ("kn", 1), ("kr", 1), ("dq", 1), ("dk", 1), ("sub", 1)):
    GAIN[_name] = (_at, _at + _n)
    _at += _n
GAIN_COLS = _at

BANKS = ("proj0", "proj1", "stat", "score0", "score1", "trans", "ctx", "val")
PHASES = []
for _l in range(DEPTH):
    PHASES += [
        (("norm", _l, 0), 1, dict(stat=1, sq=4, rs=1, h=DB)),
        (("latent", _l), 1, dict(proj0=2, proj1=2, stat=3, val=1, sq=4, rs=3, lat=3, kr=1, s4=1, s5=1,
                                    hi=1, split=1)),
        (("pair", _l), PAIRS, dict(proj0=4, proj1=3, stat=5, score0=3, score1=3, trans=4, ctx=2, val=3,
                                   sq=5, rs=5, qk=6, v=2, mx=2, dmx=2, p=2, pd=2, pn=2, w=2, pt=4,
                                   gate=2, s0=1, s1=1, s2=1, s3=1, hi=4, split=4)),
        (("merge", _l), 1, dict(proj0=6, proj1=6, stat=4, sq=1, rs=4, ob=4, sig=1, mg=4, x=4,
                                s0=1, s1=1, s2=1, s3=1, s4=1, s5=1, **({} if _l % 2 else dict(hi=2, split=2)))),
        (("norm", _l, 1), 1, dict(stat=1, sq=4, rs=1, h=DB)),
    ]
    if _l % 2 == 0:
        PHASES += [
            (("dense0", _l), 1, dict(proj0=1, proj1=1, silu=1, hid=1, s0=1, hi=2, split=2)),
            (("dense", _l), DENSE_CHUNKS // 2, dict(proj0=2, proj1=2, score0=2, score1=2, trans=2, ctx=2,
                                                    silu=2, hid=2, x=8, s0=1, s1=1, s2=1, s3=1,
                                                    hi=8, split=8)),
            (("dense1", _l), 1, dict(score0=1, score1=1, trans=1, ctx=1, x=4, s1=1, hi=0, split=0)),
        ]
    else:
        PHASES += [
            (("route", _l), 1, dict(val=2, trans=2, ctx=2, score0=2, score1=2, htok=4, xtok=4)),
        ]
START, _c = {}, {}
for _key, _trips, _per in PHASES:
    START[_key] = dict(_c)
    for _s, _n in _per.items():
        _c[_s] = _c.get(_s, 0) + _trips * _n
PER = {k: p for k, _, p in PHASES}
MOE_START = dict(_c)
def count(phase, name, k, i=0):
    start, per = START[phase].get(name, 0), PER[phase][name]
    return i * per + (start + k) if not isinstance(i, int) else start + i * per + k


MOE_PAIR = dict(proj0=14, proj1=14, trans=14, score0=2, score1=2, ctx=6, val=6, stat=2, hi=84, split=84, used=84,
                silu=14, hid=14, hthi=14, ht=14, g=2, hehi=4, he=2, st=2, y=2, comb=2, zero=0)
MOE_SLOTS = 7
GRAN = SLOT // 2
RING = 4


MOE_OPEN = dict(ctx=1, val=1, hehi=2, he=1, g=1, stat=1, st=1, score0=1, score1=1, zero=1)
MOE_CLOSE = dict(ctx=2, val=2, y=1, comb=1)


def moe_count(name, k, rnd, pair, j=0, per_j=0, opening=False):
    n, own = MOE_PAIR[name], MOE_OPEN.get(name, 0)
    v = MOE_START.get(name, 0) + k + (0 if opening else own)
    for reg, per in ((rnd, EXPERTS // 2 * n + own + MOE_CLOSE.get(name, 0)), (pair, n), (j, per_j)):
        v = v + reg * per if isinstance(reg, int) else reg * per + v
    return v


def slot_count(slot, k, rnd, pair, j=0):
    v = MOE_START.get(f"s{slot}", 0) + k
    for reg, per in ((rnd, EXPERTS // 2 * MOE_SLOTS), (pair, MOE_SLOTS), (j, 1)):
        v = v + reg * per if isinstance(reg, int) else reg * per + v
    return v


def step_items(t):
    s = t % 2
    gate, up = (("gate", t, 3 * s, t // 2), ("up", t, 3 * s + 1, t // 2))
    down = ("down", t - 1, 3 * s + 2, t // 2 - (1 - s))
    if t == 0:
        return [gate, up]
    if t == EXP_CHUNKS:
        return [down, gate, up]
    if t == 2 * EXP_CHUNKS:
        return [down]
    return [gate, up, down]


def granules_before(t):
    return 0 if t == 0 else 6 * t - 2


def build(nc, x_t, pos_row, pos_col, const, gains, lam_vecs, w_lat, w_heads, w_dqk, w_dv, w_gates, w_merge,
          w_gu, w_dn, w_router, w_exp, out):
    with ExitStack() as ctx:
        def sb(name, shape, dt=F32):
            return ctx.enter_context(nc.sbuf_tensor(name, [P] + shape, dt))

        def sem(name):
            return ctx.enter_context(nc.semaphore(name))

        with ExitStack() as twins:
            slots_r = [twins.enter_context(nc.sbuf_tensor(f"slot{s}_r", [P, SLOT], F32R)) for s in range(6)]
            gates_r = twins.enter_context(nc.sbuf_tensor("gates_r", [P, 2 * DB, T], F32R))
        slots = [sb(f"slot{s}", [SLOT]) for s in range(6)]
        gates = sb("gates", [2 * DB, T])
        cst = sb("cst", [CONST_COLS])
        gn = sb("gn", [DEPTH, GAIN_COLS])
        lams = sb("lams", [DEPTH, 8])
        poscf = sb("poscf", [TT])
        eps = sb("eps", [1])
        marks = sb("marks", [24])
        mx, nmx, sums = sb("mx", [12]), sb("nmx", [12]), sb("sums", [12])
        rcp = sb("rcp", [12])
        rt = sb("rt", [16, TT, EXPERTS])
        sc1 = sb("sc1", [16, TT])
        cnt = sb("cnt", [EXPERTS + 8])
        nrnd = sb("nrnd", [1], I32)
        place = sb("place", [TT, EXPERTS + 2])
        wt = sb("wt", [TT, EXPERTS + 2])

        rooms = (("qk", [5, 2 * T]), ("oaT", [DB, T]), ("obT", [DB, T]), ("latN", [QLB + KLB, T]),
                 ("prob", [2, TT, T]), ("dprob", [2, 2, TT, T]), ("krT", [T]), ("cosT", [T]), ("sinT", [T]),
                 ("dist", [TT, T]), ("lamv", [DEPTH, 4, 64]), ("tmp", [2, T]), ("rsp", [2, 2 * T]),
                 ("msp", [2, 2 * T]), ("probT", [2, TT, T]), ("xT", [DB, T]), ("hT", [DB, T]), ("merged", [DB, T]))

        def attention_tensors(stack, dt, suffix=""):
            return {n: stack.enter_context(nc.sbuf_tensor(n + suffix, [P] + shape, dt)) for n, shape in rooms}

        with ExitStack() as twins:
            twin = attention_tensors(twins, F32R, "_r")
        shared = ExitStack()
        at = attention_tensors(shared, F32)
        qk, oaT, obT, latN, prob, dprob = (at[n] for n in ("qk", "oaT", "obT", "latN", "prob", "dprob"))
        krT, cosT, sinT, dist, lamv, tmp = (at[n] for n in ("krT", "cosT", "sinT", "dist", "lamv", "tmp"))
        rsp, msp, probT, xT, hT, merged = (at[n] for n in ("rsp", "msp", "probT", "xT", "hT", "merged"))
        posr, posc = (shared.enter_context(nc.sbuf_tensor(n, [P, w], I32)) for n, w in (("posr", T), ("posc", TT)))
        flat_mg = merged[:].rearrange("p a b -> p (a b)")
        sqp = flat_mg[:, 0:4 * T].rearrange("p (a b) -> p a b", a=2)
        v_mla, v_diff = (flat_mg[:, n * 2 * T:(n + 1) * 2 * T].rearrange("p (a b) -> p a b", a=TT) for n in (2, 3))
        silu = prob[:].rearrange("p a b c -> p (a b c)")
        hid = [dprob[:, i].rearrange("p a b c -> p (a b c)") for i in range(2)]
        def flat(t):
            return t[:].rearrange("p a b -> p (a b)")

        def halves(slot):
            return [slot[:, n * 2048:(n + 1) * 2048].rearrange("p (k c) -> p k c", k=DB) for n in range(2)]

        h_hi, h_lo = halves(slots_r[5])
        head_hi = halves(slots_r[4])

        def head_weights(slots_, job):
            if job < 2:
                return halves(slots_[1])[job]
            return slots_[3][:].rearrange("p (k c) -> p k c", k=DB)[:, :, (job - 2) * 2 * P:(job - 1) * 2 * P]

        gu_hi = [[flat(twin["oaT"]), flat(twin["obT"])],
                 [flat(gates_r)[:, n * 2048:(n + 1) * 2048] for n in range(2)]]
        dn_hi = [flat(twin["qk"])[:, 0:2048], flat(twin["merged"])]
        hid_lo, hid_hi = ([twin["dprob"][:, i].rearrange("p a b c -> p (a b c)")[:, n * 2 * T:(n + 1) * 2 * T]
                           for i in range(2)] for n in range(2))
        hT_lo = [twin["hT"][:, k] for k in range(DB)]
        hT_hi = [twin["latN"][:, k] for k in range(QLB + KLB)] + [twin["tmp"][:, k] for k in range(2)]
        wr = probT[:].rearrange("p a b c -> p (a b c)")[:, 0:DB * EXPERTS]
        htok = gates[:, 0:8].rearrange("p a b -> p (a b)").rearrange("p (t d) -> p t d", t=TT)
        acc = gates[:, 8:16].rearrange("p a b -> p (a b)").rearrange("p (t d) -> p t d", t=TT)
        shared.close()
        w_hi = [sb(f"w_hi{n}", [GRAN], F32R) for n in range(RING)]
        w_lo = [sb(f"w_lo{n}", [GRAN], F32R) for n in range(RING)]
        he_hi = sb("he_hi", [DB, CAP], F32R)
        he_lo = sb("he_lo", [DB, CAP], F32R)
        hidT_hi, hidT_lo = sb("hidT_hi", [4, CAP], F32R), sb("hidT_lo", [4, CAP], F32R)
        silu_e, hid_e = sb("silu_e", [4 * P]), sb("hid_e", [4 * P])
        yrow = sb("yrow", [D])
        G = [sb(f"G{n}", [TT, CAP]) for n in range(2)]
        Gw = sb("Gw", [TT, CAP])
        S = [sb(f"S{n}", [T]) for n in range(2)]

        ps = {b: ctx.enter_context(nc.psum_tensor(f"ps_{b}", [P, 2 * T], F32)) for b in BANKS}
        full = {b: sem(f"{b}_full") for b in BANKS}
        free = {b: sem(f"{b}_free") for b in BANKS}
        slot_full = [sem(f"slot{s}_full") for s in range(6)]
        slot_free = [sem(f"slot{s}_free") for s in range(6)]
        const_in = sem("const_in")
        gains_in = sem("gains_in")
        pos_in = sem("pos_in")
        x_in = sem("x_in")
        router_in = sem("router_in")
        eps_set = sem("eps_set")
        angle_ready = sem("angle_ready")
        sin_ready = sem("sin_ready")
        lam_dot = sem("lam_dot")
        lam_exp = sem("lam_exp")
        x_ready = sem("x_ready")
        sq_ready = sem("sq_ready")
        rs_ready = sem("rs_ready")
        h_ready = sem("h_ready")
        lat_ready = sem("lat_ready")
        kr_ready = sem("kr_ready")
        qk_ready = sem("qk_ready")
        v_ready = sem("v_ready")
        mla_max = sem("mla_max")
        diff_max = sem("diff_max")
        mla_exp = sem("mla_exp")
        diff_exp = sem("diff_exp")
        mla_prob = sem("mla_prob")
        diff_prob = sem("diff_prob")
        probT_ready = sem("probT_ready")
        gate_raw = sem("gate_raw")
        ob_ready = sem("ob_ready")
        gate_ready = sem("gate_ready")
        merged_ready = sem("merged_ready")
        silu_ready = sem("silu_ready")
        hid_ready = sem("hid_ready")
        route_exp_in = sem("route_exp_in")
        route_exp_out = sem("route_exp_out")
        sel_ready = sem("sel_ready")
        htok_ready = sem("htok_ready")
        xtok_ready = sem("xtok_ready")
        rounds_ready = sem("rounds_ready")
        gather_ready = sem("gather_ready")
        h_hi_ready = sem("h_hi_ready")
        h_split_ready = sem("h_split_ready")
        hi_ready = sem("hi_ready")
        split_ready = sem("split_ready")
        split_free = sem("split_free")
        he_hi_ready = sem("he_hi_ready")
        he_ready = sem("he_ready")
        hidT_hi_ready = sem("hidT_hi_ready")
        hidT_ready = sem("hidT_ready")
        scatter_ready = sem("scatter_ready")
        y_ready = sem("y_ready")
        comb_done = sem("comb_done")
        zero_ready = sem("zero_ready")
        out_ready = sem("out_ready")
        out_sent = sem("out_sent")

        def c_(name):
            a, b = CONST[name]
            return cst[:, a:b]

        def g_(l, name, j=0):
            a = GAIN[name][0] + j
            return gn[:, l, a:a + 1]

        def blk(ap, b, n=P):
            return ap[:, b * n:(b + 1) * n]

        block = ctx.enter_context(nc.Block())

        @block.sync
        def _(sp):
            sp.dma_start(cst[:], const).then_inc(const_in, 16)
            sp.dma_start(xT[:], x_t).then_inc(x_in, 16)
            sp.dma_start(gn[:], gains).then_inc(gains_in, 16)

            def load(slot, before, src, width=SLOT):
                sp.wait_ge(slot_free[slot], before + 1)
                sp.dma_start(slots[slot][:, 0:width], src).then_inc(slot_full[slot], 16)

            def one(arr, i):
                return arr[bass.ds(i, 1)].rearrange("a p n -> p (a n)")

            for l in range(DEPTH):
                load(5, count(("latent", l), "s5", 0), w_lat[l, :, 4096:4096 + 3072], 3072)
                load(4, count(("latent", l), "s4", 0), w_lat[l, :, 0:4096])
                if l == 0:
                    for dst, src in ((lamv[:], lam_vecs), (posr[:], pos_row), (posc[:], pos_col)):
                        sp.dma_start(dst, src).then_inc(pos_in, 16)
                with sp.Fori(0, PAIRS) as i:
                    for s, arr in enumerate((w_heads, w_dqk, w_dv, w_gates)):
                        load(s, count(("pair", l), f"s{s}", 0, i), one(arr, i + l * PAIRS), arr.shape[2])
                for s in range(6):
                    load(s, count(("merge", l), f"s{s}", 0), w_merge[l, s])
                if l % 2 == 0:
                    load(0, count(("dense0", l), "s0", 0), w_gu[0])
                    load(1, count(("dense", l), "s1", 0), w_dn[0], 2048)
                    with sp.Fori(0, DENSE_CHUNKS // 2) as i:
                        load(2, count(("dense", l), "s2", 0, i), one(w_gu, i * 2 + 1))
                        load(3, count(("dense", l), "s3", 0, i), one(w_dn, i * 2 + 1), 2048)
                        load(0, count(("dense", l), "s0", 0, i), one(w_gu, i * 2 + 2))
                        load(1, count(("dense", l), "s1", 1, i), one(w_dn, i * 2 + 2), 2048)

            sp.wait_ge(x_ready, count(("merge", 1), "x", 4))
            sp.dma_start(wr, w_router).then_inc(router_in, 16)

            def experts(rnd):
                with sp.Fori(0, EXPERTS // 2) as pair:
                    def step(t, j=0):
                        for kind, chunk, slot, used in step_items(t):
                            at = chunk * 3 + ("gate", "up", "down").index(kind)
                            idx = pair * (2 * EXP_CHUNKS * 3)
                            idx = idx + at if isinstance(j, int) else idx + j * 6 + at
                            load(slot, slot_count(slot, used, rnd, pair, j), one(w_exp, idx))

                    step(0)
                    for t0 in (1, EXP_CHUNKS + 1):
                        with sp.Fori(0, EXP_CHUNKS // 2) as j:
                            step(t0, j)
                            step(t0 + 1, j)
                        step(t0 + EXP_CHUNKS - 1)

            experts(0)
            sp.wait_ge(rounds_ready, 1)
            n = sp.value_load(nrnd[0:1, 0:1], min_val=1, max_val=MAX_ROUNDS)
            with sp.If(n > 1):
                with sp.Fori(1, n) as rnd:
                    experts(rnd)
            sp.wait_ge(out_ready, 1)
            sp.dma_start(out.rearrange("(t p) d -> p t d", p=P), acc).then_inc(out_sent, 16)
            sp.wait_ge(out_sent, 16)

        @block.tensor
        def _(pe):
            def take(bank, n):
                pe.wait_ge(free[bank], n + 1)
                return ps[bank]

            def need(slot, before):
                pe.wait_ge(slot_full[slot], before * 16 + 16)

            owed = []

            def release(sem_):
                owed.append(sem_)

            def settle():
                while owed:
                    nc.tensor.drain().then_inc(owed.pop(0), 1)

            def mm(out_, lhsT, rhs, k, n):
                m = nc.tensor.matmul(out_, lhsT, rhs, start=(k == 0), stop=(k == n - 1))
                if owed and k < n - 1:
                    m.then_inc(owed.pop(0), 1)
                return m

            def exact(o, w_h, w_l, x_h, x_l, k, n):
                m = nc.tensor.matmul(o, w_h, x_h, start=(k == 0), stop=False)
                if owed:
                    m.then_inc(owed.pop(0), 1)
                nc.tensor.matmul(o, w_h, x_l, start=False, stop=False)
                return nc.tensor.matmul(o, w_l, x_h, start=False, stop=(k == n - 1))

            def norm(l, which, ks=range(DB)):
                ph = ("norm", l, which)
                o = take("stat", count(ph, "stat", 0)) if ks[0] == 0 else ps["stat"]
                for k in ks:
                    if k % 2 == 0:
                        pe.wait_ge(sq_ready, count(ph, "sq", k // 2 + 1))
                    m = mm(o[:, 0:T], c_("ones"), gates[:, k], k, DB)
                if ks[-1] == DB - 1:
                    m.then_inc(full["stat"], 1)

            def latent(l):
                ph = ("latent", l)
                def stat(s, sq_n, ones, blocks, first=True, last=True):
                    pe.wait_ge(sq_ready, count(ph, "sq", sq_n))
                    o = take("stat", count(ph, "stat", s)) if first else ps["stat"]
                    for k in blocks:
                        m = nc.tensor.matmul(o[:, 0:T], c_(ones), gates[:, k], start=first and k == blocks[0],
                                             stop=last and k == blocks[-1])
                    if last:
                        m.then_inc(full["stat"], 1)

                def block_(o, b, slot, width, c0):
                    for k in range(DB):
                        if slot == 5:
                            pe.wait_ge(h_ready, count(("norm", l, 0), "h", k + 1))
                        c = k * width + c0
                        m = mm(o[:, b * T:(b + 1) * T], slots[slot][:, c:c + P], hT[:, k], k, DB)
                    return m

                need(5, count(ph, "s5", 0))
                o = take("proj1", count(ph, "proj1", 0))
                block_(o, 0, 5, 3 * P, 2 * P).then_inc(full["proj1"], 1)
                o = take("proj0", count(ph, "proj0", 0))
                block_(o, 0, 5, 3 * P, 0)
                stat(0, 1, "half_ones", (6,))
                block_(o, 1, 5, 3 * P, P).then_inc(full["proj0"], 1)
                need(4, count(ph, "s4", 0))
                o = take("proj1", count(ph, "proj1", 1))
                block_(o, 0, 4, 4 * P, 0)
                stat(1, 2, "ones", (4, 5))
                block_(o, 1, 4, 4 * P, P).then_inc(full["proj1"], 1)
                o = take("proj0", count(ph, "proj0", 1))
                block_(o, 0, 4, 4 * P, 2 * P)
                pe.wait_ge(lat_ready, count(ph, "lat", 1))
                mm(take("val", count(ph, "val", 0))[:, 0:T], c_("rot"), gates[:, 14], 0, 1).then_inc(full["val"], 1)
                block_(o, 1, 4, 4 * P, 3 * P).then_inc(full["proj0"], 1)
                stat(2, 3, "ones", (0, 1), last=False)
                stat(2, 4, "ones", (2, 3), first=False)

            def pair(l, i):
                ph = ("pair", l)

                def cn(name, k):
                    return count(ph, name, k, i)

                def stat(g):
                    pe.wait_ge(sq_ready, cn("sq", g + 1))
                    o = take("stat", cn("stat", g))
                    w = T if g == 2 else 2 * T
                    mm(o[:, 0:w], c_("ones" if g < 2 else "half_ones"), sqp[:, g % 2, 0:w], 0, 1)\
                        .then_inc(full["stat"], 1)

                heads = slots[0][:, 0:2560]
                uq = heads[:, 0:1536].rearrange("p (k c) -> p k c", k=QLB)
                ukv = heads[:, 1536:2560].rearrange("p (k c) -> p k c", k=KLB)
                need(0, cn("s0", 0))
                pe.wait_ge(lat_ready, count(("latent", l), "lat", 3))
                o = take("proj0", cn("proj0", 0))
                for h in range(2):
                    for k in range(QLB):
                        m = mm(o[:, h * T:(h + 1) * T], blk(uq[:, k], h), latN[:, k], k, QLB)
                m.then_inc(full["proj0"], 1)
                o = take("proj1", cn("proj1", 0))
                for h in range(2):
                    for k in range(KLB):
                        m = mm(o[:, h * T:(h + 1) * T], blk(ukv[:, k], h), latN[:, QLB + k], k, KLB)
                m.then_inc(full["proj1"], 1)
                stat(0)
                o = take("proj0", cn("proj0", 1))
                for k in range(QLB):
                    m = mm(o[:, 0:T], blk(uq[:, k], 2), latN[:, k], k, QLB)
                m.then_inc(full["proj0"], 1)
                stat(1)
                o = take("val", cn("val", 0))
                for t in range(TT):
                    for k in range(KLB):
                        m = mm(o[:, t * T:(t + 1) * T], latN[:, QLB + k, t * P:(t + 1) * P],
                               ukv[:, k, 2 * P:4 * P], k, KLB)
                m.then_inc(full["val"], 1)
                release(slot_free[0])

                def split_product(o, job, b, ks=range(DB)):
                    if ks[0] == 0 and b == 0:
                        pe.wait_ge(split_ready, cn("split", job + 1))
                    hi, lo = head_hi[job % 2], head_weights(slots_r, job)
                    for k in ks:
                        m = exact(o[:, b * T:(b + 1) * T], blk(hi[:, k], b), blk(lo[:, k], b), h_hi[:, k], h_lo[:, k],
                                  k, DB)
                    return m

                o = take("proj1", cn("proj1", 1))
                split_product(o, 0, 0)
                stat(2)
                split_product(o, 0, 1).then_inc(full["proj1"], 1)
                o = take("proj0", cn("proj0", 2))
                split_product(o, 1, 0)
                stat(3)
                pe.wait_ge(qk_ready, cn("qk", 3))
                rot = take("val", cn("val", 1))
                mm(rot[:, 0:T], c_("rot"), qk[:, 2, 0:T], 0, 1).then_inc(full["val"], 1)
                split_product(o, 1, 1).then_inc(full["proj0"], 1)
                release(slot_free[1])

                dv = slots[2][:, 0:2048].rearrange("p (k c) -> p k c", k=DB)
                need(2, cn("s2", 0))
                o = take("val", cn("val", 2))
                for t in range(TT):
                    for k in range(DB):
                        m = mm(o[:, t * T:(t + 1) * T], hT[:, k, t * P:(t + 1) * P], dv[:, k], k, DB)
                    if t == 0:
                        stat(4)
                m.then_inc(full["val"], 1)
                release(slot_free[2])

                def gate(o, b, ks=range(DB)):
                    return split_product(o, 2 + b // 2, b % 2, ks)

                pe.wait_ge(qk_ready, cn("qk", 4))
                pe.wait_ge(kr_ready, count(("latent", l), "kr", 1))
                for h in range(2):
                    o = take(f"score{h}", cn(f"score{h}", 0))
                    for q in range(TT):
                        mm(o[:, q * T:(q + 1) * T], qk[:, 0, h * T + q * P:h * T + (q + 1) * P],
                           qk[:, 1, h * T:(h + 1) * T], 0, 2)
                        m = mm(o[:, q * T:(q + 1) * T], qk[64 * h:64 * h + 64, 2, T + q * P:T + (q + 1) * P],
                               krT[64 * h:64 * h + 64, :], 1, 2)
                    m.then_inc(full[f"score{h}"], 1)

                def diff_scores(h):
                    if h == 0:
                        pe.wait_ge(qk_ready, cn("qk", 6))
                    for c in range(2):
                        o = take(f"score{c}", cn(f"score{c}", 1 + h))
                        for q in range(TT):
                            r = slice(64 * c, 64 * c + 64)
                            m = mm(o[:, q * T:(q + 1) * T], qk[r, 3, h * T + q * P:h * T + (q + 1) * P],
                                   qk[r, 4, h * T:(h + 1) * T], 0, 1)
                        m.then_inc(full[f"score{c}"], 1)

                def turn(n, src, ready, value):
                    pe.wait_ge(ready, value)
                    o = take("trans", cn("trans", n))
                    for k in range(TT):
                        for q in range(TT):
                            m = nc.tensor.transpose(o[:, k * T + q * P:k * T + (q + 1) * P],
                                                    src[:, q, k * P:(k + 1) * P], c_("ident"))
                    m.then_inc(full["trans"], 1)

                def weigh(branch, v, ready):
                    pe.wait_ge(v_ready, ready)
                    o = take("ctx", cn("ctx", branch))
                    for h in range(2):
                        pe.wait_ge(probT_ready, cn("pt", 2 * branch + h + 1))
                        for k in range(TT):
                            m = mm(o[:, h * T:(h + 1) * T], v[:, k, h * P:(h + 1) * P], probT[:, h, k], k, TT)
                    m.then_inc(full["ctx"], 1)

                g = take("proj1", cn("proj1", 2))
                gate(g, 0)
                diff_scores(0)
                for h in range(2):
                    turn(h, prob[:, h], mla_prob, cn("pn", h + 1))
                gate(g, 1).then_inc(full["proj1"], 1)
                weigh(0, v_mla, cn("v", 1))
                diff_scores(1)
                g = take("proj0", cn("proj0", 3))
                gate(g, 2)
                turn(2, dprob[:, 0, 0], diff_prob, cn("w", 1))
                gate(g, 3).then_inc(full["proj0"], 1)
                turn(3, dprob[:, 1, 0], diff_prob, cn("w", 2))
                release(slot_free[3])
                weigh(1, v_diff, cn("v", 2))

            def merge(l):
                ph = ("merge", l)
                jobs = [0, 0]

                def product(slot, b0, src, bank, between=lambda b, k: None):
                    w = slots[slot][:].rearrange("p (k c) -> p k c", k=DB)
                    o = take(f"proj{bank}", count(ph, f"proj{bank}", jobs[bank]))
                    jobs[bank] += 1
                    for b in range(2):
                        for k in range(DB):
                            m = mm(o[:, b * T:(b + 1) * T], blk(w[:, k], b0 + b), src[:, k], k, DB)
                            between(b, k)
                    m.then_inc(full[f"proj{bank}"], 1)

                def sub_stat(g):
                    if g == 0:
                        pe.wait_ge(sq_ready, count(ph, "sq", 1))
                    o = take("stat", count(ph, "stat", g))
                    mm(o[:], c_("ones"), merged[:, 2 * g:2 * g + 2].rearrange("p a b -> p (a b)"), 0, 1)\
                        .then_inc(full["stat"], 1)

                pe.wait_ge(free["ctx"], count(("pair", l), "ctx", 2, PAIRS - 1) + 1)
                need(0, count(ph, "s0", 0))
                product(0, 0, oaT, 0, lambda b, k: sub_stat({(0, 7): 0, (1, 3): 1}[b, k])
                        if (b, k) in ((0, 7), (1, 3)) else None)
                sub_stat(2)
                product(0, 2, oaT, 1, lambda b, k: sub_stat(3) if (b, k) == (0, 3) else None)
                release(slot_free[0])
                need(1, count(ph, "s1", 0))
                product(1, 0, oaT, 0)
                product(1, 2, oaT, 1)
                release(slot_free[1])
                pe.wait_ge(ob_ready, count(ph, "ob", 4))
                for slot in (2, 3):
                    need(slot, count(ph, f"s{slot}", 0))
                    product(slot, 0, obT, 0)
                    product(slot, 2, obT, 1)
                    release(slot_free[slot])
                pe.wait_ge(merged_ready, count(ph, "mg", 4))
                need(4, count(ph, "s4", 0))
                product(4, 0, merged, 0)
                product(4, 2, merged, 1)
                release(slot_free[4])
                need(5, count(ph, "s5", 0))
                product(5, 0, merged, 0)
                norm(l, 1, range(0, 4))
                product(5, 2, merged, 1)
                release(slot_free[5])

            def dense(l):
                def gate_up(ph, i, slot, job, split_value, parity):
                    w = slots_r[slot][:].rearrange("p (m k c) -> p m k c", m=2, k=DB)
                    for m_ in range(2):
                        pe.wait_ge(split_ready, split_value - 1 + m_)
                        hi = gu_hi[parity][m_].rearrange("p (k c) -> p k c", k=DB)
                        o = take(f"proj{m_}", count(ph, f"proj{m_}", job, i))
                        for b in range(2):
                            for k in range(DB):
                                if ph[0] == "dense0" and m_ == 0 and b == 0:
                                    pe.wait_ge(h_split_ready, k + 1)
                                m = exact(o[:, b * T:(b + 1) * T], blk(hi[:, k], b), blk(w[:, m_, k], b),
                                          hT_hi[k], hT_lo[k], k, DB)
                        m.then_inc(full[f"proj{m_}"], 1)
                    release(slot_free[slot])

                def down(ph, i, slot, job, split_value, parity):
                    w = slots_r[slot][:, 0:2048].rearrange("p (f c) -> p f c", f=2)
                    hi = dn_hi[parity].rearrange("p (f c) -> p f c", f=2)
                    h_lo, h_hi = (a.rearrange("p (f t) -> p f t", f=2) for a in (hid_lo[parity], hid_hi[parity]))
                    pe.wait_ge(split_ready, split_value)
                    for q, bank in enumerate(("score0", "score1", "trans", "ctx")):
                        o = take(bank, count(ph, bank, job, i))
                        for b in range(2):
                            for f in range(2):
                                m = exact(o[:, b * T:(b + 1) * T], blk(hi[:, f], 2 * q + b), blk(w[:, f], 2 * q + b),
                                          h_hi[:, f], h_lo[:, f], f, 2)
                        m.then_inc(full[bank], 1)
                    release(slot_free[slot])

                first, loop, last = ("dense0", l), ("dense", l), ("dense1", l)
                gate_up(first, 0, 0, 0, count(first, "split", 0), 0)
                settle()

                def two_chunks(i):
                    gate_up(loop, i, 2, 0, count(loop, "split", 0, i), 1)
                    down(loop, i, 1, 0, count(loop, "split", 2, i), 0)
                    gate_up(loop, i, 0, 1, count(loop, "split", 4, i), 0)
                    down(loop, i, 3, 1, count(loop, "split", 6, i), 1)
                    settle()

                with pe.Fori(0, DENSE_CHUNKS // 2) as i:
                    two_chunks(i)
                down(last, 0, 1, 0, count(last, "split", 0), 0)

            def route(l):
                ph = ("route", l)
                pe.wait_ge(router_in, 16)
                o = take("val", count(ph, "val", 0))
                for t in range(TT):
                    for k in range(DB):
                        if t == 0:
                            pe.wait_ge(h_ready, count(("norm", l, 1), "h", k + 1))
                        m = mm(o[:, t * EXPERTS:(t + 1) * EXPERTS], hT[:, k, t * P:(t + 1) * P],
                               wr[:, k * EXPERTS:(k + 1) * EXPERTS], k, DB)
                m.then_inc(full["val"], 1)
                for src, banks in ((hT, ("trans", "ctx")), (xT, ("score0", "score1"))):
                    for t in range(TT):
                        for half, bank in enumerate(banks):
                            o = take(bank, count(ph, bank, t))
                            for k in range(4):
                                m = nc.tensor.transpose(o[:, k * P:(k + 1) * P],
                                                        src[:, half * 4 + k, t * P:(t + 1) * P], c_("ident"))
                            m.then_inc(full[bank], 1)
                pe.wait_ge(sel_ready, 1)
                o = take("val", count(ph, "val", 1))
                E = EXPERTS
                mm(o[:, 0:E], c_("before"), rt[:, 0, 0], 0, 1)
                mm(o[:, E:2 * E], c_("before"), rt[:, 0, 1], 0, 2)
                mm(o[:, E:2 * E], c_("ones"), rt[:, 0, 0], 1, 2)
                mm(o[:, 2 * E:3 * E], c_("ones"), rt[:, 0, 0], 0, 2)
                mm(o[:, 2 * E:3 * E], c_("ones"), rt[:, 0, 1], 1, 2).then_inc(full["val"], 1)

            def gather(par, half, g_value, value):
                if half == 0:
                    pe.wait_ge(gather_ready, g_value)
                bank = ("ctx", "val")[half]
                o = take(bank, value)
                for b in range(4):
                    for t in range(TT):
                        c = (half * 4 + b) * P
                        m = mm(o[:, b * CAP:(b + 1) * CAP], htok[:, t, c:c + P], G[par][:, t], t, TT)
                m.then_inc(full[bank], 1)

            def scatter_matrix(value):
                o = take("stat", value)
                for t in range(TT):
                    m = nc.tensor.transpose(o[:, t * P:(t + 1) * P], Gw[:, t], c_("ident"))
                    if owed and t == 0:
                        m.then_inc(owed.pop(0), 1)
                m.then_inc(full["stat"], 1)

            def combine(t, par, y_value, st_value, bank_value):
                if t == 0:
                    pe.wait_ge(y_ready, y_value)
                    pe.wait_ge(scatter_ready, st_value + 1)
                for half, bank in enumerate(("ctx", "val")):
                    o = take(bank, bank_value(bank) + t)
                    mm(o[:], S[par][:, t * P:(t + 1) * P], yrow[:, half * 512:(half + 1) * 512], 0, 1)\
                        .then_inc(full[bank], 1)

            def experts(rnd):
                def opening(name, k=0):
                    return moe_count(name, k, rnd, 0, opening=True)

                for half, bank in enumerate(("ctx", "val")):
                    gather(0, half, opening("g", 1), opening(bank))
                scatter_matrix(opening("stat"))
                pe.wait_ge(zero_ready, opening("zero", 1))
                for bank in ("score0", "score1"):
                    o = take(bank, opening(bank))
                    mm(o[:], S[1][:, 0:P], cst[:, 0:2 * T], 0, 1).then_inc(full[bank], 1)
                settle()
                with pe.Fori(0, EXPERTS // 2) as pair_:
                    def cn(name, k, j=0, per_j=0):
                        return moe_count(name, k, rnd, pair_, j, per_j)

                    def gather_next(par):
                        for half, bank in enumerate(("ctx", "val")):
                            gather(par, half, cn("g", 2 - par), cn(bank, 5 - 3 * par))
                        scatter_matrix(cn("stat", 1 - par))

                    def combine_last(t, n):
                        combine(t, 1 - n, cn("y", n + 1), cn("st", n), lambda bank: cn(bank, 3 * n))

                    def exact(o, a_hi, a_lo, w_h, w_l, first, last):
                        m = nc.tensor.matmul(o, a_hi, w_h, start=first, stop=False)
                        if owed:
                            m.then_inc(owed.pop(0), 1)
                        nc.tensor.matmul(o, a_hi, w_l, start=False, stop=False)
                        return nc.tensor.matmul(o, a_lo, w_h, start=False, stop=last)

                    def step(t, j=0):
                        par = 0 if t < EXP_CHUNKS else 1

                        def granule(n):
                            n = n + granules_before(t)
                            pe.wait_ge(split_ready, cn("split", n + 1, j, 12))
                            return w_hi[n % RING][:], w_lo[n % RING][:]

                        def gate_up(m_, n0):
                            o = take(f"proj{m_}", cn(f"proj{m_}", t, j, 2))
                            if t in (0, EXP_CHUNKS) and m_ == 0:
                                pe.wait_ge(he_ready, cn("he", par))
                            for half in range(2):
                                h, lo_ = granule(n0 + half)
                                for k in range(4):
                                    kk = half * 4 + k
                                    m = exact(o[:], he_hi[:, kk], he_lo[:, kk], blk(h, k, 512),
                                              blk(lo_, k, 512), kk == 0, kk == DB - 1)
                                if half == 0:
                                    m.then_inc(split_free, 1)
                            m.then_inc(full[f"proj{m_}"], 1)
                            release(split_free)

                        def turn():
                            pe.wait_ge(hid_ready, cn("hid", t, j, 2))
                            o = take("trans", cn("trans", t - 1, j, 2))
                            for f in range(4):
                                m = nc.tensor.transpose(o[:, f * CAP:(f + 1) * CAP], hid_e[:, f * P:(f + 1) * P],
                                                        c_("ident"))
                                if owed and f < 3:
                                    m.then_inc(owed.pop(0), 1)
                            m.then_inc(full["trans"], 1)

                        def down(n0):
                            own, c = divmod(t - 1, EXP_CHUNKS)
                            looped = not isinstance(j, int)
                            if c == 0 and not looped:
                                for b in range(2):
                                    take(f"score{b}", cn(f"score{b}", own))
                            pe.wait_ge(hidT_ready, cn("ht", t, j, 2))
                            for half in range(2):
                                h, lo_ = granule(n0 + half)
                                for k in range(2):
                                    f = half * 2 + k
                                    for b in range(2):
                                        m = exact(ps[f"score{b}"][:], hidT_hi[:, f], hidT_lo[:, f],
                                                  h[:, k * D + b * 512:k * D + (b + 1) * 512],
                                                  lo_[:, k * D + b * 512:k * D + (b + 1) * 512],
                                                  c == 0 and f == 0 and not looped, c == EXP_CHUNKS - 1 and f == 3)
                                        if c == EXP_CHUNKS - 1 and f == 3:
                                            m.then_inc(full[f"score{b}"], 1)
                                if half == 0 or c < EXP_CHUNKS - 1:
                                    m.then_inc(split_free, 1)
                                else:
                                    release(split_free)

                        if t == 0:
                            gate_up(0, 0)
                            combine_last(0, 0)
                            combine_last(1, 0)
                            gate_up(1, 2)
                        elif t % EXP_CHUNKS == 0:
                            turn()
                            gather_next(1 if t == EXP_CHUNKS else 0)
                            down(0)
                            if t == EXP_CHUNKS:
                                gate_up(0, 2)
                                gate_up(1, 4)
                        else:
                            after_first = t == EXP_CHUNKS + 1 and isinstance(j, int)
                            gate_up(0, 0)
                            if after_first:
                                combine_last(0, 1)
                            turn()
                            if after_first:
                                combine_last(1, 1)
                            gate_up(1, 2)
                            down(4)

                    step(0)
                    for t0 in (1, EXP_CHUNKS + 1):
                        step(t0)
                        step(t0 + 1)
                        settle()
                        with pe.Fori(1, EXP_CHUNKS // 2) as j:
                            step(t0, j)
                            step(t0 + 1, j)
                            settle()
                        step(t0 + EXP_CHUNKS - 1)
                    settle()
                end = EXPERTS // 2
                for t in range(TT):
                    combine(t, 1, moe_count("y", 1, rnd, end), moe_count("st", 0, rnd, end),
                            lambda bank: moe_count(bank, 0, rnd, end))

            pe.wait_ge(const_in, 16)
            for l in range(DEPTH):
                norm(l, 0)
                latent(l)
                settle()
                with pe.Fori(0, PAIRS) as i:
                    pair(l, i)
                    settle()
                release(slot_free[4])
                release(slot_free[5])
                merge(l)
                norm(l, 1, range(4, DB))
                if l % 2 == 0:
                    dense(l)
                else:
                    route(l)
            settle()
            experts(0)
            pe.wait_ge(rounds_ready, 1)
            n = pe.value_load(nrnd[0:1, 0:1], min_val=1, max_val=MAX_ROUNDS)
            with pe.If(n > 1):
                with pe.Fori(1, n) as rnd:
                    experts(rnd)

        @block.scalar
        def _(act):
            def fresh(bank, n):
                act.wait_ge(full[bank], n + 1)
                return ps[bank]

            A = nc.scalar.activation
            exp_ln = "natural_log_exp_and_others"

            def rsqrt(bank_n, at, width, mean):
                o = fresh("stat", bank_n)
                h, c = at
                out_, ms = rsp[:, h, c:c + width], msp[:, h, c:c + width]
                A(ms, o[:, 0:width], ACT.Identity, bias=eps[:, 0:1], scale=mean)
                A(out_, o[:, 0:width], ACT.Ln, bias=eps[:, 0:1], scale=mean)
                act.drain().then_inc(free["stat"], 1)
                A(out_, out_, ACT.Exp, scale=-0.5).then_inc(rs_ready, 1)

            def norm(l, which, x_value):
                ph = ("norm", l, which)
                for g in range(4):
                    if x_value:
                        act.wait_ge(x_ready, x_value - 3 + g)
                    A(gates[:, 2 * g:2 * g + 2], xT[:, 2 * g:2 * g + 2], ACT.Square).then_inc(sq_ready, 1)
                rsqrt(count(ph, "stat", 0), (0, 0), T, 1.0 / D)

            def latent(l):
                ph = ("latent", l)
                def latent_(bank, job, b0, nb):
                    o = fresh(bank, count(ph, bank, job))[:, 0:nb * T].rearrange("p (b t) -> p b t", t=T)
                    A(gates[:, 8 + b0:8 + b0 + nb], o, ACT.Copy)
                    A(gates[:, b0:b0 + nb], o, ACT.Square).then_inc(sq_ready, 1)
                    act.drain().then_inc(free[bank], 1)

                latent_("proj1", 0, 6, 1)
                act.wait_ge(h_ready, count(("norm", l, 0), "h", DB))
                rsqrt(count(ph, "stat", 0), (0, 0), T, 1.0 / ROPE)
                if l == 0:
                    act.wait_ge(angle_ready, 1)
                    A(sinT[:], tmp[:, 0], ACT.Sin)
                    A(cosT[:], tmp[:, 1], ACT.Sin).then_inc(sin_ready, 1)
                    act.preload_act_table_set(exp_ln)
                    act.wait_ge(lam_dot, 1)
                    for d in range(DEPTH):
                        m = A(lams[:, d, 2:4], lams[:, d, 0:2], ACT.Exp)
                    m.then_inc(lam_exp, 1)
                latent_("proj0", 0, 4, 2)
                A(h_hi, hT[:], ACT.Copy).then_inc(hi_ready, 1)
                rsqrt(count(ph, "stat", 1), (0, T), T, 1.0 / (KLB * P))
                latent_("proj1", 1, 0, 2)
                latent_("proj0", 1, 2, 2)
                rsqrt(count(ph, "stat", 2), (1, 0), T, 1.0 / (QLB * P))

            def pair(l, i):
                ph = ("pair", l)

                def cn(name, k):
                    return count(ph, name, k, i)

                def take(g, bank, job):
                    o = fresh(bank, cn(bank, job))
                    w = T if g == 2 else 2 * T
                    A(qk[:, g, 0:w], o[:, 0:w], ACT.Copy)
                    if g >= 2:
                        act.wait_ge(full["stat"], cn("stat", g - 1))
                    A(sqp[:, g % 2, 0:w], o[:, 0:w], ACT.Square).then_inc(sq_ready, 1)
                    act.drain().then_inc(free[bank], 1)

                def factors(g):
                    w = T if g == 2 else 2 * T
                    if g >= 2:
                        act.wait_ge(qk_ready, cn("qk", (1, 2, 3)[g - 2]))
                    rsqrt(cn("stat", g), (g % 2, 0), w, 1.0 / (P if g < 2 else ROPE))

                def high(job):
                    if job < 2:
                        bank = ("proj1", "proj0")[job]
                        act.wait_ge(full[bank], cn(bank, 0))
                    if job % 2 == 0:
                        slot = (1, 3)[job // 2]
                        act.wait_ge(slot_full[slot], cn(f"s{slot}", 0) * 16 + 16)
                    A(head_hi[job % 2], head_weights(slots, job), ACT.Copy).then_inc(hi_ready, 1)

                high(0)
                high(1)
                take(0, "proj0", 0)
                take(1, "proj1", 0)
                factors(0)
                take(2, "proj0", 1)
                factors(1)
                factors(2)
                take(3, "proj1", 1)
                high(2)
                factors(3)
                take(4, "proj0", 2)
                factors(4)
                high(3)

                for h in range(2):
                    act.wait_ge(mla_max, cn("mx", h + 1))
                    o = fresh(f"score{h}", cn(f"score{h}", 0))
                    for q in range(TT):
                        m = A(prob[:, h, q], o[:, q * T:(q + 1) * T], ACT.Exp, bias=nmx[:, 2 * h + q:2 * h + q + 1],
                              scale=MLA_SCALE, accum_out=sums[:, 2 * h + q:2 * h + q + 1])
                    m.then_inc(mla_exp, 1)
                    act.drain().then_inc(free[f"score{h}"], 1)

                def turned(n):
                    o = fresh("trans", cn("trans", n))
                    if n >= 2:
                        act.wait_ge(full["ctx"], cn("ctx", 1))
                    A(probT[:, n % 2].rearrange("p a b -> p (a b)"), o[:], ACT.Copy).then_inc(probT_ready, 1)
                    act.drain().then_inc(free["trans"], 1)

                def diff_exps(h):
                    act.wait_ge(diff_max, cn("dmx", h + 1))
                    for c in range(2):
                        for q in range(TT):
                            n = 4 + 4 * h + 2 * c + q
                            m = A(dprob[:, h, c, q], dprob[:, h, c, q], ACT.Exp, bias=nmx[:, n:n + 1],
                                  scale=DIFF_SCALE, accum_out=sums[:, n:n + 1])
                    m.then_inc(diff_exp, 1)

                turned(0)
                turned(1)
                diff_exps(0)
                diff_exps(1)
                turned(2)
                turned(3)

            def merge(l):
                ph = ("merge", l)
                act.wait_ge(free["ctx"], count(("pair", l), "ctx", 2, PAIRS - 1) + 1)
                A(merged[:], obT[:], ACT.Square).then_inc(sq_ready, 1)
                for g in range(4):
                    if g >= 2:
                        act.wait_ge(ob_ready, count(ph, "ob", g - 1))
                    rsqrt(count(ph, "stat", g), (g % 2, 0), 2 * T, 1.0 / P)
                A(gates[:], gates[:], ACT.Sigmoid).then_inc(gate_ready, 1)
                if l % 2 == 0:
                    act.wait_ge(merged_ready, count(ph, "mg", 4))
                    act.wait_ge(slot_full[0], count(("dense0", l), "s0", 0) * 16 + 16)
                    high_gate_up(0, 0)

            def high_gate_up(slot, parity):
                for m_ in range(2):
                    A(gu_hi[parity][m_], slots[slot][:, m_ * 2048:(m_ + 1) * 2048], ACT.Copy)\
                        .then_inc(hi_ready, 1)

            def dense(l):
                first, loop, last = ("dense0", l), ("dense", l), ("dense1", l)

                def load_of(slot, k, ph, i=0):
                    act.wait_ge(slot_full[slot], count(ph, f"s{slot}", k, i) * 16 + 16)

                def silu_of_gate(ph, job, i=0):
                    o = fresh("proj0", count(ph, "proj0", job, i))
                    act.wait_ge(hid_ready, count(ph, "hid", job, i))
                    A(silu[:, 0:2 * T], o[:], ACT.Silu).then_inc(silu_ready, 1)
                    act.drain().then_inc(free["proj0"], 1)

                def high_down(ph, k, i, slot, parity):
                    act.wait_ge(hid_ready, count(ph, "hid", k, i) if ph == loop else START[ph]["hid"])
                    A(hid_hi[parity], hid[parity][:, 0:2 * T], ACT.Copy).then_inc(hi_ready, 1)
                    load_of(slot, 0, ph, i)
                    A(dn_hi[parity], slots[slot][:, 0:2048], ACT.Copy).then_inc(hi_ready, 1)

                act.preload_act_table(ACT.Silu)
                for k in range(DB):
                    act.wait_ge(h_ready, count(("norm", l, 1), "h", k + 1))
                    A(hT_hi[k], hT[:, k], ACT.Copy).then_inc(h_hi_ready, 1)
                load_of(2, 0, loop)
                high_gate_up(2, 1)
                silu_of_gate(first, 0)

                def two_chunks(i, more):
                    high_down(loop, 0, i, 1, 0)
                    silu_of_gate(loop, 0, i)
                    load_of(0, 0, loop, i)
                    high_gate_up(0, 0)
                    high_down(loop, 1, i, 3, 1)
                    silu_of_gate(loop, 1, i)
                    if more:
                        load_of(2, 1, loop, i)
                        high_gate_up(2, 1)

                with act.Fori(0, DENSE_CHUNKS // 2 - 1) as i:
                    two_chunks(i, True)
                two_chunks(DENSE_CHUNKS // 2 - 1, False)
                high_down(last, 0, 0, 1, 0)

            def route(l):
                ph = ("route", l)
                for name, banks, dst, ready in (("h", ("trans", "ctx"), htok, htok_ready),
                                                ("x", ("score0", "score1"), acc, xtok_ready)):
                    for t in range(TT):
                        for half, bank in enumerate(banks):
                            o = fresh(bank, count(ph, bank, t))
                            A(dst[:, t, half * 512:(half + 1) * 512], o[:], ACT.Copy).then_inc(ready, 1)
                            act.drain().then_inc(free[bank], 1)
                    if name == "h":
                        act.wait_ge(route_exp_in, 1)
                        A(sc1[:, 4], sc1[:, 3], ACT.Exp).then_inc(route_exp_out, 1)

            def gathered_half(half, value):
                o = fresh(("ctx", "val")[half], value)
                A(he_hi[:, half * 4:half * 4 + 4].rearrange("p a b -> p (a b)"), o[:], ACT.Copy).then_inc(he_hi_ready, 1)

            def scatter_matrix(par, stat_value, comb_value):
                o = fresh("stat", stat_value)
                act.wait_ge(comb_done, comb_value + 1)
                A(S[par][:], o[:, 0:T], ACT.Copy).then_inc(scatter_ready, 1)
                act.drain().then_inc(free["stat"], 1)

            def outputs(comb_value, score_value):
                act.wait_ge(comb_done, comb_value + 1)
                for b in range(2):
                    o = fresh(f"score{b}", score_value(f"score{b}"))
                    m = A(yrow[:, b * 512:(b + 1) * 512], o[:], ACT.Copy)
                    if b:
                        m.then_inc(y_ready, 1)
                    act.drain().then_inc(free[f"score{b}"], 1)

            def experts(rnd):
                def opening(name, k=0):
                    return moe_count(name, k, rnd, 0, opening=True)

                for half, bank in enumerate(("ctx", "val")):
                    gathered_half(half, opening(bank))
                scatter_matrix(0, opening("stat"), opening("comb"))
                with act.Fori(0, EXPERTS // 2) as pair_:
                    def cn(name, k, j=0, per_j=0):
                        return moe_count(name, k, rnd, pair_, j, per_j)

                    def gathered(par):
                        for half, bank in enumerate(("ctx", "val")):
                            gathered_half(half, cn(bank, 5 - 3 * par))
                        scatter_matrix(par, cn("stat", 1 - par), cn("comb", 2 - par))

                    def outputs_last(n):
                        outputs(cn("comb", n), lambda bank: cn(bank, n - 1))

                    def step(t, j=0):
                        items = step_items(t)

                        def high(n):
                            kind, chunk, slot, used = items[n // 2]
                            if n % 2 == 0:
                                act.wait_ge(slot_full[slot], slot_count(slot, used, rnd, pair_, j) * 16 + 16)
                            g = granules_before(t) + n
                            act.wait_ge(split_free, cn("used", g + 1, j, 12))
                            A(w_hi[g % RING][:], slots[slot][:, n % 2 * GRAN:(n % 2 + 1) * GRAN], ACT.Copy)\
                                .then_inc(hi_ready, 1)

                        def turned():
                            o = fresh("trans", cn("trans", t - 1, j, 2))
                            A(hidT_hi[:].rearrange("p a b -> p (a b)"), o[:], ACT.Copy).then_inc(hidT_hi_ready, 1)

                        def silu_of_gate():
                            o = fresh("proj0", cn("proj0", t, j, 2))
                            act.wait_ge(hid_ready, cn("hid", t, j, 2))
                            A(silu_e[:], o[:], ACT.Silu).then_inc(silu_ready, 1)
                            act.drain().then_inc(free["proj0"], 1)

                        if t == 0:
                            high(0)
                            high(1)
                            outputs_last(0)
                            high(2)
                            high(3)
                            silu_of_gate()
                        elif t == EXP_CHUNKS:
                            high(0)
                            high(1)
                            high(2)
                            high(3)
                            turned()
                            gathered(1)
                            high(4)
                            high(5)
                            outputs_last(1)
                            silu_of_gate()
                        elif t == 2 * EXP_CHUNKS:
                            high(0)
                            high(1)
                            turned()
                            gathered(0)
                        else:
                            high(0)
                            high(1)
                            high(2)
                            high(3)
                            turned()
                            silu_of_gate()
                            high(4)
                            high(5)

                    step(0)
                    for t0 in (1, EXP_CHUNKS + 1):
                        with act.Fori(0, EXP_CHUNKS // 2) as j:
                            step(t0, j)
                            step(t0 + 1, j)
                        step(t0 + EXP_CHUNKS - 1)
                end = EXPERTS // 2
                outputs(moe_count("comb", 0, rnd, end), lambda bank: moe_count(bank, -1, rnd, end))

            act.preload_act_table_set(exp_ln)
            act.wait_ge(x_in, 16)
            act.wait_ge(eps_set, 1)
            for l in range(DEPTH):
                norm(l, 0, START[("norm", l, 0)].get("x", 0))
                latent(l)
                act.wait_ge(lat_ready, count(("latent", l), "lat", 3))
                with act.Fori(0, PAIRS) as i:
                    pair(l, i)
                merge(l)
                act.preload_act_table_set(exp_ln)
                norm(l, 1, count(("merge", l), "x", 4))
                if l % 2 == 0:
                    dense(l)
                    act.preload_act_table_set(exp_ln)
                else:
                    route(l)
            act.preload_act_table(ACT.Silu)
            experts(0)
            act.wait_ge(rounds_ready, 1)
            n = act.value_load(nrnd[0:1, 0:1], min_val=1, max_val=MAX_ROUNDS)
            with act.If(n > 1):
                with act.Fori(1, n) as rnd:
                    experts(rnd)

        @block.vector
        def _(dve):
            V = nc.vector

            def fresh(bank, n):
                dve.wait_ge(full[bank], n + 1)
                return ps[bank]

            def then(*ops):
                for op in ops:
                    op()
                    dve.drain()

            def setup():
                V.memset(eps[:], EPS).then_inc(eps_set, 1)
                for n, s in enumerate(slot_free + list(free.values()) + [comb_done, scatter_ready] + [split_free] * RING):
                    V.memset(marks[:, n:n + 1], 0.0).then_inc(s, 1)
                dve.wait_ge(const_in, 16)
                dve.wait_ge(gains_in, 16)

            def positions():
                dve.wait_ge(pos_in, 48)
                V.tensor_copy(tmp[:, 0], posr[:])
                V.tensor_copy(poscf[:], posc[:])
                dve.drain()
                for q in range(TT):
                    V.tensor_scalar(dist[:, q], tmp[:, 0], poscf[:, q:q + 1], None, ALU.subtract)
                dve.drain()
                V.tensor_scalar(probT[:, 0], dist[:], -1.0, None, ALU.mult)
                dve.drain()
                V.tensor_tensor(dist[:], dist[:], probT[:, 0], ALU.max)
                ang, turns = tmp[:, 0], tmp[:, 1]
                then(lambda: V.tensor_scalar(ang, tmp[:, 0], c_("inv_freq"), None, ALU.mult),
                     lambda: V.tensor_scalar(turns, ang, float(0.5 / np.pi), None, ALU.mult),
                     lambda: V.tensor_scalar(turns, turns, ROUND, -ROUND, ALU.add, ALU.add),
                     lambda: V.scalar_tensor_tensor(ang, turns, -TWO_PI_HI, ang, ALU.mult, ALU.add),
                     lambda: V.scalar_tensor_tensor(ang, turns, -TWO_PI_MID, ang, ALU.mult, ALU.add),
                     lambda: V.scalar_tensor_tensor(ang, turns, -TWO_PI_LO, ang, ALU.mult, ALU.add),
                     lambda: V.tensor_scalar(turns, ang, float(np.pi / 2), float(np.pi), ALU.add, ALU.is_gt),
                     lambda: V.tensor_scalar(turns, turns, float(-2 * np.pi), float(np.pi / 2), ALU.mult, ALU.add),
                     lambda: V.tensor_tensor(turns, turns, ang, ALU.add),
                     lambda: V.tensor_scalar(ang, ang, PI_IN, -PI_IN, ALU.min, ALU.max))
                V.tensor_scalar(turns, turns, PI_IN, -PI_IN, ALU.min, ALU.max).then_inc(angle_ready, 1)
                for l in range(DEPTH):
                    V.tensor_tensor(lamv[:, l, 0:4:2], lamv[:, l, 0:4:2], lamv[:, l, 1:4:2], ALU.mult)
                    V.tensor_scalar(g_(l, "sub"), g_(l, "sub"), 1.0 - LAMBDA_INIT[l], None, ALU.mult)
                dve.drain()
                for l in range(DEPTH):
                    m = V.tensor_reduce(lams[:, l, 0:2], lamv[:, l, 0:4:2], AX.X, ALU.add)
                m.then_inc(lam_dot, 1)
                dve.wait_ge(lam_exp, 1)
                for l in range(DEPTH):
                    V.tensor_tensor(lams[:, l, 4:5], lams[:, l, 3:4], lams[:, l, 2:3], ALU.subtract)
                dve.drain()
                for l in range(DEPTH):
                    V.tensor_scalar(lams[:, l, 5:6], lams[:, l, 4:5], -LAMBDA_INIT[l], None, ALU.add)
                dve.wait_ge(sin_ready, 1)
                dve.drain()

            def root(value, at, width):
                dve.wait_ge(rs_ready, value)
                h, c = at
                y, m_ = rsp[:, h, c:c + width], msp[:, h, c:c + width]
                V.scalar_tensor_tensor(m_, m_, -0.5, y, ALU.mult, ALU.mult)
                dve.drain()
                V.tensor_tensor(m_, m_, y, ALU.mult)
                dve.drain()
                V.scalar_tensor_tensor(y, m_, 1.5, y, ALU.add, ALU.mult)
                dve.drain()
                return y

            def norm(l, which):
                ph = ("norm", l, which)
                y = root(count(ph, "rs", 1), (0, 0), T)
                for b in range(DB):
                    V.scalar_tensor_tensor(hT[:, b], xT[:, b], g_(l, "attn" if which == 0 else "ffn", b),
                                           y, ALU.mult, ALU.mult).then_inc(h_ready, 1)

            def latent(l):
                ph = ("latent", l)
                def latent_(s, name, blocks, at):
                    r = root(count(ph, "rs", s + 1), at, T)
                    for j, b in enumerate(blocks):
                        dst = latN[:, b] if s else gates[:, 14]
                        m = V.scalar_tensor_tensor(dst, gates[:, 8 + b], g_(l, name, j), r, ALU.mult, ALU.mult)
                    m.then_inc(lat_ready, 1)

                latent_(0, "kr", (6,), (0, 0))
                latent_(1, "kv_lat", (4, 5), (0, T))
                low(count(ph, "hi", 1), h_hi, h_lo, hT[:])
                dve.drain()
                o = fresh("val", count(ph, "val", 0))
                V.tensor_tensor(tmp[:, 0], o[:, 0:T], sinT[:], ALU.mult).then_inc(free["val"], 1)
                V.tensor_tensor(tmp[:, 1], gates[:, 14], cosT[:], ALU.mult)
                dve.drain()
                V.tensor_tensor(krT[:], tmp[:, 0], tmp[:, 1], ALU.add).then_inc(kr_ready, 1)
                latent_(2, "q_lat", (0, 1, 2, 3), (1, 0))

            def pair(l, i):
                ph = ("pair", l)

                def cn(name, k):
                    return count(ph, name, k, i)

                def scale(g, name):
                    w = T if g == 2 else 2 * T
                    y = root(cn("rs", g + 1), (g % 2, 0), w)
                    V.scalar_tensor_tensor(qk[:, g, 0:w], qk[:, g, 0:w], g_(l, name), y,
                                           ALU.mult, ALU.mult).then_inc(qk_ready, 1)

                def values(dst, job):
                    o = fresh("val", cn("val", job))
                    V.tensor_copy(dst.rearrange("p a b -> p (a b)"), o[:]).then_inc(v_ready, 1)
                    dve.drain().then_inc(free["val"], 1)

                def low_weights(job):
                    low(cn("hi", job + 1), head_hi[job % 2], head_weights(slots_r, job), head_weights(slots, job))

                low_weights(0)
                low_weights(1)
                values(v_mla, 0)
                scale(0, "qn")
                scale(1, "kn")
                scale(2, "qr")
                dve.drain()
                o = fresh("val", cn("val", 1))
                V.tensor_tensor(tmp[:, 0], o[:, 0:T], sinT[:], ALU.mult).then_inc(free["val"], 1)
                V.tensor_tensor(tmp[:, 1], qk[:, 2, 0:T], cosT[:], ALU.mult)
                dve.drain()
                V.tensor_tensor(qk[:, 2, T:2 * T], tmp[:, 0], tmp[:, 1], ALU.add).then_inc(qk_ready, 1)
                scale(3, "dq")
                low_weights(2)
                scale(4, "dk")
                values(v_diff, 2)

                for h in range(2):
                    o = fresh(f"score{h}", cn(f"score{h}", 0))
                    V.tensor_reduce(mx[:, 2 * h:2 * h + 2], o[:].rearrange("p (q t) -> p q t", t=T), AX.X, ALU.max)
                    dve.drain()
                    V.tensor_scalar(nmx[:, 2 * h:2 * h + 2], mx[:, 2 * h:2 * h + 2], -MLA_SCALE, None, ALU.mult)\
                        .then_inc(mla_max, 1)

                def diff_logits(h):
                    for c in range(2):
                        o = fresh(f"score{c}", cn(f"score{c}", 1 + h))
                        V.scalar_tensor_tensor(dprob[:, h, c].rearrange("p a b -> p (a b)"),
                                               dist[:].rearrange("p a b -> p (a b)"),
                                               cst[:, bass.ds(i * 2 + (CONST["slope"][0] + h), 1)], o[:],
                                               ALU.mult, ALU.add).then_inc(free[f"score{c}"], 1)
                    dve.drain()
                    n = 4 + 4 * h
                    V.tensor_reduce(mx[:, n:n + 4], dprob[:, h].rearrange("p c q t -> p (c q) t"), AX.X, ALU.max)
                    dve.drain()
                    V.tensor_scalar(nmx[:, n:n + 4], mx[:, n:n + 4], -DIFF_SCALE, None, ALU.mult).then_inc(diff_max, 1)

                def gate(bank, job, b0):
                    o = fresh(bank, cn(bank, job))
                    V.tensor_scalar(gates[:, bass.ds(i * 4 + b0, 2)], o[:].rearrange("p (b t) -> p b t", t=T),
                                    1.0, None, ALU.mult).then_inc(free[bank], 1)

                def context(branch, dst):
                    o = fresh("ctx", cn("ctx", branch))
                    V.tensor_scalar(dst[:, bass.ds(i * 2, 2)], o[:].rearrange("p (h t) -> p h t", h=2), 1.0, None,
                                    ALU.mult).then_inc(free["ctx"], 1)

                def diff_weights(h):
                    dve.wait_ge(diff_exp, cn("pd", h + 1))
                    n = 4 + 4 * h
                    V.reciprocal(rcp[:, n:n + 4], sums[:, n:n + 4])
                    dve.drain()
                    V.tensor_scalar(rcp[:, n + 2:n + 4], rcp[:, n + 2:n + 4], lams[:, l, 5:6], None, ALU.mult)
                    for q in range(TT):
                        V.tensor_scalar(dprob[:, h, 0, q], dprob[:, h, 0, q], rcp[:, n + q:n + q + 1], None, ALU.mult)
                    dve.drain()
                    for q in range(TT):
                        m = V.scalar_tensor_tensor(dprob[:, h, 0, q], dprob[:, h, 1, q], rcp[:, n + 2 + q:n + 3 + q],
                                                   dprob[:, h, 0, q], ALU.mult, ALU.add)
                    m.then_inc(diff_prob, 1)

                for h in range(2):
                    dve.wait_ge(mla_exp, cn("p", h + 1))
                    V.reciprocal(rcp[:, 2 * h:2 * h + 2], sums[:, 2 * h:2 * h + 2])
                    dve.drain()
                    for q in range(TT):
                        m = V.tensor_scalar(prob[:, h, q], prob[:, h, q], rcp[:, 2 * h + q:2 * h + q + 1], None, ALU.mult)
                    m.then_inc(mla_prob, 1)
                diff_logits(0)
                low_weights(3)
                gate("proj1", 2, 0)
                diff_weights(0)
                context(0, oaT)
                diff_logits(1)
                diff_weights(1)
                gate("proj0", 3, 2)
                context(1, obT)
                dve.drain()

            def merge(l):
                ph = ("merge", l)
                jobs = [0, 0]

                def job(bank):
                    o = fresh(f"proj{bank}", count(ph, f"proj{bank}", jobs[bank]))
                    jobs[bank] += 1
                    return o

                def two(ap, b):
                    return ap[:, b:b + 2].rearrange("p a b -> p (a b)")

                for g in range(4):
                    y = root(count(ph, "rs", g + 1), (g % 2, 0), 2 * T)
                    V.scalar_tensor_tensor(two(obT, 2 * g), two(obT, 2 * g), g_(l, "sub"), y,
                                           ALU.mult, ALU.mult).then_inc(ob_ready, 1)
                dve.wait_ge(gate_ready, count(ph, "sig", 1))
                for half in range(2):
                    for bank in range(2):
                        b = 4 * half + 2 * bank
                        V.tensor_tensor(two(merged, b), job(bank)[:], two(gates, b), ALU.mult)\
                            .then_inc(free[f"proj{bank}"], 1)
                for half in range(2):
                    for bank in range(2):
                        b = 4 * half + 2 * bank
                        V.tensor_tensor(tmp[:].rearrange("p a b -> p (a b)"), job(bank)[:], two(gates, DB + b), ALU.mult)\
                            .then_inc(free[f"proj{bank}"], 1)
                        dve.drain()
                        V.tensor_tensor(two(merged, b), two(merged, b), tmp[:].rearrange("p a b -> p (a b)"), ALU.add)\
                            .then_inc(merged_ready, 1)
                        dve.drain()
                if l % 2 == 0:
                    low_gate_up(0, 0, count(ph, "hi", 0))
                for half in range(2):
                    for bank in range(2):
                        b = 4 * half + 2 * bank
                        V.tensor_tensor(two(xT, b), two(xT, b), job(bank)[:], ALU.add).then_inc(x_ready, 1)
                        dve.drain().then_inc(free[f"proj{bank}"], 1)

            def low(value, hi, lo, src):
                dve.wait_ge(hi_ready, value)
                V.tensor_tensor(lo, src, hi.bitcast(F32), ALU.subtract).then_inc(split_ready, 1)

            def low_gate_up(slot, parity, before):
                for m_ in range(2):
                    half = slice(m_ * 2048, (m_ + 1) * 2048)
                    low(before + (m_ + 1), gu_hi[parity][m_], slots_r[slot][:, half], slots[slot][:, half])

            def dense(l):
                first, loop, last = ("dense0", l), ("dense", l), ("dense1", l)

                def hidden(ph, job, i, parity):
                    o = fresh("proj1", count(ph, "proj1", job, i))
                    dve.wait_ge(silu_ready, count(ph, "silu", job + 1, i))
                    V.tensor_tensor(hid[parity][:, 0:2 * T], o[:], silu[:, 0:2 * T], ALU.mult).then_inc(hid_ready, 1)
                    dve.drain().then_inc(free["proj1"], 1)

                def add(ph, job, i):
                    for q, bank in enumerate(("score0", "score1", "trans", "ctx")):
                        o = fresh(bank, count(ph, bank, job, i))
                        x2 = xT[:, 2 * q:2 * q + 2].rearrange("p a b -> p (a b)")
                        V.tensor_tensor(x2, x2, o[:], ALU.add).then_inc(x_ready, 1)
                        dve.drain().then_inc(free[bank], 1)

                def low_down(slot, parity, before):
                    low(before + 1, hid_hi[parity], hid_lo[parity], hid[parity][:, 0:2 * T])
                    low(before + 2, dn_hi[parity], slots_r[slot][:, 0:2048], slots[slot][:, 0:2048])

                for k in range(DB):
                    dve.wait_ge(h_hi_ready, k + 1)
                    V.tensor_tensor(hT_lo[k], hT[:, k], hT_hi[k].bitcast(F32), ALU.subtract).then_inc(h_split_ready, 1)
                low_gate_up(2, 1, count(first, "hi", 0))
                hidden(first, 0, 0, 0)

                def two_chunks(i, more):
                    low_down(1, 0, count(loop, "hi", 0, i))
                    low_gate_up(0, 0, count(loop, "hi", 2, i))
                    hidden(loop, 0, i, 1)
                    add(loop, 0, i)
                    low_down(3, 1, count(loop, "hi", 4, i))
                    if more:
                        low_gate_up(2, 1, count(loop, "hi", 6, i))
                    hidden(loop, 1, i, 0)
                    add(loop, 1, i)

                with dve.Fori(0, DENSE_CHUNKS // 2 - 1) as i:
                    two_chunks(i, True)
                two_chunks(DENSE_CHUNKS // 2 - 1, False)
                low_down(1, 0, count(last, "hi", -2))
                add(last, 0, 0)

            def route(l):
                ph = ("route", l)
                lg, oh1, l2, oh2, sc = (rt[:, n] for n in range(1, 6))
                sel, w8, place8 = rt[:, 0], wt[:, :, 0:EXPERTS], place[:, :, 0:EXPERTS]
                V.memset(place[:, :, EXPERTS:], 1.0e6)
                V.memset(wt[:, :, EXPERTS:], 0.0)
                o = fresh("val", count(ph, "val", 0))
                V.tensor_copy(lg.rearrange("p a b -> p (a b)"), o[:, 0:TT * EXPERTS]).then_inc(free["val"], 1)
                dve.drain()

                def best(src, m_, f_, onehot):
                    V.tensor_reduce(sc1[:, m_], src, AX.X, ALU.max)
                    dve.drain()
                    for t in range(TT):
                        V.scalar_tensor_tensor(sc[:, t], src[:, t], sc1[:, m_, t:t + 1], c_("first_wins"),
                                               ALU.is_equal, ALU.mult)
                    dve.drain()
                    V.tensor_reduce(sc1[:, f_], sc, AX.X, ALU.max)
                    dve.drain()
                    for t in range(TT):
                        V.tensor_scalar(onehot[:, t], c_("first_wins"), sc1[:, f_, t:t + 1], None, ALU.is_equal)
                    dve.drain()

                best(lg, 0, 1, oh1)
                V.scalar_tensor_tensor(l2, oh1, -3.0e38, lg, ALU.mult, ALU.add)
                dve.drain()
                best(l2, 2, 1, oh2)
                V.tensor_tensor(sel, oh1, oh2, ALU.add).then_inc(sel_ready, 1)
                V.tensor_tensor(sc1[:, 3], sc1[:, 2], sc1[:, 0], ALU.subtract).then_inc(route_exp_in, 1)
                dve.wait_ge(route_exp_out, 1)
                V.tensor_scalar(sc1[:, 5], sc1[:, 4], 1.0, None, ALU.add)
                dve.drain()
                V.reciprocal(sc1[:, 6], sc1[:, 5])
                dve.drain()
                V.tensor_tensor(sc1[:, 7], sc1[:, 6], sc1[:, 4], ALU.mult)
                dve.drain()
                for t in range(TT):
                    V.tensor_scalar(w8[:, t], oh1[:, t], sc1[:, 6, t:t + 1], None, ALU.mult)
                dve.drain()
                for t in range(TT):
                    V.scalar_tensor_tensor(w8[:, t], oh2[:, t], sc1[:, 7, t:t + 1], w8[:, t], ALU.mult, ALU.add)
                o = fresh("val", count(ph, "val", 1))
                E = EXPERTS
                V.tensor_copy(place8, o[:, 0:2 * E].rearrange("p (a b) -> p a b", a=TT))
                V.tensor_reduce(cnt[:, E:E + 1], o[:, 2 * E:3 * E], AX.X, ALU.max)
                dve.drain().then_inc(free["val"], 1)
                V.tensor_scalar(sc, sel, -1.0e6, 1.0e6, ALU.mult, ALU.add)
                for r in range(MAX_ROUNDS):
                    V.tensor_scalar(cnt[:, r:r + 1], cnt[:, E:E + 1], float(CAP * r), None, ALU.is_gt)
                dve.drain()
                V.tensor_tensor(place8, place8, sc, ALU.add)
                V.tensor_reduce(cnt[:, E + 1:E + 2], cnt[:, 0:MAX_ROUNDS], AX.X, ALU.add)
                dve.drain()
                V.tensor_copy(nrnd[:], cnt[:, E + 1:E + 2]).then_inc(rounds_ready, 1)
                dve.drain()
                dve.wait_ge(xtok_ready, 4)
                dve.wait_ge(htok_ready, 4)

            def one_hot(par, e, turned_before):
                dve.wait_ge(scatter_ready, turned_before + 1)
                for t in range(TT):
                    V.tensor_scalar(G[par][:, t], c_("slot_no"), place[:, t, bass.ds(e, 1)], None, ALU.is_equal)
                    m = V.tensor_scalar(Gw[:, t], c_("slot_no"), place[:, t, bass.ds(e, 1)],
                                        wt[:, t, bass.ds(e, 1)], ALU.is_equal, ALU.mult)
                m.then_inc(gather_ready, 1)

            def gathered_half(half, value):
                dve.wait_ge(he_hi_ready, value)
                h = he_hi[:, half * 4:half * 4 + 4].rearrange("p a b -> p (a b)")
                bank = ("ctx", "val")[half]
                m = V.tensor_tensor(he_lo[:, half * 4:half * 4 + 4].rearrange("p a b -> p (a b)"),
                                    ps[bank][:], h.bitcast(F32), ALU.subtract)
                if half:
                    m.then_inc(he_ready, 1)
                dve.drain().then_inc(free[bank], 1)

            def combined(t, bank_value):
                for half, bank in enumerate(("ctx", "val")):
                    o = fresh(bank, bank_value(bank) + t)
                    a = acc[:, t, half * 512:(half + 1) * 512]
                    m = V.tensor_tensor(a, a, o[:], ALU.add)
                    if t and half:
                        m.then_inc(comb_done, 1)
                    dve.drain().then_inc(free[bank], 1)

            def experts(rnd):
                def opening(name, k=0):
                    return moe_count(name, k, rnd, 0, opening=True)

                V.memset(S[1][:], 0.0).then_inc(zero_ready, 1)
                one_hot(0, 0, opening("st"))
                for half in range(2):
                    gathered_half(half, opening("hehi", half + 1))
                with dve.Fori(0, EXPERTS // 2) as pair_:
                    def cn(name, k, j=0, per_j=0):
                        return moe_count(name, k, rnd, pair_, j, per_j)

                    def gathered(par):
                        for half in range(2):
                            gathered_half(half, cn("hehi", 2 * (1 - par) + half + 1))

                    def combined_last(t, n):
                        combined(t, lambda bank: cn(bank, 3 * n))

                    def step(t, j=0):
                        items = step_items(t)

                        def low(n):
                            kind, chunk, slot, used = items[n // 2]
                            g = granules_before(t) + n
                            dve.wait_ge(hi_ready, cn("hi", g + 1, j, 12))
                            V.tensor_tensor(w_lo[g % RING][:], slots[slot][:, n % 2 * GRAN:(n % 2 + 1) * GRAN],
                                            w_hi[g % RING][:].bitcast(F32), ALU.subtract).then_inc(split_ready, 1)
                            if n % 2:
                                dve.drain().then_inc(slot_free[slot], 1)

                        def turned():
                            dve.wait_ge(hidT_hi_ready, cn("hthi", t, j, 2))
                            V.tensor_tensor(hidT_lo[:].rearrange("p a b -> p (a b)"), ps["trans"][:],
                                            hidT_hi[:].rearrange("p a b -> p (a b)").bitcast(F32), ALU.subtract)\
                                .then_inc(hidT_ready, 1)
                            dve.drain().then_inc(free["trans"], 1)

                        def hidden(c=t):
                            o = fresh("proj1", cn("proj1", c, j, 2))
                            dve.wait_ge(silu_ready, cn("silu", c + 1, j, 2))
                            V.tensor_tensor(hid_e[:], o[:], silu_e[:], ALU.mult).then_inc(hid_ready, 1)
                            dve.drain().then_inc(free["proj1"], 1)

                        if t == 0:
                            low(0)
                            low(1)
                            low(2)
                            low(3)
                            combined_last(0, 0)
                            combined_last(1, 0)
                        elif t == EXP_CHUNKS:
                            low(0)
                            low(1)
                            low(2)
                            low(3)
                            turned()
                            gathered(1)
                            low(4)
                            low(5)
                        elif t == 2 * EXP_CHUNKS:
                            low(0)
                            low(1)
                            turned()
                            gathered(0)
                        elif isinstance(j, int) and t % EXP_CHUNKS == 1:
                            n = t // EXP_CHUNKS
                            low(0)
                            low(1)
                            hidden(t - 1)
                            low(2)
                            low(3)
                            if n:
                                combined_last(0, n)
                            turned()
                            if n:
                                combined_last(1, n)
                            low(4)
                            low(5)
                            hidden()
                            one_hot(1 - n, pair_ * 2 + (n + 1), cn("st", n))
                        else:
                            low(0)
                            low(1)
                            low(2)
                            low(3)
                            turned()
                            low(4)
                            low(5)
                            hidden()

                    step(0)
                    for t0 in (1, EXP_CHUNKS + 1):
                        step(t0)
                        step(t0 + 1)
                        with dve.Fori(1, EXP_CHUNKS // 2) as j:
                            step(t0, j)
                            step(t0 + 1, j)
                        step(t0 + EXP_CHUNKS - 1)
                end = EXPERTS // 2
                for t in range(TT):
                    combined(t, lambda bank: moe_count(bank, 0, rnd, end))
                place8 = place[:, :, 0:EXPERTS]
                dve.drain()
                V.tensor_scalar(place8, place8, float(-CAP), None, ALU.add)
                dve.drain()

            setup()
            for l in range(DEPTH):
                norm(l, 0)
                if l == 0:
                    positions()
                latent(l)
                with dve.Fori(0, PAIRS) as i:
                    pair(l, i)
                merge(l)
                norm(l, 1)
                if l % 2 == 0:
                    dense(l)
                else:
                    route(l)
            experts(0)
            n = dve.value_load(nrnd[0:1, 0:1], min_val=1, max_val=MAX_ROUNDS)
            with dve.If(n > 1):
                with dve.Fori(1, n) as rnd:
                    experts(rnd)
            dve.drain().then_inc(out_ready, 1)


def constants():
    c = np.zeros((P, CONST_COLS), np.float32)

    def put(name, a):
        c[:, CONST[name][0]:CONST[name][1]] = a

    p = np.arange(P)
    put("ident", np.eye(P))
    put("ones", 1.0)
    put("half_ones", p[:, None] // 64 == p[None, :] // 64)
    rot = np.zeros((P, P))
    for m in range(P):
        rot[m + 32 if m % 64 < 32 else m - 32, m] = -1.0 if m % 64 < 32 else 1.0
    put("rot", rot)
    put("before", p[:, None] < p[None, :])
    put("slot_no", np.arange(CAP)[None])
    put("first_wins", np.arange(EXPERTS, 0, -1)[None])
    half = ROPE // 2
    freq = np.float32(10000.0) ** (-np.arange(half, dtype=np.float32) / np.float32(half))
    put("inv_freq", freq[p % half][:, None])
    put("slope", -(2.0 ** -(np.arange(1, HEADS + 1))) * (1 / DIFF_SCALE))
    return c


def layout(a):
    f = {k: np.asarray(v) for k, v in a.items()}
    L = DEPTH

    def kp(w, blocks):
        return np.moveaxis(w.reshape(w.shape[:-2] + (blocks, P, w.shape[-1])), -3, -2)

    def cols(v):
        return v.reshape(L, -1, P).transpose(2, 0, 1)

    def twice(v):
        return cols(np.concatenate([v, v], axis=1))

    gains = np.concatenate([cols(f["attn_norm_g"]), cols(f["ffn_norm_g"]), cols(f["mla_q_norm_g"]),
                            cols(f["mla_kv_norm_g"]), cols(f["mla_qn_nope_g"]), twice(f["mla_qn_rope_g"]),
                            cols(f["mla_kn_nope_g"]), twice(f["mla_kn_rope_g"]), twice(f["diff_qn_g"]),
                            twice(f["diff_kn_g"]), cols(f["diff_subln_g"])], axis=2)
    lam = np.stack([f["diff_lam_q1"], f["diff_lam_k1"], f["diff_lam_q2"], f["diff_lam_k2"]], axis=1)
    w_in = kp(f["w_in"], DB)
    kr = w_in[..., 768:832]
    w_lat = np.concatenate([w_in[..., 0:512].reshape(L, P, -1),
                            np.concatenate([w_in[..., 512:768], kr, kr], axis=-1).reshape(L, P, -1)], axis=2)

    def by_pair(w, n):
        return np.moveaxis(w.reshape(w.shape[:3] + (PAIRS, n)), 3, 1).reshape(L * PAIRS, P, w.shape[2], n)

    uq = by_pair(kp(f["mla_w_uq"], QLB), 384)
    ukv = by_pair(kp(f["mla_w_ukv"], KLB), 512)
    w_heads = np.concatenate([
        np.concatenate([uq[..., 0:128], uq[..., 192:320], uq[..., 128:192], uq[..., 320:384]], -1).reshape(L * PAIRS, P, -1),
        np.concatenate([ukv[..., 0:128], ukv[..., 256:384], ukv[..., 128:256], ukv[..., 384:512]], -1).reshape(L * PAIRS, P, -1)],
        axis=2)
    dq, dk, dv = (by_pair(w_in[..., 832 + n * 1024:832 + (n + 1) * 1024], 256).reshape(L * PAIRS, P, -1) for n in range(3))
    w_dqk = np.concatenate([dq, dk], axis=2)
    w_gates = by_pair(kp(f["w_gate"], DB), 512).reshape(L * PAIRS, P, -1)
    wa, wb, wo = (kp(f[n], DB) for n in ("w_branch_a", "w_branch_b", "w_out"))
    w_merge = np.stack([w[..., h * 512:(h + 1) * 512].reshape(L, P, -1)
                        for w, h in ((wa, 0), (wa, 1), (wb, 0), (wb, 1), (wo, 0), (wo, 1))], axis=1)
    C = DENSE_CHUNKS
    g, u = (np.moveaxis(kp(f[n][0], DB).reshape(P, DB, C, 256), 2, 0).reshape(C, P, -1)
            for n in ("dense_w_gate", "dense_w_up"))
    w_gu = np.concatenate([g, u], axis=2)
    w_dn = f["dense_w_down"][0].reshape(C, 2, P, D).transpose(0, 2, 1, 3).reshape(C, P, -1)
    w_router = kp(f["moe_w_router"][0], DB).reshape(P, -1)
    E, C = EXPERTS, EXP_CHUNKS
    g, u = (np.moveaxis(kp(f[n][0], DB).reshape(E, P, DB, C, 512), 3, 1).reshape(E, C, P, SLOT)
            for n in ("moe_w_gate", "moe_w_up"))
    d = f["moe_w_down"][0].reshape(E, C, 4, P, D).transpose(0, 1, 3, 2, 4).reshape(E, C, P, SLOT)
    w_exp = np.stack([g, u, d], axis=2).reshape(E * C * 3, P, SLOT)
    pos = f["positions"]
    return dict(
        x_t=f["x"][0].T.reshape(DB, P, T).transpose(1, 0, 2), pos_row=np.repeat(pos, P, axis=0),
        pos_col=pos.reshape(TT, P).T, const=constants(), gains=gains,
        lam_vecs=np.broadcast_to(lam[None], (P, L, 4, 64)), w_lat=w_lat, w_heads=w_heads, w_dqk=w_dqk, w_dv=dv,
        w_gates=w_gates, w_merge=w_merge, w_gu=w_gu, w_dn=w_dn, w_router=w_router, w_exp=w_exp)


def kernel(**inputs):
    import concourse.bacc as bacc
    from concourse.bass_utils import run_bass_kernel_spmd

    nc = bacc.Bacc("TRN2", target_bir_lowering=False, num_devices=1)
    arrays = {f"in_{k}": np.ascontiguousarray(v) for k, v in layout(inputs).items()}
    args = [nc.dram_tensor(k, v.shape, mybir.dt.from_np(v.dtype), kind="ExternalInput").ap() for k, v in arrays.items()]
    out = nc.dram_tensor("out_rows", (T, D), F32, kind="ExternalOutput").ap()
    build(nc, *args, out)
    r = run_bass_kernel_spmd(nc, [arrays], core_ids=[0])
    return r.results[0]["out_rows"].reshape(1, T, D)
```
